# Optimizing a Trainium2 kernel written in Bass

```python
import math
import jax, jax.numpy as jnp
from jax import lax
import numpy as np

D_MODEL = 1024
BATCH = 1
SEQ = 256
DEPTH = 2

PLE_DIM = 256
FOX_HEADS = 8
FOX_HEAD_DIM = 64
FOX_WIDTH = FOX_HEADS * FOX_HEAD_DIM
Q_BLOCK = 128
POOL_WINDOWS = (2, 4, 8, 16)
POOL_GROUPS = 4
POOL_GROUP_DIM = 128
POOL_WIDTH = POOL_GROUPS * POOL_GROUP_DIM
GDN_HEADS = 4
GDN_HEAD_DIM = 128
GDN_WIDTH = GDN_HEADS * GDN_HEAD_DIM
GDN_CONV = 4
GDN_CHUNK = 64
N_BRANCHES = 3
IN_SPLITS = (3 * FOX_WIDTH, FOX_HEADS, POOL_WIDTH, 3 * GDN_WIDTH, GDN_HEADS, GDN_HEADS, GDN_WIDTH, N_BRANCHES * D_MODEL)
IN_WIDTH = sum(IN_SPLITS)
PEER_HEADS = 8
PEER_KEYS = 128
PEER_N_EXPERTS = PEER_KEYS * PEER_KEYS
PEER_QUERY_DIM = 256
PEER_HALF = PEER_QUERY_DIM // 2
PEER_TOPK = 16
PEER_TOKEN_BLOCK = 128
DEEPNORM_ALPHA = (2 * DEPTH) ** 0.25
DEEPNORM_BETA = (8 * DEPTH) ** -0.25
LN_EPS = 1e-5
RMS_EPS = 1e-6
L2_EPS = 1e-6

kernel_name = "hybrid_fox_pool_gdn_peer_deepnorm"

def layer_norm(x, g, b):
    xf = x.astype(jnp.float32)
    mu = jnp.mean(xf, axis=-1, keepdims=True)
    var = jnp.mean(jnp.square(xf - mu), axis=-1, keepdims=True)
    return ((xf - mu) * lax.rsqrt(var + LN_EPS) * g.astype(jnp.float32) + b.astype(jnp.float32)).astype(x.dtype)

def forgetting_attention(q, k, v, f_logit):
    B, S, H, Dh = q.shape
    nb = S // Q_BLOCK
    cum = jnp.cumsum(jax.nn.log_sigmoid(f_logit.astype(jnp.float32)), axis=1)
    cum_k = cum.transpose(0, 2, 1)[:, :, None, :]
    kpos = jnp.arange(S)
    scale = FOX_HEAD_DIM ** -0.5
    qb = q.reshape(B, nb, Q_BLOCK, H, Dh).transpose(1, 0, 2, 3, 4)
    cb = cum.reshape(B, nb, Q_BLOCK, H).transpose(1, 0, 3, 2)
    starts = jnp.arange(nb) * Q_BLOCK

    def block(args):
        qi, ci, start = args
        s = jnp.einsum('bqhd,bkhd->bhqk', qi, k).astype(jnp.float32) * scale
        s = s + ci[..., None] - cum_k
        qpos = start + jnp.arange(Q_BLOCK)
        causal = qpos[:, None] >= kpos[None, :]
        s = jnp.where(causal, s, -jnp.inf)
        pr = jax.nn.softmax(s, axis=-1).astype(v.dtype)
        return jnp.einsum('bhqk,bkhd->bqhd', pr, v)

    out = lax.map(block, (qb, cb, starts))
    return out.transpose(1, 0, 2, 3, 4).reshape(B, S, H * Dh)

def multiscale_pool(xp, w_pool, pool_scale):
    B, S, _ = xp.shape
    xg = xp.reshape(B, S, POOL_GROUPS, POOL_GROUP_DIM).astype(jnp.float32)
    cs = jnp.concatenate([jnp.zeros_like(xg[:, :1]), jnp.cumsum(xg, axis=1)], axis=1)
    t = jnp.arange(S)
    windows = jnp.array(POOL_WINDOWS, dtype=jnp.int32)
    lo = jnp.maximum(t[:, None] + 1 - windows[None, :], 0)
    grp = jnp.arange(POOL_GROUPS)[None, :]
    win_sum = cs[:, 1:] - cs[:, lo, grp, :]
    count = (t[:, None] + 1 - lo).astype(jnp.float32)
    pooled = win_sum / count[None, :, :, None] - xg
    mixed = jnp.einsum('bsgc,gcd->bsgd', pooled, w_pool.astype(jnp.float32))
    out = mixed.reshape(B, S, POOL_WIDTH) * pool_scale.astype(jnp.float32)
    return out.astype(xp.dtype)

def causal_depthwise_conv(x, w):
    C = x.shape[-1]
    return lax.conv_general_dilated(x, w.astype(x.dtype), window_strides=(1,), padding=[(GDN_CONV - 1, 0)],
                                    dimension_numbers=('NWC', 'WIO', 'NWC'), feature_group_count=C)

def l2norm(x):
    return x * lax.rsqrt(jnp.sum(x * x, axis=-1, keepdims=True) + L2_EPS)

def gated_delta_rule(q, k, v, g, beta):
    B, S, H, D = q.shape
    C = GDN_CHUNK
    n = S // C

    def chunks(a):
        a = a.reshape((B, n, C, H) + a.shape[3:])
        return jnp.moveaxis(a, 3, 1)

    q = chunks(q) * (D ** -0.5)
    k = chunks(k)
    v = chunks(v)
    g = jnp.cumsum(chunks(g), axis=-1)
    beta = chunks(beta)
    k_beta = k * beta[..., None]
    v_beta = v * beta[..., None]
    tri_strict = jnp.tril(jnp.ones((C, C), dtype=bool), -1)
    tri_incl = jnp.tril(jnp.ones((C, C), dtype=bool))

    def decay(mask):
        return jnp.exp(jnp.where(mask, g[..., :, None] - g[..., None, :], -jnp.inf))

    L = jnp.einsum('bhnid,bhnjd->bhnij', k_beta, k) * decay(tri_strict)
    eye = jnp.eye(C, dtype=jnp.float32)
    T = lax.linalg.triangular_solve(eye + L, jnp.broadcast_to(eye, L.shape), left_side=True, lower=True,
                                    unit_diagonal=True)
    u = T @ v_beta
    w = T @ (k_beta * jnp.exp(g)[..., None])
    a_intra = jnp.einsum('bhnid,bhnjd->bhnij', q, k) * decay(tri_incl)
    g_last = g[..., -1]

    def step(state, xs):
        q_c, k_c, u_c, w_c, a_c, g_c, gl = xs
        v_new = u_c - w_c @ state
        o = (q_c * jnp.exp(g_c)[..., None]) @ state + a_c @ v_new
        k_dec = k_c * jnp.exp(gl[..., None] - g_c)[..., None]
        state = state * jnp.exp(gl)[..., None, None] + jnp.einsum('bhcd,bhce->bhde', k_dec, v_new)
        return state, o

    xs = tuple(jnp.moveaxis(a, 2, 0) for a in (q, k, u, w, a_intra, g, g_last))
    s0 = jnp.zeros((B, H, D, D), dtype=jnp.float32)
    _, o = lax.scan(step, s0, xs)
    return o.transpose(1, 0, 3, 2, 4).reshape(B, S, H, D)

def gated_deltanet(qkv, b_logit, a_logit, z, conv_w, a_log, dt_bias, norm_g):
    B, S, _ = qkv.shape
    act = jax.nn.silu(causal_depthwise_conv(qkv, conv_w)).astype(jnp.float32)
    q, k, v = jnp.split(act, 3, axis=-1)
    q = l2norm(q.reshape(B, S, GDN_HEADS, GDN_HEAD_DIM))
    k = l2norm(k.reshape(B, S, GDN_HEADS, GDN_HEAD_DIM))
    v = v.reshape(B, S, GDN_HEADS, GDN_HEAD_DIM)
    beta = jax.nn.sigmoid(b_logit.astype(jnp.float32))
    g = -jnp.exp(a_log.astype(jnp.float32)) * jax.nn.softplus(a_logit.astype(jnp.float32) + dt_bias.astype(jnp.float32))
    o = gated_delta_rule(q, k, v, g, beta)
    o = o * lax.rsqrt(jnp.mean(o * o, axis=-1, keepdims=True) + RMS_EPS) * norm_g.astype(jnp.float32)
    o = o * jax.nn.silu(z.astype(jnp.float32).reshape(B, S, GDN_HEADS, GDN_HEAD_DIM))
    return o.reshape(B, S, GDN_WIDTH).astype(qkv.dtype)

def token_mixer(h, w_in, fox_fb, pool_w, pool_scale, gdn_conv, gdn_a_log, gdn_dt_bias, gdn_norm, w_branch, w_out):
    B, S, _ = h.shape
    proj = h @ w_in
    offsets = [int(o) for o in np.cumsum(IN_SPLITS)[:-1]]
    fox_qkv, fox_f, pool_in, gdn_qkv, gdn_b, gdn_a, gdn_z, gates = jnp.split(proj, offsets, axis=-1)
    fq, fk, fv = [t.reshape(B, S, FOX_HEADS, FOX_HEAD_DIM) for t in jnp.split(fox_qkv, 3, axis=-1)]
    branch_a = forgetting_attention(fq, fk, fv, fox_f + fox_fb)
    branch_b = multiscale_pool(pool_in, pool_w, pool_scale)
    branch_c = gated_deltanet(gdn_qkv, gdn_b, gdn_a, gdn_z, gdn_conv, gdn_a_log, gdn_dt_bias, gdn_norm)
    branches = jnp.stack([branch_a, branch_b, branch_c], axis=2)
    to_model = jnp.einsum('bsnw,nwd->bsnd', branches, w_branch)
    gate = jax.nn.sigmoid(gates.reshape(B, S, N_BRANCHES, D_MODEL))
    merged = jnp.sum(gate * to_model, axis=2)
    return merged @ w_out

def peer_ffn(h, w_q, sub_k1, sub_k2, u_tab, v_tab):
    B, S, D = h.shape
    q = (h @ w_q).reshape(B, S, PEER_HEADS, 2, PEER_HALF)
    s1 = jnp.einsum('bshd,hnd->bshn', q[..., 0, :], sub_k1).astype(jnp.float32)
    s2 = jnp.einsum('bshd,hnd->bshn', q[..., 1, :], sub_k2).astype(jnp.float32)
    v1, i1 = lax.top_k(s1, PEER_TOPK)
    v2, i2 = lax.top_k(s2, PEER_TOPK)
    cand_s = (v1[..., :, None] + v2[..., None, :]).reshape(B, S, PEER_HEADS, PEER_TOPK * PEER_TOPK)
    cand_i = (i1[..., :, None] * PEER_KEYS + i2[..., None, :]).reshape(B, S, PEER_HEADS, PEER_TOPK * PEER_TOPK)
    top_s, pos = lax.top_k(cand_s, PEER_TOPK)
    idx = jnp.take_along_axis(cand_i, pos, axis=-1)
    wts = jax.nn.softmax(top_s, axis=-1).astype(h.dtype)
    n_blk = (B * S) // PEER_TOKEN_BLOCK
    xt = h.reshape(n_blk, PEER_TOKEN_BLOCK, D)
    it = idx.reshape(n_blk, PEER_TOKEN_BLOCK, PEER_HEADS, PEER_TOPK)
    wt = wts.reshape(n_blk, PEER_TOKEN_BLOCK, PEER_HEADS, PEER_TOPK)

    def block(args):
        xb, ib, wb = args
        u_sel = u_tab[ib]
        act = jax.nn.gelu(jnp.einsum('thkd,td->thk', u_sel, xb), approximate=False)
        return jnp.einsum('thk,thkd->td', act * wb, v_tab[ib])

    out = lax.map(block, (xt, it, wt))
    return out.reshape(B, S, D)

def setup_inputs(seed: int = 0) -> dict:
    key = jax.random.key(seed)
    ks = jax.random.split(key, 26)
    f32 = jnp.float32
    nrm = lambda k, shape, s: jax.random.normal(k, shape, f32) * s
    dt = jnp.exp(jax.random.uniform(ks[9], (DEPTH, GDN_HEADS), f32, math.log(1e-3), math.log(1e-1)))
    return {
        "x": nrm(ks[0], (BATCH, SEQ, D_MODEL), 1.0),
        "p": nrm(ks[1], (DEPTH, BATCH, SEQ, PLE_DIM), 1.0),
        "w_in": nrm(ks[2], (DEPTH, D_MODEL, IN_WIDTH), D_MODEL ** -0.5),
        "fox_fb": 3.0 + nrm(ks[3], (DEPTH, FOX_HEADS), 0.5),
        "pool_w": nrm(ks[4], (DEPTH, POOL_GROUPS, POOL_GROUP_DIM, POOL_GROUP_DIM), POOL_GROUP_DIM ** -0.5),
        "pool_scale": 1.0 + nrm(ks[5], (DEPTH, POOL_WIDTH), 0.1),
        "gdn_conv": nrm(ks[6], (DEPTH, GDN_CONV, 1, 3 * GDN_WIDTH), GDN_CONV ** -0.5),
        "gdn_a_log": jnp.log(jax.random.uniform(ks[7], (DEPTH, GDN_HEADS), f32, 1.0, 16.0)),
        "gdn_dt_bias": dt + jnp.log(-jnp.expm1(-dt)),
        "gdn_norm": 1.0 + nrm(ks[8], (DEPTH, GDN_HEAD_DIM), 0.05),
        "w_branch": nrm(ks[10], (DEPTH, N_BRANCHES, FOX_WIDTH, D_MODEL), FOX_WIDTH ** -0.5),
        "w_out": nrm(ks[11], (DEPTH, D_MODEL, D_MODEL), D_MODEL ** -0.5 * DEEPNORM_BETA),
        "ln1_g": 1.0 + nrm(ks[12], (DEPTH, D_MODEL), 0.05),
        "ln1_b": nrm(ks[13], (DEPTH, D_MODEL), 0.02),
        "peer_wq": nrm(ks[14], (DEPTH, D_MODEL, PEER_HEADS * PEER_QUERY_DIM), D_MODEL ** -0.5),
        "peer_k1": nrm(ks[15], (DEPTH, PEER_HEADS, PEER_KEYS, PEER_HALF), PEER_HALF ** -0.5),
        "peer_k2": nrm(ks[16], (DEPTH, PEER_HEADS, PEER_KEYS, PEER_HALF), PEER_HALF ** -0.5),
        "peer_u": nrm(ks[17], (DEPTH, PEER_N_EXPERTS, D_MODEL), D_MODEL ** -0.5),
        "peer_v": nrm(ks[18], (DEPTH, PEER_N_EXPERTS, D_MODEL), DEEPNORM_BETA),
        "ple_gate": nrm(ks[19], (DEPTH, D_MODEL, D_MODEL), D_MODEL ** -0.5),
        "ple_proj": nrm(ks[20], (DEPTH, PLE_DIM, D_MODEL), PLE_DIM ** -0.5 * DEEPNORM_BETA),
        "ln2_g": 1.0 + nrm(ks[21], (DEPTH, D_MODEL), 0.05),
        "ln2_b": nrm(ks[22], (DEPTH, D_MODEL), 0.02),
    }

def reference(x, p, w_in, fox_fb, pool_w, pool_scale, gdn_conv, gdn_a_log, gdn_dt_bias, gdn_norm, w_branch, w_out,
              ln1_g, ln1_b, peer_wq, peer_k1, peer_k2, peer_u, peer_v, ple_gate, ple_proj, ln2_g, ln2_b):
    h = x
    for i in range(DEPTH):
        mix = token_mixer(h, w_in[i], fox_fb[i], pool_w[i], pool_scale[i], gdn_conv[i], gdn_a_log[i],
                          gdn_dt_bias[i], gdn_norm[i], w_branch[i], w_out[i])
        h = layer_norm(DEEPNORM_ALPHA * h + mix, ln1_g[i], ln1_b[i])
        ffn = peer_ffn(h, peer_wq[i], peer_k1[i], peer_k2[i], peer_u[i], peer_v[i])
        ple = jax.nn.sigmoid(h @ ple_gate[i]) * (p[i] @ ple_proj[i])
        h = layer_norm(DEEPNORM_ALPHA * h + ffn + ple, ln2_g[i], ln2_b[i])
    return h


_drawn_inputs = setup_inputs


def setup_inputs(seed=0):
    import zlib

    import numpy as np

    out = dict(_drawn_inputs(seed))
    spreads = {}
    factors = {}
    for name, (base, spread) in spreads.items():
        noise = np.random.default_rng([zlib.crc32(name.encode()), seed]).standard_normal(out[name].shape)
        drawn = base * np.exp(spread * noise) if base else spread * noise
        out[name] = __import__('jax').numpy.asarray(drawn.astype(out[name].dtype))
    for name, factor in factors.items():
        out[name] = (out[name] * factor).astype(out[name].dtype)
    return out
```

```python
from contextlib import ExitStack

import numpy as np

import concourse.bass as bass
from concourse import mybir

F32 = mybir.dt.float32
U32 = mybir.dt.uint32
ALU = mybir.AluOpType
ACT = mybir.ActivationFunctionType
AX_X = mybir.AxisListType.X

P = 128
D = 1024
KT = D // P
T = 256
NB = T // P
DEPTH = 2
PLE = 256
FH, FD = 8, 64
GH, GD = 4, 128
CHUNK = 64
WINDOWS = (2, 4, 8, 16)
CONV = 4
BW = 512
EH, KEYS, TOPK = 8, 128, 16
NE = KEYS * KEYS
ALPHA = (2 * DEPTH) ** 0.25
LN_EPS, RMS_EPS, L2_EPS = 1e-5, 1e-6, 1e-6
MASKED = -1e30
LEVELS = 6

CAND_RUNS = ((0, 1, 16), (1, 1, 8), (2, 1, 5), (3, 1, 4), (4, 1, 3), (5, 3, 2), (8, 8, 1))
NCAND = sum(n * w for _, n, w in CAND_RUNS)

U_POOL, U_GDN, U_Z, U_FQ, U_FK, U_FV, U_GATE, U_BR, U_OUT, U_WQ, U_KEYS, U_PLEG = 0, 1, 4, 5, 6, 7, 8, 14, 17, 19, 23, 24
UNITS = 26
UCOLS = 4096
WSLOTS = 3

C_ID, C_TRI, C_ONES, C_BTRI, C_AFTER, C_ZERO, C_CMASK, C_DMASK = (i * P for i in range(8))
C_LEV = 8 * P
C_BAND = C_LEV + LEVELS * P
C_IOTA = C_BAND + 3 * 4 * P
C_SIGN = C_IOTA + 64
NCONST = C_SIGN + 16
Q_CONV, Q_PSC, Q_NORM = 0, 48, 52
Q_BIAS, Q_ALOG = 56, 72
Q_WS = 80
Q_PW = Q_WS + KT * 16
Q_PT = Q_PW + 512
NPARAM = Q_PT + 2 * T

RING = 8
RANKS = EH * TOPK


def steps():
    s = [("hT", b, q) for b in range(2) for q in range(2)]
    s += [("small", 0), ("small", 1), ("pool", 0), ("pool", 1), ("softplus",)]
    s += [("gdn", 0, 0), ("gdn", 0, 1), ("cum", 0), ("cum", 1)]
    s += [("gdn", 1, 0), ("gdn", 1, 1), ("gbc", 0), ("gbc", 1)]
    s += [("gdn", 2, 0), ("gdn", 2, 1), ("pooled", 0), ("pooled", 1), ("z", 0), ("z", 1)]
    s += [("poolmix", 0), ("poolmix", 1)]
    s += [("tr", 0, 0), ("tr", 1, 0), ("tr", 2, 0), ("fq", 0), ("fq", 1)]
    s += [("t4", k, 0) for k in range(4)]
    s += [("tr", 0, 1), ("tr", 1, 1), ("tr", 2, 1), ("fk", 0), ("fk", 1)]
    s += [("t4", k, 1) for k in range(4)]
    s += [("lt", 0), ("at", 0), ("lt", 1), ("at", 1), ("fv", 0), ("fv", 1), ("t0", 0), ("t0", 1)]
    fox = []
    for b in range(2):
        for hp in range(4):
            fox.append(("fs", b, hp))
            if hp:
                fox += [("pt", b, hp - 1), ("fo", b, hp - 1)]
        fox += [("pt", b, 3), ("fo", b, 3), ("foT", b)]
    gates = [("gate", n, c, b) for n in range(3) for c in range(2) for b in range(2)]
    chain = []
    for lev in range(1, LEVELS):
        chain.append([("y", b, lev) for b in range(2)])
        chain.append([(k, b, lev) for b in range(2) for k in (("ty", "uy") if lev < LEVELS - 1 else ("uy",))])
    chain.append([("wT", 0), ("wT", 1)])
    for b in range(2):
        for c in range(2):
            chain.append([("vn", b, c)])
            chain.append([("o", b, c)] + ([("dS", b, c)] if (b, c) != (1, 1) else []))
        chain.append([("onorm", b)])
    fill = [fox[i:i + 3] for i in range(0, len(fox), 3)] + [[g] for g in gates]
    tail = [("oT", 0), ("oT", 1)]
    for i in range(max(len(chain), len(fill))):
        s += chain[i] if i < len(chain) else []
        s += fill[i] if i < len(fill) else []
    s += tail
    s += [("br", n, c, b) for n in range(3) for c in range(2) for b in range(2)]
    s += [("mT", b, q) for b in range(2) for q in range(2)]
    s += [("out", c, b) for c in range(2) for b in range(2)]
    s += [("ln1", 0), ("h1T", 0, 0), ("h1T", 0, 1), ("ln1", 1), ("h1T", 1, 0), ("h1T", 1, 1)]
    s += [("wq", u, p) for u in range(4) for p in range(2)]
    s += [("sc", 0, g) for g in range(4)] + [("sc", 1, g) for g in range(4)]
    s += [("topk", 0)]
    for c in range(2):
        s += [("pg", c, 0), ("pg", c, 1), ("pp", c, 0), ("pp", c, 1)]
    s += [("experts", 0), ("ln2", 0), ("topk", 1), ("experts", 1), ("ln2", 1)]
    return s


NO_BANK = {"softplus", "onorm", "ln1", "ln2", "topk", "experts"}
STEPS = steps()
FILLS = [s for s in STEPS if s[0] not in NO_BANK]
NBANK = 6


def build(nc, x, weights, params, lnrows, consts, experts, out):
    with ExitStack() as ctx:
        def sb(name, cols, dt=F32):
            return ctx.enter_context(nc.sbuf_tensor(name, [P, cols], dt))

        def sem(name):
            return ctx.enter_context(nc.semaphore(name))

        cst = sb("cst", NCONST)
        par = sb("par", NPARAM)
        lnr = sb("lnr", 2 * D)
        h = sb("h", NB * D).rearrange("p (b d) -> p b d", b=NB)
        hT = sb("hT", KT * T).rearrange("p (k t) -> p k t", k=KT)
        wring = sb("wring", WSLOTS * UCOLS).rearrange("p (s n) -> p s n", s=WSLOTS)
        arena = sb("arena", 28196)

        def at(off, n):
            return arena[:, off:off + n]

        brT = at(0, 12 * T).rearrange("p (k t) -> p k t", k=12)
        gates = at(3072, 2 * 3072).rearrange("p (b n) -> p b n", b=2)
        zs = at(9216, 1024).rearrange("p (b n) -> p b n", b=2)
        fq = at(3072, 1024).rearrange("p (k t) -> p k t", k=4)
        fk = at(4096, 1024).rearrange("p (k t) -> p k t", k=4)
        fv = at(5120, 1024).rearrange("p (b n) -> p b n", b=2)
        fE = at(6144, 1024).rearrange("p (i j k) -> p i j k", i=2, j=2)
        fP = at(7168, 1024).rearrange("p (i n) -> p i n", i=2)
        fo = at(8192, 512)
        cin = at(10240, 12 * 259).rearrange("p (k t) -> p k t", k=12)
        cT = at(13348, 12 * 256).rearrange("p (k t) -> p k t", k=12)
        late = [at(10240 + 1024 * i, 1024).rearrange("p (b n) -> p b n", b=2) for i in range(6)]
        lt, att, Um, Tm, Ym, Xm = late
        fT = at(16420, 4096).rearrange("p (b k n) -> p b k n", b=2, k=4)
        kbe = at(20516, 1024).rearrange("p (b n) -> p b n", b=2)
        kdec = at(21540, 1024).rearrange("p (b n) -> p b n", b=2)
        vb = at(22564, 1024).rearrange("p (b n) -> p b n", b=2)
        tmp4 = at(23588, 2048).rearrange("p (k n) -> p k n", k=4)
        poolx = at(23588, 1024).rearrange("p (b n) -> p b n", b=2)
        pooledT = at(24612, 1024).rearrange("p (g t) -> p g t", g=4)
        om = at(23588, 1024).rearrange("p (b n) -> p b n", b=2)
        Sm = at(24612, 1024).rearrange("p (i n) -> p i n", i=2)
        DT = at(25636, 1024).rearrange("p (b n) -> p b n", b=2)
        vnew = at(26660, 1024).rearrange("p (b n) -> p b n", b=2)
        sq = at(27684, 512)
        merged = at(10240, 2048).rearrange("p (b d) -> p b d", b=2)
        mT = at(12288, 2048).rearrange("p (k t) -> p k t", k=8)
        rr = at(14336, 2048).rearrange("p (b d) -> p b d", b=2)
        slots = at(0, RING * 2 * D).rearrange("p (s n) -> p s n", s=RING)
        qpT = at(12288, 4096).rearrange("p (k t) -> p k t", k=16)
        scs = at(16384, 4096).rearrange("p (b l n) -> p b l n", b=2, l=16)
        base = at(20480, 2048).rearrange("p (b d) -> p b d", b=2)
        tv = at(22528, 256).rearrange("p (l k) -> p l k", l=16)
        tif = at(22784, 256).rearrange("p (l k) -> p l k", l=16)
        cand = at(23040, 400).rearrange("p (h c) -> p h c", h=8)
        candi = at(23440, 400).rearrange("p (h c) -> p h c", h=8)
        top = at(23840, 128).rearrange("p (h k) -> p h k", h=8)
        posf = at(23968, 128).rearrange("p (h k) -> p h k", h=8)
        eq = at(24096, 1600).rearrange("p (h k c) -> p h k c", h=2, k=16)
        idxf = at(25696, 128).rearrange("p (h k) -> p h k", h=8)
        texp = at(25824, 128).rearrange("p (h k) -> p h k", h=8)
        diag = at(25952, 512).rearrange("p (i n) -> p i n", i=4)
        tiu = sb("tiu", 256, U32)[:, :].rearrange("p (l k) -> p l k", l=16)
        posu = sb("posu", 128, U32)[:, :].rearrange("p (h k) -> p h k", h=8)
        idxu = sb("idxu", NB * RANKS, U32)
        stage = sb("stage", 16, U32)
        wts = sb("wts", NB * RANKS)
        wst, dots, gel = sb("wst", 16), sb("dots", 16), sb("gel", 16)
        tsum, trec = sb("tsum", 8), sb("trec", 8)
        sm = sb("sm", 32)[:, :].rearrange("p (b n) -> p b n", b=2)
        spy, spe, spu, spl, spz, spd = (sb(f"sp{i}", 24)[:, :].rearrange("p (b n) -> p b n", b=2) for i in range(6))
        logs = sb("logs", 24)[:, :].rearrange("p (b n) -> p b n", b=2)
        spb, beta = sb("spb", 8)[:, :].rearrange("p (b n) -> p b n", b=2), sb("beta", 8)[:, :].rearrange("p (b n) -> p b n", b=2)
        aexp = sb("aexp", 4)
        cneg = sb("cneg", 24)[:, :].rearrange("p (b n) -> p b n", b=2)
        cpos, ecum = (sb(n, 16)[:, :].rearrange("p (b n) -> p b n", b=2) for n in ("cpos", "ecum"))
        glast, egl = (sb(n, 16)[:, :].rearrange("p (b n) -> p b n", b=2) for n in ("glast", "egl"))
        ssq, rsq = (sb(n, 16)[:, :].rearrange("p (b n) -> p b n", b=2) for n in ("ssq", "rsq"))
        rs2 = sb("rs2", 24)[:, :].rearrange("p (i n) -> p i n", i=6)
        fmax, fsum, frs = (sb(n, 16)[:, :].rearrange("p (b n) -> p b n", b=2) for n in ("fmax", "fsum", "frs"))
        oss, ors = (sb(n, 8)[:, :].rearrange("p (b n) -> p b n", b=2) for n in ("oss", "ors"))
        bst, mv, rstd = sb("bst", 12), sb("mv", 2), sb("rstd", 1)

        psum = ctx.enter_context(nc.psum_tensor("psum", [P, NBANK, 512], F32))
        acc = ctx.enter_context(nc.psum_tensor("acc", [P, D], F32))

        ident = cst[:, C_ID:C_ID + P]
        tri = cst[:, C_TRI:C_TRI + P]
        tri_ones = cst[:, C_TRI:C_TRI + 2 * P]
        ones = cst[:, C_ONES:C_ONES + P]
        btri = cst[:, C_BTRI:C_BTRI + P]
        after = cst[:, C_AFTER:C_AFTER + P]
        zero = cst[:, C_ZERO:C_ZERO + P]
        fmask = cst[:, C_ZERO:C_ZERO + 2 * P]
        dmask = cst[:, C_DMASK:C_DMASK + P]

        def lev(i):
            return cst[:, C_LEV + i * P:C_LEV + (i + 1) * P]

        def band(kind, g):
            return cst[:, C_BAND + (4 * kind + g) * P:][:, 0:P]

        def heads(ap, n=GH):
            return ap.rearrange("p (h d) -> p h d", h=n)

        def over(ap, n):
            return ap.unsqueeze(2).broadcast_to([ap.shape[0], ap.shape[1], n])

        def each(ap, n):
            return ap.unsqueeze(1).broadcast_to([ap.shape[0], n, ap.shape[1]])

        consts_in, x_in, out_sent = sem("consts_in"), sem("x_in"), sem("out_sent")
        params_in, ln_in = sem("params_in"), sem("ln_in")
        unit_in = [sem(f"unit_in{i}") for i in range(WSLOTS)]
        unit_used = [sem(f"unit_used{i}") for i in range(WSLOTS)]
        bank_filled = [sem(f"bank_filled{i}") for i in range(NBANK)]
        bank_drained = [sem(f"bank_drained{i}") for i in range(NBANK)]
        dve_step, act_step, pe_step = sem("dve_step"), sem("act_step"), sem("pe_step")
        sp_neg, sp_exp, sp_one, sp_ln, logs_ready = (sem(n) for n in ("sp_neg", "sp_exp", "sp_one", "sp_ln", "logs_ready"))
        ecum_ready, dt_ready, conv_ready, silu_ready = (sem(n) for n in ("ecum_ready", "dt_ready", "conv_ready", "silu_ready"))
        sq_ready, ss_ready, rs_ready = (sem(n) for n in ("sq_ready", "ss_ready", "rs_ready"))
        u_init, x1_ready, x_ready = (sem(n) for n in ("u_init", "x1_ready", "x_ready"))
        fmax_ready, fexp_ready = sem("fmax_ready"), sem("fexp_ready")
        oss_ready, ors_ready, on_ready = (sem(n) for n in ("oss_ready", "ors_ready", "on_ready"))
        merged_ready, var_ready, rstd_ready = (sem(n) for n in ("merged_ready", "var_ready", "rstd_ready"))
        h1_ready, h2_ready = sem("h1_ready"), sem("h2_ready")
        top_ready, texp_ready, idx_ready = (sem(n) for n in ("top_ready", "texp_ready", "idx_ready"))
        slot_in = [sem(f"slot_in{i}") for i in range(RING)]
        idx_staged, wts_staged = sem("idx_staged"), sem("wts_staged")
        dot_ready, gelu_ready, diag_ready, row_used = (sem(n) for n in ("dot_ready", "gelu_ready", "diag_ready", "row_used"))
        acc_filled, acc_drained, base_ready = sem("acc_filled"), sem("acc_drained"), sem("base_ready")

        def place(L, step):
            n = L * len(FILLS) + FILLS.index(step)
            return n % NBANK, n // NBANK

        def bank(L, step):
            return psum[:, place(L, step)[0], :]

        def filled(L, step):
            b, use = place(L, step)
            return bank_filled[b], use + 1

        def drained(L, step):
            b, use = place(L, step)
            return bank_drained[b], use + 1

        def wt(L, u):
            return wring[:, (L * UNITS + u) % WSLOTS, :]

        block = ctx.enter_context(nc.Block())

        @block.sync
        def _(sp):
            sp.dma_start(cst[:, :], consts[:, :]).then_inc(consts_in, 16)
            for b in range(NB):
                sp.dma_start(h[:, b, :], x[b * P:(b + 1) * P, :]).then_inc(x_in, 16)
            full, rest = divmod(DEPTH * UNITS, WSLOTS)
            for s in range(WSLOTS):
                sp.dma_start(wring[:, s, :], weights[s]).then_inc(unit_in[s], 16)
            with sp.Fori(1, full) as r:
                for s in range(WSLOTS):
                    sp.wait_ge(unit_used[s], r)
                    sp.nop(nofuse=True)
                    sp.dma_start(wring[:, s, :], weights[bass.ds(r * WSLOTS + s, 1)].rearrange("a p n -> p (a n)")).then_inc(unit_in[s], 16)
            for s in range(rest):
                sp.wait_ge(unit_used[s], full)
                sp.dma_start(wring[:, s, :], weights[full * WSLOTS + s]).then_inc(unit_in[s], 16)
            for b in range(NB):
                sp.wait_ge(h2_ready, (DEPTH - 1) * NB + b + 1)
                sp.dma_start(out[b * P:(b + 1) * P, :], h[:, b, :]).then_inc(out_sent, 16)
            sp.wait_ge(out_sent, 16 * NB)

        @block.gpsimd
        def _(pool):
            pool.dma_start(par[:, :], params[0]).then_inc(params_in, 16)
            pool.dma_start(lnr[:, :], lnrows[0, 0]).then_inc(ln_in, 16)
            pool.sem_inc(row_used, RING)
            pool.wait_ge(consts_in, 16)
            for L in range(DEPTH):
                for step in STEPS:
                    kind = step[0]
                    if kind == "y" and step[2] < LEVELS - 1:
                        _, b, l = step
                        pool.wait_ge(*filled(L, step))
                        nc.gpsimd.tensor_tensor(heads(Xm[:, b, :]), heads(lt[:, b, :]), each(lev(l + 1), GH), ALU.mult).then_inc(x_ready, 1)
                    if kind == "topk" and step[1] == 0:
                        pool.wait_ge(h1_ready, NB * (L + 1))
                        pool.dma_start(lnr[:, :], lnrows[L, 1]).then_inc(ln_in, 16)
                    if kind == "experts":
                        b = step[1]
                        n0 = (L * NB + b) * RANKS
                        pool.wait_ge(idx_ready, L * NB + b + 1)
                        pool.wait_ge(*filled(L, ("sc", 1, 3)))
                        with pool.Fori(0, EH) as r:
                            for i in range(TOPK):
                                pool.wait_ge(row_used, r * TOPK + (n0 + i + 1))
                                pool.nop(nofuse=True)
                                if i % RING == 0:
                                    nc.gpsimd.tensor_copy(stage[:, i:i + RING], idxu[:, bass.ds(r * TOPK + (b * RANKS + i), RING)]).then_inc(idx_staged, 1)
                                    pool.wait_ge(idx_staged, r * 2 + ((L * NB + b) * 2 * EH + i // RING + 1))
                                    pool.nop(nofuse=True)
                                nc.gpsimd.indirect_dma_start(
                                    slots[:, i % RING, :], None, experts[:, :],
                                    bass.IndirectOffsetOnAxis(stage[:, i:i + 1], 0)).then_inc(slot_in[i % RING], 16)
                        if b == 0 and L + 1 < DEPTH:
                            pool.wait_ge(*filled(L, ("pp", 1, 1)))
                            pool.dma_start(par[:, :], params[L + 1]).then_inc(params_in, 16)
                    if kind == "ln2" and step[1] == 1 and L + 1 < DEPTH:
                        pool.wait_ge(h2_ready, NB * (L + 1))
                        pool.dma_start(lnr[:, :], lnrows[L + 1, 0]).then_inc(ln_in, 16)

        @block.tensor
        def _(pe):
            mm, tp = nc.tensor.matmul, nc.tensor.transpose
            links = [0]
            pe.wait_ge(consts_in, 16)

            def unit(L, u):
                n = L * UNITS + u
                pe.wait_ge(unit_in[n % WSLOTS], 16 * (n // WSLOTS + 1))
                return wt(L, u)

            def token_major(ps, w, src, b, kt, c0, width, step):
                for k in range(kt):
                    last = mm(ps[:, 0:width], src[:, k, b * P:(b + 1) * P], w[:, k * step + c0:k * step + c0 + width], start=k == 0, stop=k == kt - 1)
                return last

            def feature_major(ps, w, p):
                for i in range(2):
                    for k in range(KT):
                        last = mm(ps[:, i * T:(i + 1) * T], w[:, k * 512 + (2 * p + i) * P:][:, 0:P], hT[:, k, :], start=k == 0, stop=k == KT - 1)
                return last

            for L in range(DEPTH):
                for step in FILLS + [("experts", 0), ("experts", 1)]:
                    kind = step[0]
                    if kind == "experts":
                        b = step[1]
                        n0 = (L * NB + b) * RANKS
                        if L or b:
                            pe.wait_ge(acc_drained, L * NB + b)
                        for c in range(2):
                            mm(acc[:, c * 512:(c + 1) * 512], zero, cst[:, 0:512], start=True, stop=False)
                        with pe.Fori(0, EH) as r:
                            for i in range(TOPK):
                                pe.wait_ge(diag_ready, r * TOPK + (n0 + i + 2))
                                pe.nop(nofuse=True)
                                for c in range(2):
                                    last = mm(acc[:, c * 512:(c + 1) * 512], diag[:, i % 4, :], slots[:, i % RING, D + c * 512:D + (c + 1) * 512], start=False, stop=False)
                                last.then_inc(row_used, 1)
                        for c in range(2):
                            last = mm(acc[:, c * 512:(c + 1) * 512], zero, cst[:, 0:512], start=False, stop=True)
                        last.then_inc(acc_filled, 1)
                        continue
                    bk, use = place(L, step)
                    ps = psum[:, bk, :]
                    if use:
                        pe.wait_ge(bank_drained[bk], use)
                    frees = None
                    if kind in ("hT", "h1T"):
                        _, b, q = step
                        if kind == "h1T":
                            pe.wait_ge(h1_ready, L * NB + b + 1)
                        elif L:
                            pe.wait_ge(h2_ready, (L - 1) * NB + b + 1)
                        else:
                            pe.wait_ge(x_in, 16 * NB)
                        for j in range(4):
                            last = tp(ps[:, j * P:(j + 1) * P], h[:, b, (4 * q + j) * P:(4 * q + j + 1) * P], ident)
                    elif kind == "small":
                        b = step[1]
                        pe.wait_ge(params_in, 16 * (L + 1))
                        pe.wait_ge(*drained(L, ("hT", b, 1)))
                        last = token_major(ps, par[:, Q_WS:], hT, b, KT, 0, 16, 16)
                    elif kind in ("pool", "z", "fv"):
                        b = step[1]
                        u = {"pool": U_POOL, "z": U_Z, "fv": U_FV}[kind]
                        last = token_major(ps, unit(L, u), hT, b, KT, 0, 512, 512)
                        frees = u if b else None
                    elif kind in ("gdn", "fq", "fk", "wq"):
                        p = step[-1]
                        u = {"gdn": U_GDN, "fq": U_FQ, "fk": U_FK, "wq": U_WQ}[kind] + (step[1] if len(step) == 3 else 0)
                        if kind == "wq" and u == U_WQ:
                            pe.wait_ge(*drained(L, ("h1T", 1, 1)))
                        last = feature_major(ps, unit(L, u), p)
                        frees = u if p else None
                    elif kind == "cum":
                        b = step[1]
                        pe.wait_ge(logs_ready, L + 1)
                        if b:
                            mm(ps[:, 0:8], ones, logs[:, 0, 0:8], start=True, stop=False)
                        mm(ps[:, 0:8], tri, logs[:, b, 0:8], start=not b, stop=True)
                        mm(ps[:, 8:12], btri, logs[:, b, 8:12], start=True, stop=True)
                        last = mm(ps[:, 12:16], after, logs[:, b, 8:12], start=True, stop=True)
                    elif kind == "gbc":
                        b = step[1]
                        for hd in range(GH):
                            last = mm(ps[:, hd * P:(hd + 1) * P], logs[:, b, 8 + hd:9 + hd].broadcast_to([P, P]), btri, start=True, stop=True)
                    elif kind == "pooled":
                        pe.wait_ge(*drained(L, ("pool", 1)))
                        for i in range(2):
                            g = 2 * step[1] + i
                            cs = slice(g * P, (g + 1) * P)
                            mm(ps[:, i * T:i * T + P], poolx[:, 0, cs], band(0, g), start=True, stop=True)
                            mm(ps[:, i * T + P:(i + 1) * T], poolx[:, 0, cs], band(1, g), start=True, stop=False)
                            last = mm(ps[:, i * T + P:(i + 1) * T], poolx[:, 1, cs], band(2, g), start=False, stop=True)
                    elif kind == "poolmix":
                        pe.wait_ge(*drained(L, ("pooled", step[1])))
                        for i in range(2):
                            g = 2 * step[1] + i
                            last = mm(ps[:, i * T:(i + 1) * T], par[:, Q_PW + g * P:Q_PW + (g + 1) * P], pooledT[:, g, :], start=True, stop=True)
                    elif kind == "tr":
                        _, k3, b = step
                        pe.wait_ge(silu_ready, 3 * L + k3 + 1)
                        for hd in range(GH):
                            last = tp(ps[:, hd * P:(hd + 1) * P], cT[:, 4 * k3 + hd, b * P:(b + 1) * P], ident)
                    elif kind == "t4":
                        _, k4, b = step
                        pe.wait_ge(*drained(L, ("tr", k4 // 2, b)))
                        for hd in range(GH):
                            last = tp(ps[:, hd * P:(hd + 1) * P], tmp4[:, k4, hd * P:(hd + 1) * P], ident)
                    elif kind in ("lt", "at"):
                        b = step[1]
                        moving = 3 if kind == "lt" else 0
                        pe.wait_ge(*drained(L, ("t4", 2, b)))
                        pe.wait_ge(*drained(L, ("t4", moving, b)))
                        for hd in range(GH):
                            cs = slice(hd * P, (hd + 1) * P)
                            last = mm(ps[:, cs], fT[:, b, 2, cs], fT[:, b, moving, cs], start=True, stop=True)
                    elif kind == "t0":
                        b = step[1]
                        pe.wait_ge(u_init, L * NB + b + 1)
                        for hd in range(GH):
                            last = tp(ps[:, hd * P:(hd + 1) * P], Um[:, b, hd * P:(hd + 1) * P], ident)
                    elif kind == "y":
                        _, b, l = step
                        if l == 1:
                            pe.wait_ge(x1_ready, L * NB + b + 1)
                            pe.wait_ge(*drained(L, ("t0", b)))
                        else:
                            pe.wait_ge(x_ready, L * NB * (LEVELS - 2) + (l - 2) * NB + b + 1)
                            pe.wait_ge(*drained(L, ("ty", b, l - 1)))
                        for hd in range(GH):
                            cs = slice(hd * P, (hd + 1) * P)
                            last = mm(ps[:, cs], Xm[:, b, cs], Tm[:, b, cs], start=True, stop=True)
                    elif kind in ("ty", "uy"):
                        _, b, l = step
                        pe.wait_ge(*drained(L, ("y", b, l)))
                        if l == 1:
                            pe.wait_ge(u_init, L * NB + b + 1)
                        else:
                            pe.wait_ge(*drained(L, ("uy", b, l - 1)))
                        for hd in range(GH):
                            cs = slice(hd * P, (hd + 1) * P)
                            if kind == "ty":
                                last = mm(ps[:, cs], Um[:, b, cs], Ym[:, b, cs], start=True, stop=True)
                            else:
                                last = mm(ps[:, cs], Ym[:, b, cs], Um[:, b, cs], start=True, stop=True)
                    elif kind == "wT":
                        b = step[1]
                        pe.wait_ge(*drained(L, ("uy", b, LEVELS - 1)))
                        for hd in range(GH):
                            cs = slice(hd * P, (hd + 1) * P)
                            last = mm(ps[:, cs], kbe[:, b, cs], Um[:, b, cs], start=True, stop=True)
                    elif kind in ("vn", "o"):
                        _, b, c = step
                        n = 2 * b + c
                        rows = slice(c * CHUNK, (c + 1) * CHUNK)
                        if kind == "vn":
                            pe.wait_ge(*drained(L, ("wT", b)))
                            if n:
                                pe.wait_ge(*drained(L, ("dS", (n - 1) // 2, (n - 1) % 2)))
                        else:
                            pe.wait_ge(*drained(L, ("vn", b, c)))
                        for hd in range(GH):
                            cs = slice(hd * P, (hd + 1) * P)
                            t0 = hd * P + c * CHUNK
                            left = Tm[:, b, t0:t0 + CHUNK] if kind == "vn" else fT[:, b, 1, t0:t0 + CHUNK]
                            if n:
                                mm(ps[rows, cs], left, Sm[:, n % 2, cs], start=True, stop=False)
                            if kind == "vn":
                                last = mm(ps[rows, cs], Um[:, b, t0:t0 + CHUNK], vb[:, b, cs], start=not n, stop=True)
                            else:
                                last = mm(ps[rows, cs], att[rows, b, t0:t0 + CHUNK], vnew[rows, b, cs], start=not n, stop=True)
                    elif kind == "dS":
                        _, b, c = step
                        rows = slice(c * CHUNK, (c + 1) * CHUNK)
                        for hd in range(GH):
                            cs = slice(hd * P, (hd + 1) * P)
                            last = mm(ps[:, cs], kdec[rows, b, cs], vnew[rows, b, cs], start=True, stop=True)
                    elif kind == "oT":
                        b = step[1]
                        pe.wait_ge(on_ready, L * NB + b + 1)
                        for hd in range(GH):
                            last = tp(ps[:, hd * P:(hd + 1) * P], om[:, b, hd * P:(hd + 1) * P], ident)
                    elif kind == "fs":
                        _, b, hp = step
                        if hp == 0:
                            pe.wait_ge(*drained(L, ("fq", 1)))
                            pe.wait_ge(*drained(L, ("fk", 1)))
                        width = (b + 1) * P
                        for j in range(2):
                            hd = 2 * hp + j
                            rows = slice(j * FD, (j + 1) * FD)
                            if j:
                                links[0] += 1
                                last.then_inc(pe_step, 1)
                                pe.wait_ge(pe_step, links[0])
                            mm(ps[:, j * T:j * T + width], fq[rows, hp, b * P:(b + 1) * P], fk[rows, hp, 0:width], start=True, stop=False)
                            last = mm(ps[:, j * T:j * T + width], logs[:, 0, hd:hd + 1].broadcast_to([P, P]), tri_ones[:, 0:width], start=False, stop=b == 0)
                            if b:
                                last = mm(ps[:, j * T + P:(j + 1) * T], logs[:, 1, hd:hd + 1].broadcast_to([P, P]), tri, start=False, stop=True)
                    elif kind == "pt":
                        _, b, hp = step
                        pe.wait_ge(fexp_ready, 2 * (L * 8 + b * 4 + hp + 1))
                        for j in range(2):
                            for kb in range(b + 1):
                                col = (j * (b + 1) + kb) * P
                                last = tp(ps[:, col:col + P], fE[:, hp % 2, j, kb * P:(kb + 1) * P], ident)
                    elif kind == "fo":
                        _, b, hp = step
                        pe.wait_ge(*drained(L, ("pt", b, hp)))
                        pe.wait_ge(*drained(L, ("fv", 1)))
                        for j in range(2):
                            hd = 2 * hp + j
                            for kb in range(b + 1):
                                col = (j * (b + 1) + kb) * P
                                last = mm(ps[:, j * FD:(j + 1) * FD], fP[:, hp % 2, col:col + P], fv[:, kb, hd * FD:(hd + 1) * FD], start=kb == 0, stop=kb == b)
                    elif kind == "foT":
                        b = step[1]
                        pe.wait_ge(*drained(L, ("fo", b, 3)))
                        for j in range(4):
                            last = tp(ps[:, j * P:(j + 1) * P], fo[:, j * P:(j + 1) * P], ident)
                    elif kind == "gate":
                        _, n, c, b = step
                        last = token_major(ps, unit(L, U_GATE + 2 * n + c), hT, b, KT, 0, 512, 512)
                        frees = U_GATE + 2 * n + c if b else None
                    elif kind == "br":
                        _, n, c, b = step
                        if n == 0 and c == 0:
                            pe.wait_ge(*drained(L, ("foT", b)))
                        if n == 1:
                            pe.wait_ge(*drained(L, ("poolmix", 1)))
                        if n == 2:
                            pe.wait_ge(*drained(L, ("oT", b)))
                        last = token_major(ps, unit(L, U_BR + n), brT[:, 4 * n:4 * n + 4, :], b, 4, c * 512, 512, D)
                        frees = U_BR + n if (b and c) else None
                    elif kind == "mT":
                        _, b, q = step
                        pe.wait_ge(merged_ready, L * 4 + 2 + b + 1)
                        for j in range(4):
                            last = tp(ps[:, j * P:(j + 1) * P], merged[:, b, (4 * q + j) * P:(4 * q + j + 1) * P], ident)
                    elif kind == "out":
                        _, c, b = step
                        pe.wait_ge(*drained(L, ("mT", b, 1)))
                        last = token_major(ps, unit(L, U_OUT + c), mT, b, KT, 0, 512, 512)
                        frees = U_OUT + c if b else None
                    elif kind == "sc":
                        _, b, g = step
                        pe.wait_ge(*drained(L, ("wq", g, 1)))
                        w = unit(L, U_KEYS)
                        for j in range(4):
                            li = 4 * g + j
                            last = mm(ps[:, j * P:(j + 1) * P], qpT[:, li, b * P:(b + 1) * P], w[:, li * P:(li + 1) * P], start=True, stop=True)
                    elif kind == "pg":
                        _, c, b = step
                        last = token_major(ps, unit(L, U_PLEG + c), hT, b, KT, 0, 512, 512)
                        frees = U_PLEG + c if b else None
                    elif kind == "pp":
                        _, c, b = step
                        pT = par[:, Q_PT:Q_PT + 2 * T].rearrange("p (k t) -> p k t", k=2)
                        last = token_major(ps, wt(L, U_KEYS)[:, 2048:4096], pT, b, 2, c * 512, 512, D)
                        frees = U_KEYS if (b and c) else None
                    last.then_inc(bank_filled[bk], 1)
                    if frees is not None:
                        pe.wait_ge(bank_filled[bk], use + 1)
                        pe.sem_inc(unit_used[(L * UNITS + frees) % WSLOTS], 1)

        @block.scalar
        def _(act):
            AC = nc.scalar.activation
            links = [0]

            def link(ins):
                links[0] += 1
                ins.then_inc(act_step, 1)
                act.wait_ge(act_step, links[0])

            def inv_sqrt(dst, src, tmp, ready):
                link(AC(tmp, src, ACT.Ln))
                AC(dst, tmp, ACT.Exp, scale=-0.5).then_inc(ready, 1)

            act.wait_ge(consts_in, 16)
            for L in range(DEPTH):
                for step in STEPS:
                    kind = step[0]
                    if kind == "softplus":
                        act.wait_ge(sp_neg, L + 1)
                        AC(spe, spz, ACT.Exp).then_inc(sp_exp, 1)
                        AC(spb, sm[:, :, 12:16], ACT.Exp, scale=-1.0).then_inc(sp_exp, 1)
                        AC(aexp[:, :], par[:, Q_ALOG:Q_ALOG + 4], ACT.Exp).then_inc(sp_exp, 1)
                        act.wait_ge(sp_one, L + 1)
                        AC(spl, spu, ACT.Ln).then_inc(sp_ln, 1)
                        continue
                    if kind in ("ln1", "ln2"):
                        n = L * 4 + (step[1] if kind == "ln1" else 2 + step[1]) + 1
                        act.wait_ge(var_ready, n)
                        inv_sqrt(rstd[:, :], mv[:, 1:2], mv[:, 1:2], rstd_ready)
                        continue
                    if kind == "onorm":
                        b = step[1]
                        act.wait_ge(oss_ready, L * NB + b + 1)
                        inv_sqrt(ors[:, b, :], oss[:, b, :], oss[:, b, :], ors_ready)
                        continue
                    if kind == "topk":
                        act.wait_ge(top_ready, L * NB + step[1] + 1)
                        AC(texp, texp, ACT.Exp).then_inc(texp_ready, 1)
                        continue
                    if kind == "experts":
                        n0 = (L * NB + step[1]) * RANKS
                        with act.Fori(0, EH) as r:
                            for i in range(TOPK):
                                act.wait_ge(dot_ready, r * TOPK + (n0 + i + 1))
                                act.nop(nofuse=True)
                                AC(gel[:, i:i + 1], dots[:, i:i + 1], ACT.Gelu).then_inc(gelu_ready, 1)
                        continue
                    ps = bank(L, step)
                    bk, use = place(L, step)
                    done = bank_drained[bk]
                    if kind in ("small", "lt", "at", "ty", "uy", "dS", "br", "out", "pp"):
                        continue
                    if kind == "cum":
                        b = step[1]
                        act.wait_ge(*drained(L, step))
                        AC(ecum[:, b, :], cpos[:, b, :], ACT.Exp).then_inc(ecum_ready, 1)
                        continue
                    if kind == "gbc":
                        b = step[1]
                        act.wait_ge(*drained(L, step))
                        AC(DT[:, b, :], DT[:, b, :], ACT.Exp).then_inc(dt_ready, 1)
                        AC(egl[:, b, :], glast[:, b, :], ACT.Exp).then_inc(dt_ready, 1)
                        continue
                    if kind == "tr":
                        _, k3, b = step
                        if k3 < 2:
                            n = L * 4 + b * 2 + k3 + 1
                            act.wait_ge(*filled(L, step))
                            if n > 1:
                                act.wait_ge(ss_ready, n - 1)
                            AC(sq, ps, ACT.Square).then_inc(sq_ready, 1)
                            act.wait_ge(ss_ready, n)
                            inv_sqrt(rsq[:, b, 4 * k3:4 * k3 + 4], ssq[:, b, 4 * k3:4 * k3 + 4], ssq[:, b, 4 * k3:4 * k3 + 4], rs_ready)
                        continue
                    if kind == "fs":
                        _, b, hp = step
                        act.wait_ge(fmax_ready, L * 8 + b * 4 + hp + 1)
                        for j in range(2):
                            hd = 2 * hp + j
                            e = fE[:, hp % 2, j, 0:(b + 1) * P]
                            AC(e, e, ACT.Exp, bias=fmax[:, b, hd:hd + 1], accum_out=fsum[:, b, hd:hd + 1]).then_inc(fexp_ready, 1)
                        continue
                    if kind == "fo":
                        continue
                    act.wait_ge(*filled(L, step))
                    if kind in ("hT", "h1T", "mT"):
                        _, b, q = step
                        dst = mT if kind == "mT" else hT
                        last = AC(dst[:, 4 * q:4 * q + 4, b * P:(b + 1) * P], ps.rearrange("p (k t) -> p k t", k=4), ACT.Copy)
                    elif kind == "pool":
                        last = AC(poolx[:, step[1], :], ps, ACT.Copy)
                    elif kind == "gdn":
                        _, u, p = step
                        if u == 0 and p == 0:
                            act.wait_ge(logs_ready, L + 1)
                        last = AC(cin[:, 4 * u + 2 * p:4 * u + 2 * p + 2, 3:3 + T], ps.rearrange("p (k t) -> p k t", k=2), ACT.Copy)
                    elif kind == "pooled":
                        last = AC(pooledT[:, 2 * step[1]:2 * step[1] + 2, :], ps.rearrange("p (k t) -> p k t", k=2), ACT.Copy)
                    elif kind == "poolmix":
                        for i in range(2):
                            g = 2 * step[1] + i
                            last = AC(brT[:, 4 + g, :], ps[:, i * T:(i + 1) * T], ACT.Copy, scale=par[:, Q_PSC + g:Q_PSC + g + 1])
                    elif kind == "z":
                        last = AC(zs[:, step[1], :], ps, ACT.Silu)
                    elif kind == "fq":
                        last = AC(fq[:, 2 * step[1]:2 * step[1] + 2, :], ps.rearrange("p (k t) -> p k t", k=2), ACT.Copy, scale=FD ** -0.5)
                    elif kind == "fk":
                        last = AC(fk[:, 2 * step[1]:2 * step[1] + 2, :], ps.rearrange("p (k t) -> p k t", k=2), ACT.Copy)
                    elif kind == "fv":
                        last = AC(fv[:, step[1], :], ps, ACT.Copy)
                    elif kind == "t4":
                        last = AC(fT[:, step[2], step[1], :], ps, ACT.Copy)
                    elif kind == "t0":
                        last = AC(Tm[:, step[1], :], ps, ACT.Copy)
                    elif kind == "y":
                        last = AC(Ym[:, step[1], :], ps, ACT.Copy)
                    elif kind == "wT":
                        last = AC(Tm[:, step[1], :], ps, ACT.Copy, scale=-1.0)
                    elif kind in ("vn", "o"):
                        _, b, c = step
                        rows = slice(c * CHUNK, (c + 1) * CHUNK)
                        last = AC((vnew if kind == "vn" else om)[rows, b, :], ps[rows, :], ACT.Copy)
                    elif kind == "oT":
                        b = step[1]
                        last = AC(brT[:, 8:12, b * P:(b + 1) * P], ps.rearrange("p (k t) -> p k t", k=4), ACT.Copy, scale=par[:, Q_NORM:Q_NORM + 1])
                    elif kind == "pt":
                        _, b, hp = step
                        w = 2 * (b + 1) * P
                        last = AC(fP[:, hp % 2, 0:w], ps[:, 0:w], ACT.Copy)
                    elif kind == "foT":
                        b = step[1]
                        last = AC(brT[:, 0:4, b * P:(b + 1) * P], ps.rearrange("p (k t) -> p k t", k=4), ACT.Copy)
                    elif kind == "gate":
                        _, n, c, b = step
                        last = AC(gates[:, b, (2 * n + c) * 512:(2 * n + c + 1) * 512], ps, ACT.Sigmoid)
                    elif kind == "wq":
                        _, u, p = step
                        last = AC(qpT[:, 4 * u + 2 * p:4 * u + 2 * p + 2, :], ps.rearrange("p (k t) -> p k t", k=2), ACT.Copy)
                    elif kind == "sc":
                        _, b, g = step
                        last = AC(scs[:, b, 4 * g:4 * g + 4, :], ps.rearrange("p (l n) -> p l n", l=4), ACT.Copy)
                    elif kind == "pg":
                        _, c, b = step
                        last = AC(base[:, b, c * 512:(c + 1) * 512], ps, ACT.Sigmoid)
                    last.then_inc(done, 1)
                    if kind == "gdn" and step[2] == 1:
                        u = step[1]
                        act.wait_ge(conv_ready, 3 * L + u + 1)
                        AC(cT[:, 4 * u:4 * u + 4, :], cT[:, 4 * u:4 * u + 4, :], ACT.Silu).then_inc(silu_ready, 1)

        @block.vector
        def _(dve):
            TT, TS, STT, CP = nc.vector.tensor_tensor, nc.vector.tensor_scalar, nc.vector.scalar_tensor_tensor, nc.vector.tensor_copy
            links = [0]

            def link(ins):
                links[0] += 1
                ins.then_inc(dve_step, 1)
                dve.wait_ge(dve_step, links[0])

            def layer_norm(r, b, n):
                nc.vector.bn_stats(bst[:, 0:6], r[:, 0:512])
                link(nc.vector.bn_stats(bst[:, 6:12], r[:, 512:1024]))
                link(nc.vector.bn_aggr(mv[:, :], bst[:, :]))
                TS(mv[:, 1:2], mv[:, 1:2], LN_EPS, None, ALU.add).then_inc(var_ready, 1)
                dve.wait_ge(rstd_ready, n)
                link(TS(r, r, mv[:, 0:1], rstd[:, 0:1], ALU.subtract, ALU.mult))
                link(TT(r, r, lnr[:, 0:D], ALU.mult))
                return TT(h[:, b, :], r, lnr[:, D:2 * D], ALU.add)

            dve.sem_inc(diag_ready, 1)
            dve.wait_ge(consts_in, 16)
            for L in range(DEPTH):
                for step in STEPS:
                    kind = step[0]
                    if kind == "softplus":
                        dve.wait_ge(*drained(L, ("small", 1)))
                        link(TT(spy, sm[:, :, 0:12], each(cst[:, C_SIGN:C_SIGN + 12], 2), ALU.mult))
                        STT(spz, spy, -1.0, spy, ALU.mult, ALU.min).then_inc(sp_neg, 1)
                        nc.vector.memset(cin[:, :, 0:3], 0.0)
                        dve.wait_ge(sp_exp, 3 * (L + 1))
                        TS(spb, spb, 1.0, None, ALU.add)
                        TS(spu, spe, 1.0, None, ALU.add).then_inc(sp_one, 1)
                        dve.wait_ge(sp_one, L + 1)
                        nc.vector.reciprocal(beta, spb)
                        link(TS(spz, spu, -1.0, 0.0, ALU.add, ALU.is_equal))
                        link(STT(spd, spu, -1.0, spz, ALU.add, ALU.add))
                        link(nc.vector.reciprocal(spd, spd))
                        link(TT(spd, spd, spe, ALU.mult))
                        dve.wait_ge(sp_ln, L + 1)
                        link(TT(spz, spl, spz, ALU.add))
                        link(TT(spd, spd, spz, ALU.mult))
                        link(STT(logs, spy, 0.0, spd, ALU.max, ALU.add))
                        STT(logs[:, :, 8:12], logs[:, :, 8:12], -1.0, each(aexp[:, :], 2), ALU.mult, ALU.mult).then_inc(logs_ready, 1)
                        continue
                    if kind == "onorm":
                        b = step[1]
                        o = heads(om[:, b, :])
                        dve.wait_ge(*drained(L, ("o", b, 1)))
                        link(TT(heads(sq), o, o, ALU.mult))
                        link(nc.vector.tensor_reduce(oss[:, b, :], heads(sq), AX_X, ALU.add))
                        TS(oss[:, b, :], oss[:, b, :], 1.0 / GD, RMS_EPS, ALU.mult, ALU.add).then_inc(oss_ready, 1)
                        dve.wait_ge(ors_ready, L * NB + b + 1)
                        link(TT(o, o, over(ors[:, b, :], GD), ALU.mult))
                        TT(o, o, heads(zs[:, b, :]), ALU.mult).then_inc(on_ready, 1)
                        continue
                    if kind == "ln1":
                        b = step[1]
                        if b == 0:
                            dve.wait_ge(ln_in, 16 * (2 * L + 1))
                        dve.wait_ge(*drained(L, ("out", 1, b)))
                        layer_norm(rr[:, b, :], b, L * 4 + b + 1).then_inc(h1_ready, 1)
                        continue
                    if kind == "ln2":
                        b = step[1]
                        dve.wait_ge(ln_in, 16 * (2 * L + 2))
                        dve.wait_ge(acc_filled, L * NB + b + 1)
                        dve.wait_ge(base_ready, L * NB + b + 1)
                        for c in range(2):
                            cs = slice(c * 512, (c + 1) * 512)
                            last = TT(base[:, b, cs], base[:, b, cs], acc[:, cs], ALU.add)
                        last.then_inc(acc_drained, 1)
                        dve.wait_ge(acc_drained, L * NB + b + 1)
                        layer_norm(base[:, b, :], b, L * 4 + 2 + b + 1).then_inc(h2_ready, 1)
                        continue
                    if kind == "topk":
                        b = step[1]
                        dve.wait_ge(*drained(L, ("sc", b, 3)))
                        for li in range(16):
                            last = nc.vector.max(tv[:, li, 0:8], scs[:, b, li, :])
                        link(last)
                        for li in range(16):
                            last = nc.vector.max_index(tiu[:, li, 0:8], tv[:, li, 0:8], scs[:, b, li, :])
                        link(last)
                        for li in range(16):
                            last = nc.vector.match_replace(scs[:, b, li, :], tv[:, li, 0:8], scs[:, b, li, :], -3e38)
                        link(last)
                        for li in range(16):
                            last = nc.vector.max(tv[:, li, 8:16], scs[:, b, li, :])
                        link(last)
                        for li in range(16):
                            last = nc.vector.max_index(tiu[:, li, 8:16], tv[:, li, 8:16], scs[:, b, li, :])
                        link(last)
                        link(CP(tif, tiu))
                        v2 = tv.rearrange("p (h s) k -> p h s k", s=2)
                        i2 = tif.rearrange("p (h s) k -> p h s k", s=2)
                        link(TS(i2[:, :, 0, :], i2[:, :, 0, :], float(KEYS), None, ALU.mult))
                        col = 0
                        for a, n, w in CAND_RUNS:
                            for dst, src in ((cand, v2), (candi, i2)):
                                if n == 1:
                                    o_ = dst[:, :, col:col + w]
                                    i0 = src[:, :, 0, a:a + 1].broadcast_to([P, 8, w])
                                    i1 = src[:, :, 1, 0:w]
                                else:
                                    o_ = dst[:, :, col:col + n * w].rearrange("p h (n w) -> p h n w", n=n)
                                    i0 = src[:, :, 0, a:a + n].unsqueeze(3).broadcast_to([P, 8, n, w])
                                    i1 = src[:, :, 1, 0:w].unsqueeze(2).broadcast_to([P, 8, n, w])
                                last = TT(o_, i0, i1, ALU.add)
                            col += n * w
                        link(last)
                        for hd in range(EH):
                            last = nc.vector.max(top[:, hd, 0:8], cand[:, hd, :])
                        link(last)
                        for hd in range(EH):
                            last = nc.vector.max_index(posu[:, hd, 0:8], top[:, hd, 0:8], cand[:, hd, :])
                        link(last)
                        for hd in range(EH):
                            last = nc.vector.match_replace(cand[:, hd, :], top[:, hd, 0:8], cand[:, hd, :], -3e38)
                        link(last)
                        for hd in range(EH):
                            last = nc.vector.max(top[:, hd, 8:16], cand[:, hd, :])
                        link(last)
                        for hd in range(EH):
                            last = nc.vector.max_index(posu[:, hd, 8:16], top[:, hd, 8:16], cand[:, hd, :])
                        link(last)
                        TT(texp, top, over(top[:, :, 0], TOPK), ALU.subtract).then_inc(top_ready, 1)
                        link(CP(posf, posu))
                        for h2 in range(0, EH, 2):
                            places = cst[:, C_IOTA:C_IOTA + NCAND].unsqueeze(1).unsqueeze(1).broadcast_to([P, 2, 16, NCAND])
                            link(TT(eq, places, posf[:, h2:h2 + 2, :].unsqueeze(3).broadcast_to([P, 2, 16, NCAND]), ALU.is_equal))
                            link(TT(eq, eq, candi[:, h2:h2 + 2, :].unsqueeze(2).broadcast_to([P, 2, 16, NCAND]), ALU.mult))
                            link(nc.vector.tensor_reduce(idxf[:, h2:h2 + 2, :], eq, AX_X, ALU.add))
                        link(TS(idxu[:, b * RANKS:(b + 1) * RANKS].rearrange("p (h k) -> p h k", h=8), idxf, float(L * NE), None, ALU.add))
                        dve.wait_ge(texp_ready, L * NB + b + 1)
                        link(nc.vector.tensor_reduce(tsum[:, :], texp, AX_X, ALU.add))
                        link(nc.vector.reciprocal(trec[:, :], tsum[:, :]))
                        TT(wts[:, b * RANKS:(b + 1) * RANKS].rearrange("p (h k) -> p h k", h=8), texp, over(trec[:, :], TOPK), ALU.mult).then_inc(idx_ready, 1)
                        continue
                    if kind == "experts":
                        b = step[1]
                        n0 = (L * NB + b) * RANKS
                        r0 = (L * NB + b) * EH
                        dve.wait_ge(idx_ready, L * NB + b + 1)
                        with dve.Fori(0, EH) as r:
                            dve.wait_ge(diag_ready, r * TOPK + (n0 + 1))
                            dve.nop(nofuse=True)
                            CP(wst[:, :], wts[:, bass.ds(r * TOPK + b * RANKS, TOPK)]).then_inc(wts_staged, 1)
                            for i in range(TOPK + 2):
                                if i < TOPK:
                                    s = i % RING
                                    dve.wait_ge(slot_in[s], r * 32 + (n0 // RING + i // RING + 1) * 16)
                                    dve.nop(nofuse=True)
                                    nc.vector.tensor_tensor_reduce(slots[:, s, 0:D], slots[:, s, 0:D], h[:, b, :], 1.0, 0.0, ALU.mult, ALU.add, dots[:, i:i + 1]).then_inc(dot_ready, 1)
                                if i >= 2:
                                    j = i - 2
                                    if j == 0:
                                        dve.wait_ge(wts_staged, r + (r0 + 1))
                                    dve.wait_ge(gelu_ready, r * TOPK + (n0 + j + 1))
                                    dve.wait_ge(row_used, r * TOPK + (n0 + j + RING - 3))
                                    dve.nop(nofuse=True)
                                    TS(diag[:, j % 4, :], ident, gel[:, j:j + 1], wst[:, j:j + 1], ALU.mult, ALU.mult).then_inc(diag_ready, 1)
                        continue
                    if kind in NO_BANK:
                        continue
                    ps = bank(L, step)
                    bk, use = place(L, step)
                    done = bank_drained[bk]
                    if kind == "gdn":
                        _, u, p = step
                        dve.wait_ge(*drained(L, step))
                        tiles = (4 * u + 2 * p, 4 * u + 2 * p + 1)
                        for j in range(CONV):
                            for f in tiles:
                                tap = par[:, Q_CONV + 4 * f + j:Q_CONV + 4 * f + j + 1]
                                src = cin[:, f, j:j + T]
                                last = TS(cT[:, f, :], src, tap, None, ALU.mult) if j == 0 else STT(cT[:, f, :], src, tap, cT[:, f, :], ALU.mult, ALU.add)
                            if j < CONV - 1:
                                link(last)
                        if p:
                            last.then_inc(conv_ready, 1)
                        continue
                    if kind == "small":
                        dve.wait_ge(*filled(L, step))
                        TT(sm[:, step[1], :], ps[:, 0:16], par[:, Q_BIAS:Q_BIAS + 16], ALU.add).then_inc(done, 1)
                    elif kind == "cum":
                        b = step[1]
                        dve.wait_ge(*filled(L, step))
                        TS(cneg[:, b, :], ps[:, 0:12], -1.0, None, ALU.mult)
                        CP(cpos[:, b, :], ps[:, 8:16]).then_inc(done, 1)
                    elif kind == "gbc":
                        b = step[1]
                        dve.wait_ge(*drained(L, ("cum", b)))
                        dve.wait_ge(*filled(L, step))
                        CP(glast[:, b, :].rearrange("p (h c) -> p h c", h=4), ps.rearrange("p (h c t) -> p h c t", h=4, c=2)[:, :, :, CHUNK - 1])
                        for hd in range(GH):
                            cs = slice(hd * P, (hd + 1) * P)
                            last = STT(DT[:, b, cs], ps[:, cs], cneg[:, b, 8 + hd:9 + hd], dmask, ALU.add, ALU.add)
                        last.then_inc(done, 1)
                    elif kind == "tr":
                        _, k3, b = step
                        if k3 < 2:
                            n = L * 4 + b * 2 + k3 + 1
                            cols = slice(4 * k3, 4 * k3 + 4)
                            dve.wait_ge(sq_ready, n)
                            link(nc.vector.tensor_reduce(ssq[:, b, cols], heads(sq), AX_X, ALU.add))
                            TS(ssq[:, b, cols], ssq[:, b, cols], L2_EPS, None, ALU.add).then_inc(ss_ready, 1)
                            if k3 == 0:
                                dve.wait_ge(ecum_ready, L * NB + b + 1)
                                if b:
                                    dve.wait_ge(*filled(L, ("t4", 3, 0)))
                            dve.wait_ge(rs_ready, n)
                            if k3 == 0:
                                link(TS(rs2[:, 0, :], rsq[:, b, cols], GD ** -0.5, None, ALU.mult))
                                link(TT(rs2[:, 1, :], rs2[:, 0, :], ecum[:, b, 0:4], ALU.mult))
                                outs = ((tmp4[:, 0, :], rs2[:, 0, :]), (tmp4[:, 1, :], rs2[:, 1, :]))
                            else:
                                link(TT(rs2[:, 2, :], rsq[:, b, cols], beta[:, b, :], ALU.mult))
                                TT(rs2[:, 3, :], rs2[:, 2, :], ecum[:, b, 0:4], ALU.mult)
                                link(TT(rs2[:, 4, :], rsq[:, b, cols], ecum[:, b, 4:8], ALU.mult))
                                outs = ((tmp4[:, 2, :], rsq[:, b, cols]), (tmp4[:, 3, :], rs2[:, 2, :]), (kbe[:, b, :], rs2[:, 3, :]), (kdec[:, b, :], rs2[:, 4, :]))
                        else:
                            dve.wait_ge(*filled(L, step))
                            outs = ((vb[:, b, :], beta[:, b, :]),)
                        for dst, scale in outs:
                            last = TT(heads(dst), heads(ps), over(scale, GD), ALU.mult)
                        last.then_inc(done, 1)
                    elif kind == "lt":
                        b = step[1]
                        dve.wait_ge(dt_ready, 2 * (L * NB + b + 1))
                        dve.wait_ge(*filled(L, step))
                        TT(lt[:, b, :], ps, DT[:, b, :], ALU.mult).then_inc(done, 1)
                        dve.wait_ge(*drained(L, step))
                        link(TT(heads(Um[:, b, :]), heads(lt[:, b, :]), each(lev(0), GH), ALU.mult))
                        TT(heads(Xm[:, b, :]), heads(lt[:, b, :]), each(lev(1), GH), ALU.mult).then_inc(x1_ready, 1)
                        TT(heads(Um[:, b, :]), heads(Um[:, b, :]), each(ident, GH), ALU.add).then_inc(u_init, 1)
                    elif kind == "at":
                        b = step[1]
                        dve.wait_ge(*filled(L, step))
                        TT(att[:, b, :], ps, DT[:, b, :], ALU.mult).then_inc(done, 1)
                    elif kind in ("ty", "uy"):
                        b = step[1]
                        m = Tm if kind == "ty" else Um
                        dve.wait_ge(*filled(L, step))
                        TT(m[:, b, :], m[:, b, :], ps, ALU.add).then_inc(done, 1)
                    elif kind == "dS":
                        _, b, c = step
                        n = 2 * b + c
                        dve.wait_ge(*filled(L, step))
                        if n == 0:
                            last = CP(Sm[:, 1, :], ps)
                        else:
                            for hd in range(GH):
                                cs = slice(hd * P, (hd + 1) * P)
                                last = STT(Sm[:, (n + 1) % 2, cs], Sm[:, n % 2, cs], egl[:, b, 2 * hd + c:2 * hd + c + 1], ps[:, cs], ALU.mult, ALU.add)
                        last.then_inc(done, 1)
                    elif kind == "fs":
                        _, b, hp = step
                        w = (b + 1) * P
                        dve.wait_ge(*filled(L, step))
                        if hp >= 2:
                            dve.wait_ge(*filled(L, ("pt", b, hp - 2)))
                        elif b:
                            dve.wait_ge(*filled(L, ("pt", 0, hp + 2)))
                        for j in range(2):
                            hd = 2 * hp + j
                            last = STT(fE[:, hp % 2, j, 0:w], ps[:, j * T:j * T + w], cneg[:, b, hd:hd + 1], fmask[:, T - w:T], ALU.add, ALU.add)
                        last.then_inc(done, 1)
                        dve.wait_ge(*drained(L, step))
                        nc.vector.tensor_reduce(fmax[:, b, 2 * hp:2 * hp + 2], fE[:, hp % 2, :, 0:w], AX_X, ALU.max, negate=True).then_inc(fmax_ready, 1)
                    elif kind == "fo":
                        _, b, hp = step
                        dve.wait_ge(fexp_ready, 2 * (L * 8 + b * 4 + hp + 1))
                        link(nc.vector.reciprocal(frs[:, b, 2 * hp:2 * hp + 2], fsum[:, b, 2 * hp:2 * hp + 2]))
                        if b and hp == 0:
                            dve.wait_ge(*filled(L, ("foT", 0)))
                        dve.wait_ge(*filled(L, step))
                        TT(fo[:, hp * P:(hp + 1) * P].rearrange("p (j d) -> p j d", j=2), ps[:, 0:P].rearrange("p (j d) -> p j d", j=2), over(frs[:, b, 2 * hp:2 * hp + 2], FD), ALU.mult).then_inc(done, 1)
                    elif kind == "br":
                        _, n, c, b = step
                        cs = slice(c * 512, (c + 1) * 512)
                        g = gates[:, b, (2 * n + c) * 512:(2 * n + c + 1) * 512]
                        dve.wait_ge(*filled(L, step))
                        dve.wait_ge(*drained(L, ("gate", n, c, b)))
                        if n == 0:
                            TT(merged[:, b, cs], ps, g, ALU.mult).then_inc(done, 1)
                        else:
                            TT(g, ps, g, ALU.mult).then_inc(done, 1)
                            dve.wait_ge(*drained(L, step))
                            last = TT(merged[:, b, cs], merged[:, b, cs], g, ALU.add)
                            if n == 2:
                                last.then_inc(merged_ready, 1)
                            else:
                                link(last)
                    elif kind == "out":
                        _, c, b = step
                        cs = slice(c * 512, (c + 1) * 512)
                        dve.wait_ge(*filled(L, step))
                        STT(rr[:, b, cs], h[:, b, cs], ALPHA, ps, ALU.mult, ALU.add).then_inc(done, 1)
                    elif kind == "pp":
                        _, c, b = step
                        cs = slice(c * 512, (c + 1) * 512)
                        dve.wait_ge(*filled(L, step))
                        dve.wait_ge(*drained(L, ("pg", c, b)))
                        TT(base[:, b, cs], base[:, b, cs], ps, ALU.mult).then_inc(done, 1)
                        dve.wait_ge(*drained(L, step))
                        last = STT(base[:, b, cs], h[:, b, cs], ALPHA, base[:, b, cs], ALU.mult, ALU.add)
                        if c:
                            last.then_inc(base_ready, 1)


def constants():
    c = np.zeros((P, NCONST), np.float32)
    r, t = np.arange(P)[:, None], np.arange(P)[None, :]
    same = r // CHUNK == t // CHUNK
    c[:, C_ID:C_ID + P] = r == t
    c[:, C_TRI:C_TRI + P] = r <= t
    c[:, C_ONES:C_ONES + P] = 1
    c[:, C_BTRI:C_BTRI + P] = (r <= t) & same
    c[:, C_AFTER:C_AFTER + P] = (r > t) & same
    c[:, C_CMASK:C_CMASK + P] = np.where(t <= r, 0, MASKED)
    c[:, C_DMASK:C_DMASK + P] = np.where((t >= r) & same, 0, MASKED)
    for i in range(LEVELS):
        s = 1 << i
        c[:, C_LEV + i * P:C_LEV + (i + 1) * P] = -1.0 * ((r // (2 * s) == t // (2 * s)) & (t // s % 2 == 1) & (r // s % 2 == 0))
    for g, w in enumerate(WINDOWS):
        for kind, (rb, tb) in enumerate(((0, 0), (0, 1), (1, 1))):
            rr, tt = r + rb * P, t + tb * P
            inside = (rr <= tt) & (rr > tt - w)
            c[:, C_BAND + (4 * kind + g) * P:][:, :P] = np.where(inside, 1.0 / np.minimum(tt + 1, w), 0) - (rr == tt)
    c[:, C_IOTA:C_IOTA + 64] = np.arange(64)
    c[:, C_SIGN:C_SIGN + 8] = -1
    c[:, C_SIGN + 8:C_SIGN + 12] = 1
    return c


def k_tiles(w):
    k, n = w.shape
    return w.reshape(k // P, P, n).transpose(1, 0, 2).reshape(P, -1)


def kernel(x, p, w_in, fox_fb, pool_w, pool_scale, gdn_conv, gdn_a_log, gdn_dt_bias, gdn_norm, w_branch, w_out,
           ln1_g, ln1_b, peer_wq, peer_k1, peer_k2, peer_u, peer_v, ple_gate, ple_proj, ln2_g, ln2_b):
    import concourse.bacc as bacc
    from concourse.bass_utils import run_bass_kernel_spmd

    x, p, w_in, fox_fb, pool_w, pool_scale, gdn_conv, gdn_a_log, gdn_dt_bias, gdn_norm, w_branch, w_out, \
        ln1_g, ln1_b, peer_wq, peer_k1, peer_k2, peer_u, peer_v, ple_gate, ple_proj, ln2_g, ln2_b = (
            np.asarray(a) for a in (x, p, w_in, fox_fb, pool_w, pool_scale, gdn_conv, gdn_a_log, gdn_dt_bias, gdn_norm,
                                    w_branch, w_out, ln1_g, ln1_b, peer_wq, peer_k1, peer_k2, peer_u, peer_v, ple_gate,
                                    ple_proj, ln2_g, ln2_b))
    o_f = 3 * BW
    o_pool = o_f + FH
    o_gdn = o_pool + BW
    o_b = o_gdn + 3 * BW
    o_a = o_b + GH
    o_z = o_a + GH
    o_gate = o_z + BW
    starts = [o_pool, o_gdn, o_gdn + BW, o_gdn + 2 * BW, o_z, 0, BW, 2 * BW] + [o_gate + i * BW for i in range(6)]
    units = np.empty((DEPTH * UNITS, P, UCOLS), np.float32)
    params = np.zeros((DEPTH, P, NPARAM), np.float32)
    lnrows = np.empty((DEPTH, 2, P, 2 * D), np.float32)
    for L in range(DEPTH):
        u = units[L * UNITS:(L + 1) * UNITS]
        for i, s in enumerate(starts):
            u[i] = k_tiles(w_in[L][:, s:s + BW])
        for n in range(3):
            u[U_BR + n] = k_tiles(w_branch[L, n])
        for c in range(2):
            u[U_OUT + c] = k_tiles(w_out[L][:, c * BW:(c + 1) * BW])
            u[U_PLEG + c] = k_tiles(ple_gate[L][:, c * BW:(c + 1) * BW])
        for c in range(4):
            u[U_WQ + c] = k_tiles(peer_wq[L][:, c * BW:(c + 1) * BW])
        keys = np.stack([peer_k1[L], peer_k2[L]], 1)
        u[U_KEYS][:, 0:2048] = keys.transpose(3, 0, 1, 2).reshape(P, -1)
        u[U_KEYS][:, 2048:4096] = k_tiles(ple_proj[L])
        q = params[L]
        q[:, Q_CONV:Q_CONV + 48] = gdn_conv[L][:, 0, :].reshape(CONV, 12, P).transpose(2, 1, 0).reshape(P, 48)
        q[:, Q_PSC:Q_PSC + 4] = pool_scale[L].reshape(4, P).T
        q[:, Q_NORM] = gdn_norm[L]
        q[:, Q_BIAS:Q_BIAS + 8] = fox_fb[L]
        q[:, Q_BIAS + 8:Q_BIAS + 12] = gdn_dt_bias[L]
        q[:, Q_ALOG:Q_ALOG + 4] = gdn_a_log[L]
        small = np.concatenate([w_in[L][:, o_f:o_f + FH], w_in[L][:, o_a:o_a + GH], w_in[L][:, o_b:o_b + GH]], 1)
        q[:, Q_WS:Q_WS + KT * 16] = k_tiles(small)
        q[:, Q_PW:Q_PW + 512] = pool_w[L].transpose(1, 0, 2).reshape(P, 512)
        q[:, Q_PT:Q_PT + 2 * T] = k_tiles(p[L, 0].T)
        lnrows[L, 0] = np.concatenate([ln1_g[L], ln1_b[L]])
        lnrows[L, 1] = np.concatenate([ln2_g[L], ln2_b[L]])
    experts = np.concatenate([peer_u.reshape(DEPTH * NE, D), peer_v.reshape(DEPTH * NE, D)], 1)
    arrays = {"x": np.ascontiguousarray(x[0]), "weights": units, "params": params, "lnrows": lnrows,
              "consts": constants(), "experts": experts}

    nc = bacc.Bacc("TRN2", target_bir_lowering=False, num_devices=1)
    args = [nc.dram_tensor(n + "_dram", a.shape, F32, kind="ExternalInput").ap() for n, a in arrays.items()]
    out = nc.dram_tensor("out_dram", (T, D), F32, kind="ExternalOutput").ap()
    build(nc, *args, out)
    r = run_bass_kernel_spmd(nc, [{n + "_dram": a for n, a in arrays.items()}], core_ids=[0])
    return r.results[0]["out_dram"].reshape(1, T, D)
```

```python
from contextlib import ExitStack

import numpy as np

import concourse.bass as bass
from concourse import mybir

F32 = mybir.dt.float32
U32 = mybir.dt.uint32
ALU = mybir.AluOpType
ACT = mybir.ActivationFunctionType
AX_X = mybir.AxisListType.X

P = 128
D = 1024
KT = D // P
T = 256
NB = T // P
DEPTH = 2
PLE = 256
FH, FD = 8, 64
GH, GD = 4, 128
CHUNK = 64
WINDOWS = (2, 4, 8, 16)
CONV = 4
BW = 512
EH, KEYS, TOPK = 8, 128, 16
NE = KEYS * KEYS
ALPHA = (2 * DEPTH) ** 0.25
LN_EPS, RMS_EPS, L2_EPS = 1e-5, 1e-6, 1e-6
MASKED = -1e30
LEVELS = 6

CAND_RUNS = ((0, 1, 16), (1, 1, 8), (2, 1, 5), (3, 1, 4), (4, 1, 3), (5, 3, 2), (8, 8, 1))
NCAND = sum(n * w for _, n, w in CAND_RUNS)

U_POOL, U_GDN, U_Z, U_FQ, U_FK, U_FV, U_GATE, U_BR, U_OUT = 0, 1, 4, 5, 6, 7, 8, 14, 17
U_PLE, U_WQ, U_KEYS, U_PLE1 = 19, 22, 26, 27
UNITS = 29
KINDS = 26
M_PLE, M_WQ = 19, 22
UNIT_KIND = [*range(26), M_PLE + 2, M_PLE, M_PLE + 1]
UCOLS = 4096
WSLOTS = 3

C_ID, C_TRI, C_ONES, C_BTRI, C_AFTER, C_ZERO, C_CMASK, C_DMASK = (i * P for i in range(8))
C_LEV = 8 * P
C_BAND = C_LEV + LEVELS * P
C_IOTA = C_BAND + 3 * 4 * P
C_SIGN = C_IOTA + 64
NCONST = C_SIGN + 16
Q_CONV, Q_PSC, Q_NORM = 0, 48, 52
Q_BIAS, Q_ALOG = 56, 72
Q_WS = 80
Q_PW = Q_WS + KT * 16
Q_PT = Q_PW + 512
NPARAM = Q_PT + 2 * T

RING = 8
RANKS = EH * TOPK
SELECT_LINKS = 20


def steps():
    s = [("hT", b, q) for b in range(2) for q in range(2)]
    s += [("small", 0), ("small", 1), ("pool", 0), ("pool", 1), ("softplus",)]
    s += [("gdn", 0, 0), ("gdn", 0, 1), ("cum", 0), ("cum", 1)]
    s += [("gdn", 1, 0), ("gdn", 1, 1), ("gbc", 0), ("gbc", 1)]
    s += [("gdn", 2, 0), ("gdn", 2, 1), ("pooled", 0), ("pooled", 1), ("z", 0), ("z", 1)]
    s += [("poolmix", 0), ("poolmix", 1)]
    s += [("tr", 0, 0), ("tr", 1, 0), ("tr", 2, 0), ("fq", 0), ("fq", 1)]
    s += [("t4", k, 0) for k in range(4)]
    s += [("tr", 0, 1), ("tr", 1, 1), ("tr", 2, 1), ("fk", 0), ("fk", 1)]
    s += [("t4", k, 1) for k in range(4)]
    s += [("lt", 0), ("at", 0), ("lt", 1), ("at", 1), ("fv", 0), ("fv", 1), ("t0", 0), ("t0", 1)]
    fox = []
    for b in range(2):
        for hp in range(4):
            fox.append(("fs", b, hp))
            if hp:
                fox += [("pt", b, hp - 1), ("fo", b, hp - 1)]
        fox += [("pt", b, 3), ("fo", b, 3), ("foT", b)]
    gates = [("gate", n, c, b) for n in range(3) for c in range(2) for b in range(2)]
    chain = []
    for lev in range(1, LEVELS):
        chain.append([("y", b, lev) for b in range(2)])
        chain.append([(k, b, lev) for b in range(2) for k in (("ty", "uy") if lev < LEVELS - 1 else ("uy",))])
    chain.append([("wT", 0), ("wT", 1)])
    for b in range(2):
        for c in range(2):
            chain.append([("vn", b, c)])
            chain.append([("o", b, c)] + ([("dS", b, c)] if (b, c) != (1, 1) else []))
        chain.append([("onorm", b)])
    fill = [fox[i:i + 3] for i in range(0, len(fox), 3)] + [[g] for g in gates]
    tail = [("oT", 0), ("oT", 1)]
    for i in range(max(len(chain), len(fill))):
        s += chain[i] if i < len(chain) else []
        s += fill[i] if i < len(fill) else []
    s += tail
    s += [("br", n, c, b) for n in range(3) for c in range(2) for b in range(2)]
    s += [("mT", b, q) for b in range(2) for q in range(2)]
    s += [("out", 0, 0), ("out", 1, 0), ("ln1", 0), ("out", 0, 1), ("out", 1, 1), ("h1T", 0, 0), ("h1T", 0, 1)]
    s += [("pg", 0, 0), ("pg", 1, 0), ("ln1", 1), ("pp", 0, 0), ("pp", 1, 0), ("h1T", 1, 0), ("h1T", 1, 1)]
    s += [("wq", u, p) for u in range(4) for p in range(2)]
    s += [("sc", 0, g) for g in range(4)] + [("sc", 1, g) for g in range(4)]
    s += [("select",), ("pg", 0, 1), ("pg", 1, 1), ("pp", 0, 1), ("pp", 1, 1)]
    s += [("experts", 0), ("ln2", 0), ("experts", 1), ("ln2", 1)]
    return s


NO_BANK = {"softplus", "onorm", "ln1", "ln2", "select", "experts"}
STEPS = steps()
FILLS = [s for s in STEPS if s[0] not in NO_BANK]
NBANK = 6


def last_reader(u):
    for first, kind in ((U_GDN, "gdn"), (U_WQ, "wq")):
        if first <= u < first + {"gdn": 3, "wq": 4}[kind]:
            return kind, u - first, 1
    if U_GATE <= u < U_BR:
        return "gate", (u - U_GATE) // 2, (u - U_GATE) % 2, 1
    if U_BR <= u < U_OUT:
        return "br", u - U_BR, 1, 1
    return {U_POOL: ("pool", 1), U_Z: ("z", 1), U_FQ: ("fq", 1), U_FK: ("fk", 1), U_FV: ("fv", 1),
            U_OUT: ("out", 0, 1), U_OUT + 1: ("out", 1, 1), U_PLE: ("pg", 0, 0), U_PLE + 1: ("pg", 1, 0),
            U_PLE + 2: ("pp", 1, 0), U_KEYS: ("pp", 1, 1), U_PLE1: ("pg", 0, 1), U_PLE1 + 1: ("pg", 1, 1)}[u]


def build(nc, x, weights, params, lnrows, consts, experts, out):
    with ExitStack() as ctx:
        def sb(name, cols, dt=F32):
            return ctx.enter_context(nc.sbuf_tensor(name, [P, cols], dt))

        def sem(name):
            return ctx.enter_context(nc.semaphore(name))

        cst = sb("cst", NCONST)
        par = sb("par", NPARAM)
        lnr = sb("lnr", 2 * D)
        h = sb("h", NB * D).rearrange("p (b d) -> p b d", b=NB)
        hT = sb("hT", KT * T).rearrange("p (k t) -> p k t", k=KT)
        wring = sb("wring", WSLOTS * UCOLS).rearrange("p (s n) -> p s n", s=WSLOTS)
        arena = sb("arena", 28196)

        def at(off, n):
            return arena[:, off:off + n]

        brT = at(0, 12 * T).rearrange("p (k t) -> p k t", k=12)
        gates = at(3072, 2 * 3072).rearrange("p (b n) -> p b n", b=2)
        zs = at(9216, 1024).rearrange("p (b n) -> p b n", b=2)
        fq = at(3072, 1024).rearrange("p (k t) -> p k t", k=4)
        fk = at(4096, 1024).rearrange("p (k t) -> p k t", k=4)
        fv = at(5120, 1024).rearrange("p (b n) -> p b n", b=2)
        fE = at(6144, 1024).rearrange("p (i j k) -> p i j k", i=2, j=2)
        fP = at(7168, 1024).rearrange("p (i n) -> p i n", i=2)
        fo = at(8192, 512)
        cin = at(10240, 12 * 259).rearrange("p (k t) -> p k t", k=12)
        cT = at(13348, 12 * 256).rearrange("p (k t) -> p k t", k=12)
        late = [at(10240 + 1024 * i, 1024).rearrange("p (b n) -> p b n", b=2) for i in range(6)]
        lt, att, Um, Tm, Ym, Xm = late
        fT = at(16420, 4096).rearrange("p (b k n) -> p b k n", b=2, k=4)
        kbe = at(20516, 1024).rearrange("p (b n) -> p b n", b=2)
        kdec = at(21540, 1024).rearrange("p (b n) -> p b n", b=2)
        vb = at(22564, 1024).rearrange("p (b n) -> p b n", b=2)
        tmp4 = at(23588, 2048).rearrange("p (k n) -> p k n", k=4)
        poolx = at(23588, 1024).rearrange("p (b n) -> p b n", b=2)
        pooledT = at(24612, 1024).rearrange("p (g t) -> p g t", g=4)
        om = at(23588, 1024).rearrange("p (b n) -> p b n", b=2)
        Sm = at(24612, 1024).rearrange("p (i n) -> p i n", i=2)
        DT = at(25636, 1024).rearrange("p (b n) -> p b n", b=2)
        vnew = at(26660, 1024).rearrange("p (b n) -> p b n", b=2)
        sq = at(27684, 512)
        merged = at(10240, 2048).rearrange("p (b d) -> p b d", b=2)
        mT = at(12288, 2048).rearrange("p (k t) -> p k t", k=8)
        rr = at(14336, 2048).rearrange("p (b d) -> p b d", b=2)
        slots = at(0, RING * 2 * D).rearrange("p (s n) -> p s n", s=RING)
        qpT = at(12288, 4096).rearrange("p (k t) -> p k t", k=16)
        scs_flat = at(16384, 4096)
        scs = scs_flat.rearrange("p (b l n) -> p b l n", b=2, l=16)
        base = at(20480, 2048).rearrange("p (b d) -> p b d", b=2)
        sl = at(22528, 256).rearrange("p (s n) -> p s n", s=2)
        tv = at(22784, 32).rearrange("p (s k) -> p s k", s=2)
        tif = at(22816, 32).rearrange("p (s k) -> p s k", s=2)
        cand, candi = at(22848, NCAND), at(22912, NCAND)
        top, posf, idxf, texp = (at(22976 + 16 * i, 16) for i in range(4))
        eq = at(23040, TOPK * NCAND).rearrange("p (k c) -> p k c", k=TOPK)
        diag = at(25952, 512).rearrange("p (i n) -> p i n", i=4)
        tiu = sb("tiu", 32, U32)[:, :].rearrange("p (s k) -> p s k", s=2)
        posu = sb("posu", TOPK, U32)
        idxu = sb("idxu", NB * RANKS, U32)
        stage = sb("stage", 16, U32)
        wts = sb("wts", NB * RANKS)
        wst, dots, gel = sb("wst", 16), sb("dots", 16), sb("gel", 16)
        tsum, trec = sb("tsum", 1), sb("trec", 1)
        sm = sb("sm", 32)[:, :].rearrange("p (b n) -> p b n", b=2)
        spy, spe, spu, spl, spz, spd = (sb(f"sp{i}", 24)[:, :].rearrange("p (b n) -> p b n", b=2) for i in range(6))
        logs = sb("logs", 24)[:, :].rearrange("p (b n) -> p b n", b=2)
        spb, beta = sb("spb", 8)[:, :].rearrange("p (b n) -> p b n", b=2), sb("beta", 8)[:, :].rearrange("p (b n) -> p b n", b=2)
        aexp = sb("aexp", 4)
        cneg = sb("cneg", 24)[:, :].rearrange("p (b n) -> p b n", b=2)
        cpos, ecum = (sb(n, 16)[:, :].rearrange("p (b n) -> p b n", b=2) for n in ("cpos", "ecum"))
        glast, egl = (sb(n, 16)[:, :].rearrange("p (b n) -> p b n", b=2) for n in ("glast", "egl"))
        ssq, rsq = (sb(n, 16)[:, :].rearrange("p (b n) -> p b n", b=2) for n in ("ssq", "rsq"))
        rs2 = sb("rs2", 24)[:, :].rearrange("p (i n) -> p i n", i=6)
        fmax, fsum, frs = (sb(n, 16)[:, :].rearrange("p (b n) -> p b n", b=2) for n in ("fmax", "fsum", "frs"))
        oss, ors = (sb(n, 8)[:, :].rearrange("p (b n) -> p b n", b=2) for n in ("oss", "ors"))
        bst, mv, rstd = sb("bst", 12), sb("mv", 2), sb("rstd", 1)

        psum = ctx.enter_context(nc.psum_tensor("psum", [P, NBANK, 512], F32))
        acc = ctx.enter_context(nc.psum_tensor("acc", [P, D], F32))

        ident = cst[:, C_ID:C_ID + P]
        tri = cst[:, C_TRI:C_TRI + P]
        tri_ones = cst[:, C_TRI:C_TRI + 2 * P]
        ones = cst[:, C_ONES:C_ONES + P]
        btri = cst[:, C_BTRI:C_BTRI + P]
        after = cst[:, C_AFTER:C_AFTER + P]
        zero = cst[:, C_ZERO:C_ZERO + P]
        fmask = cst[:, C_ZERO:C_ZERO + 2 * P]
        dmask = cst[:, C_DMASK:C_DMASK + P]

        def lev(i):
            return cst[:, C_LEV + i * P:C_LEV + (i + 1) * P]

        def band(kind, g):
            return cst[:, C_BAND + (4 * kind + g) * P:][:, 0:P]

        def heads(ap, n=GH):
            return ap.rearrange("p (h d) -> p h d", h=n)

        def over(ap, n):
            return ap.unsqueeze(2).broadcast_to([ap.shape[0], ap.shape[1], n])

        def each(ap, n):
            return ap.unsqueeze(1).broadcast_to([ap.shape[0], n, ap.shape[1]])

        consts_in, x_in, out_sent = sem("consts_in"), sem("x_in"), sem("out_sent")
        params_in, ln_in = sem("params_in"), sem("ln_in")
        unit_in = [sem(f"unit_in{i}") for i in range(WSLOTS)]
        bank_filled = [sem(f"bank_filled{i}") for i in range(NBANK)]
        bank_drained = [sem(f"bank_drained{i}") for i in range(NBANK)]
        dve_step, act_step, pe_step = sem("dve_step"), sem("act_step"), sem("pe_step")
        sp_neg, sp_exp, sp_one, sp_ln, logs_ready = (sem(n) for n in ("sp_neg", "sp_exp", "sp_one", "sp_ln", "logs_ready"))
        ecum_ready, dt_ready, conv_ready, silu_ready = (sem(n) for n in ("ecum_ready", "dt_ready", "conv_ready", "silu_ready"))
        sq_ready, ss_ready, rs_ready = (sem(n) for n in ("sq_ready", "ss_ready", "rs_ready"))
        u_init, x1_ready, x_ready = (sem(n) for n in ("u_init", "x1_ready", "x_ready"))
        fmax_ready, fexp_ready = sem("fmax_ready"), sem("fexp_ready")
        oss_ready, ors_ready, on_ready = (sem(n) for n in ("oss_ready", "ors_ready", "on_ready"))
        merged_ready, var_ready, rstd_ready = (sem(n) for n in ("merged_ready", "var_ready", "rstd_ready"))
        h1_ready, h2_ready = sem("h1_ready"), sem("h2_ready")
        top_ready, texp_ready, idx_ready = (sem(n) for n in ("top_ready", "texp_ready", "idx_ready"))
        slot_in = [sem(f"slot_in{i}") for i in range(RING)]
        idx_staged, wts_staged = sem("idx_staged"), sem("wts_staged")
        dot_ready, gelu_ready, diag_ready, row_used = (sem(n) for n in ("dot_ready", "gelu_ready", "diag_ready", "row_used"))
        acc_filled, acc_drained, base_ready = sem("acc_filled"), sem("acc_drained"), sem("base_ready")

        def place(L, step):
            n = L * len(FILLS) + FILLS.index(step)
            return n % NBANK, n // NBANK

        def bank(L, step):
            return psum[:, place(L, step)[0], :]

        def filled(L, step):
            b, use = place(L, step)
            return bank_filled[b], use + 1

        def drained(L, step):
            b, use = place(L, step)
            return bank_drained[b], use + 1

        def wt(L, u):
            return wring[:, (L * UNITS + u) % WSLOTS, :]

        block = ctx.enter_context(nc.Block())

        @block.sync
        def _(sp):
            for b in range(NB):
                sp.dma_start(h[:, b, :], x[b * P:(b + 1) * P, :]).then_inc(x_in, 16)
            sp.dma_start(cst[:, :], consts[:, :]).then_inc(consts_in, 16)
            for n in range(DEPTH * UNITS):
                if n >= WSLOTS:
                    sp.wait_ge(*filled((n - WSLOTS) // UNITS, last_reader((n - WSLOTS) % UNITS)))
                sp.dma_start(wring[:, n % WSLOTS, :], weights[n // UNITS * KINDS + UNIT_KIND[n % UNITS]]).then_inc(unit_in[n % WSLOTS], 16)
            for b in range(NB):
                sp.wait_ge(h2_ready, (DEPTH - 1) * NB + b + 1)
                sp.dma_start(out[b * P:(b + 1) * P, :], h[:, b, :]).then_inc(out_sent, 16)
            sp.wait_ge(out_sent, 16 * NB)

        @block.gpsimd
        def _(pool):
            pool.dma_start(par[:, :], params[0]).then_inc(params_in, 16)
            pool.dma_start(lnr[:, :], lnrows[0, 0]).then_inc(ln_in, 16)
            pool.sem_inc(row_used, RING)
            pool.wait_ge(consts_in, 16)
            for L in range(DEPTH):
                for step in STEPS:
                    kind = step[0]
                    if kind == "y" and step[2] < LEVELS - 1:
                        _, b, l = step
                        pool.wait_ge(*filled(L, step))
                        nc.gpsimd.tensor_tensor(heads(Xm[:, b, :]), heads(lt[:, b, :]), each(lev(l + 1), GH), ALU.mult).then_inc(x_ready, 1)
                    if kind == "select":
                        pool.wait_ge(h1_ready, NB * (L + 1))
                        pool.dma_start(lnr[:, :], lnrows[L, 1]).then_inc(ln_in, 16)
                    if kind == "experts":
                        b = step[1]
                        n0 = (L * NB + b) * RANKS
                        pool.wait_ge(*filled(L, ("sc", 1, 3)))
                        with pool.Fori(0, EH) as r:
                            for i in range(TOPK):
                                pool.wait_ge(row_used, r * TOPK + (n0 + i + 1))
                                pool.nop(nofuse=True)
                                if i == 0:
                                    pool.wait_ge(idx_ready, r + ((L * NB + b) * EH + 1))
                                    pool.nop(nofuse=True)
                                if i % RING == 0:
                                    nc.gpsimd.tensor_copy(stage[:, i:i + RING], idxu[:, bass.ds(r * TOPK + (b * RANKS + i), RING)]).then_inc(idx_staged, 1)
                                    pool.wait_ge(idx_staged, r * 2 + ((L * NB + b) * 2 * EH + i // RING + 1))
                                    pool.nop(nofuse=True)
                                nc.gpsimd.indirect_dma_start(
                                    slots[:, i % RING, :], None, experts[:, :],
                                    bass.IndirectOffsetOnAxis(stage[:, i:i + 1], 0)).then_inc(slot_in[i % RING], 16)
                        if b == 0 and L + 1 < DEPTH:
                            pool.wait_ge(*filled(L, ("pp", 1, 1)))
                            pool.dma_start(par[:, :], params[L + 1]).then_inc(params_in, 16)
                    if kind == "ln2" and step[1] == 1 and L + 1 < DEPTH:
                        pool.wait_ge(h2_ready, NB * (L + 1))
                        pool.dma_start(lnr[:, :], lnrows[L + 1, 0]).then_inc(ln_in, 16)

        @block.tensor
        def _(pe):
            mm, tp = nc.tensor.matmul, nc.tensor.transpose
            links = [0]
            pe.wait_ge(consts_in, 16)

            def unit(L, u):
                n = L * UNITS + u
                pe.wait_ge(unit_in[n % WSLOTS], 16 * (n // WSLOTS + 1))
                return wt(L, u)

            def token_major(ps, w, src, b, kt, c0, width, step):
                for k in range(kt):
                    last = mm(ps[:, 0:width], src[:, k, b * P:(b + 1) * P], w[:, k * step + c0:k * step + c0 + width], start=k == 0, stop=k == kt - 1)
                return last

            def feature_major(ps, w, p):
                for i in range(2):
                    for k in range(KT):
                        last = mm(ps[:, i * T:(i + 1) * T], w[:, k * 512 + (2 * p + i) * P:][:, 0:P], hT[:, k, :], start=k == 0, stop=k == KT - 1)
                return last

            for L in range(DEPTH):
                for step in FILLS + [("experts", 0), ("experts", 1)]:
                    kind = step[0]
                    if kind == "experts":
                        b = step[1]
                        n0 = (L * NB + b) * RANKS
                        if L or b:
                            pe.wait_ge(acc_drained, L * NB + b)
                        for c in range(2):
                            mm(acc[:, c * 512:(c + 1) * 512], zero, cst[:, 0:512], start=True, stop=False)
                        with pe.Fori(0, EH) as r:
                            for i in range(TOPK):
                                pe.wait_ge(diag_ready, r * TOPK + (n0 + i + 2))
                                pe.nop(nofuse=True)
                                for c in range(2):
                                    last = mm(acc[:, c * 512:(c + 1) * 512], diag[:, i % 4, :], slots[:, i % RING, D + c * 512:D + (c + 1) * 512], start=False, stop=False)
                                last.then_inc(row_used, 1)
                        for c in range(2):
                            last = mm(acc[:, c * 512:(c + 1) * 512], zero, cst[:, 0:512], start=False, stop=True)
                        last.then_inc(acc_filled, 1)
                        continue
                    bk, use = place(L, step)
                    ps = psum[:, bk, :]
                    if use:
                        pe.wait_ge(bank_drained[bk], use)
                    if kind in ("hT", "h1T"):
                        _, b, q = step
                        if kind == "h1T":
                            pe.wait_ge(h1_ready, L * NB + b + 1)
                        elif L:
                            pe.wait_ge(h2_ready, (L - 1) * NB + b + 1)
                        else:
                            pe.wait_ge(x_in, 16 * NB)
                        for j in range(4):
                            last = tp(ps[:, j * P:(j + 1) * P], h[:, b, (4 * q + j) * P:(4 * q + j + 1) * P], ident)
                    elif kind == "small":
                        b = step[1]
                        pe.wait_ge(params_in, 16 * (L + 1))
                        pe.wait_ge(*drained(L, ("hT", b, 1)))
                        last = token_major(ps, par[:, Q_WS:], hT, b, KT, 0, 16, 16)
                    elif kind in ("pool", "z", "fv"):
                        b = step[1]
                        u = {"pool": U_POOL, "z": U_Z, "fv": U_FV}[kind]
                        last = token_major(ps, unit(L, u), hT, b, KT, 0, 512, 512)
                    elif kind in ("gdn", "fq", "fk", "wq"):
                        p = step[-1]
                        u = {"gdn": U_GDN, "fq": U_FQ, "fk": U_FK, "wq": U_WQ}[kind] + (step[1] if len(step) == 3 else 0)
                        if kind == "wq" and u == U_WQ:
                            pe.wait_ge(*drained(L, ("h1T", 1, 1)))
                        last = feature_major(ps, unit(L, u), p)
                    elif kind == "cum":
                        b = step[1]
                        pe.wait_ge(logs_ready, L + 1)
                        if b:
                            mm(ps[:, 0:8], ones, logs[:, 0, 0:8], start=True, stop=False)
                        mm(ps[:, 0:8], tri, logs[:, b, 0:8], start=not b, stop=True)
                        mm(ps[:, 8:12], btri, logs[:, b, 8:12], start=True, stop=True)
                        last = mm(ps[:, 12:16], after, logs[:, b, 8:12], start=True, stop=True)
                    elif kind == "gbc":
                        b = step[1]
                        for hd in range(GH):
                            last = mm(ps[:, hd * P:(hd + 1) * P], logs[:, b, 8 + hd:9 + hd].broadcast_to([P, P]), btri, start=True, stop=True)
                    elif kind == "pooled":
                        pe.wait_ge(*drained(L, ("pool", 1)))
                        for i in range(2):
                            g = 2 * step[1] + i
                            cs = slice(g * P, (g + 1) * P)
                            mm(ps[:, i * T:i * T + P], poolx[:, 0, cs], band(0, g), start=True, stop=True)
                            mm(ps[:, i * T + P:(i + 1) * T], poolx[:, 0, cs], band(1, g), start=True, stop=False)
                            last = mm(ps[:, i * T + P:(i + 1) * T], poolx[:, 1, cs], band(2, g), start=False, stop=True)
                    elif kind == "poolmix":
                        pe.wait_ge(*drained(L, ("pooled", step[1])))
                        for i in range(2):
                            g = 2 * step[1] + i
                            last = mm(ps[:, i * T:(i + 1) * T], par[:, Q_PW + g * P:Q_PW + (g + 1) * P], pooledT[:, g, :], start=True, stop=True)
                    elif kind == "tr":
                        _, k3, b = step
                        pe.wait_ge(silu_ready, 3 * L + k3 + 1)
                        for hd in range(GH):
                            last = tp(ps[:, hd * P:(hd + 1) * P], cT[:, 4 * k3 + hd, b * P:(b + 1) * P], ident)
                    elif kind == "t4":
                        _, k4, b = step
                        pe.wait_ge(*drained(L, ("tr", k4 // 2, b)))
                        for hd in range(GH):
                            last = tp(ps[:, hd * P:(hd + 1) * P], tmp4[:, k4, hd * P:(hd + 1) * P], ident)
                    elif kind in ("lt", "at"):
                        b = step[1]
                        moving = 3 if kind == "lt" else 0
                        pe.wait_ge(*drained(L, ("t4", 2, b)))
                        pe.wait_ge(*drained(L, ("t4", moving, b)))
                        for hd in range(GH):
                            cs = slice(hd * P, (hd + 1) * P)
                            last = mm(ps[:, cs], fT[:, b, 2, cs], fT[:, b, moving, cs], start=True, stop=True)
                    elif kind == "t0":
                        b = step[1]
                        pe.wait_ge(u_init, L * NB + b + 1)
                        for hd in range(GH):
                            last = tp(ps[:, hd * P:(hd + 1) * P], Um[:, b, hd * P:(hd + 1) * P], ident)
                    elif kind == "y":
                        _, b, l = step
                        if l == 1:
                            pe.wait_ge(x1_ready, L * NB + b + 1)
                            pe.wait_ge(*drained(L, ("t0", b)))
                        else:
                            pe.wait_ge(x_ready, L * NB * (LEVELS - 2) + (l - 2) * NB + b + 1)
                            pe.wait_ge(*drained(L, ("ty", b, l - 1)))
                        for hd in range(GH):
                            cs = slice(hd * P, (hd + 1) * P)
                            last = mm(ps[:, cs], Xm[:, b, cs], Tm[:, b, cs], start=True, stop=True)
                    elif kind in ("ty", "uy"):
                        _, b, l = step
                        pe.wait_ge(*drained(L, ("y", b, l)))
                        if l == 1:
                            pe.wait_ge(u_init, L * NB + b + 1)
                        else:
                            pe.wait_ge(*drained(L, ("uy", b, l - 1)))
                        for hd in range(GH):
                            cs = slice(hd * P, (hd + 1) * P)
                            if kind == "ty":
                                last = mm(ps[:, cs], Um[:, b, cs], Ym[:, b, cs], start=True, stop=True)
                            else:
                                last = mm(ps[:, cs], Ym[:, b, cs], Um[:, b, cs], start=True, stop=True)
                    elif kind == "wT":
                        b = step[1]
                        pe.wait_ge(*drained(L, ("uy", b, LEVELS - 1)))
                        for hd in range(GH):
                            cs = slice(hd * P, (hd + 1) * P)
                            last = mm(ps[:, cs], kbe[:, b, cs], Um[:, b, cs], start=True, stop=True)
                    elif kind in ("vn", "o"):
                        _, b, c = step
                        n = 2 * b + c
                        rows = slice(c * CHUNK, (c + 1) * CHUNK)
                        if kind == "vn":
                            pe.wait_ge(*drained(L, ("wT", b)))
                            if n:
                                pe.wait_ge(*drained(L, ("dS", (n - 1) // 2, (n - 1) % 2)))
                        else:
                            pe.wait_ge(*drained(L, ("vn", b, c)))
                        for hd in range(GH):
                            cs = slice(hd * P, (hd + 1) * P)
                            t0 = hd * P + c * CHUNK
                            left = Tm[:, b, t0:t0 + CHUNK] if kind == "vn" else fT[:, b, 1, t0:t0 + CHUNK]
                            if n:
                                mm(ps[rows, cs], left, Sm[:, n % 2, cs], start=True, stop=False)
                            if kind == "vn":
                                last = mm(ps[rows, cs], Um[:, b, t0:t0 + CHUNK], vb[:, b, cs], start=not n, stop=True)
                            else:
                                last = mm(ps[rows, cs], att[rows, b, t0:t0 + CHUNK], vnew[rows, b, cs], start=not n, stop=True)
                    elif kind == "dS":
                        _, b, c = step
                        rows = slice(c * CHUNK, (c + 1) * CHUNK)
                        for hd in range(GH):
                            cs = slice(hd * P, (hd + 1) * P)
                            last = mm(ps[:, cs], kdec[rows, b, cs], vnew[rows, b, cs], start=True, stop=True)
                    elif kind == "oT":
                        b = step[1]
                        pe.wait_ge(on_ready, L * NB + b + 1)
                        for hd in range(GH):
                            last = tp(ps[:, hd * P:(hd + 1) * P], om[:, b, hd * P:(hd + 1) * P], ident)
                    elif kind == "fs":
                        _, b, hp = step
                        if hp == 0:
                            pe.wait_ge(*drained(L, ("fq", 1)))
                            pe.wait_ge(*drained(L, ("fk", 1)))
                        width = (b + 1) * P
                        for j in range(2):
                            hd = 2 * hp + j
                            rows = slice(j * FD, (j + 1) * FD)
                            if j:
                                links[0] += 1
                                last.then_inc(pe_step, 1)
                                pe.wait_ge(pe_step, links[0])
                            mm(ps[:, j * T:j * T + width], fq[rows, hp, b * P:(b + 1) * P], fk[rows, hp, 0:width], start=True, stop=False)
                            last = mm(ps[:, j * T:j * T + width], logs[:, 0, hd:hd + 1].broadcast_to([P, P]), tri_ones[:, 0:width], start=False, stop=b == 0)
                            if b:
                                last = mm(ps[:, j * T + P:(j + 1) * T], logs[:, 1, hd:hd + 1].broadcast_to([P, P]), tri, start=False, stop=True)
                    elif kind == "pt":
                        _, b, hp = step
                        pe.wait_ge(fexp_ready, 2 * (L * 8 + b * 4 + hp + 1))
                        for j in range(2):
                            for kb in range(b + 1):
                                col = (j * (b + 1) + kb) * P
                                last = tp(ps[:, col:col + P], fE[:, hp % 2, j, kb * P:(kb + 1) * P], ident)
                    elif kind == "fo":
                        _, b, hp = step
                        pe.wait_ge(*drained(L, ("pt", b, hp)))
                        pe.wait_ge(*drained(L, ("fv", 1)))
                        for j in range(2):
                            hd = 2 * hp + j
                            for kb in range(b + 1):
                                col = (j * (b + 1) + kb) * P
                                last = mm(ps[:, j * FD:(j + 1) * FD], fP[:, hp % 2, col:col + P], fv[:, kb, hd * FD:(hd + 1) * FD], start=kb == 0, stop=kb == b)
                    elif kind == "foT":
                        b = step[1]
                        pe.wait_ge(*drained(L, ("fo", b, 3)))
                        for j in range(4):
                            last = tp(ps[:, j * P:(j + 1) * P], fo[:, j * P:(j + 1) * P], ident)
                    elif kind == "gate":
                        _, n, c, b = step
                        last = token_major(ps, unit(L, U_GATE + 2 * n + c), hT, b, KT, 0, 512, 512)
                    elif kind == "br":
                        _, n, c, b = step
                        if n == 0 and c == 0:
                            pe.wait_ge(*drained(L, ("foT", b)))
                        if n == 1:
                            pe.wait_ge(*drained(L, ("poolmix", 1)))
                        if n == 2:
                            pe.wait_ge(*drained(L, ("oT", b)))
                        last = token_major(ps, unit(L, U_BR + n), brT[:, 4 * n:4 * n + 4, :], b, 4, c * 512, 512, D)
                    elif kind == "mT":
                        _, b, q = step
                        pe.wait_ge(merged_ready, L * 4 + 2 + b + 1)
                        for j in range(4):
                            last = tp(ps[:, j * P:(j + 1) * P], merged[:, b, (4 * q + j) * P:(4 * q + j + 1) * P], ident)
                    elif kind == "out":
                        _, c, b = step
                        pe.wait_ge(*drained(L, ("mT", b, 1)))
                        last = token_major(ps, unit(L, U_OUT + c), mT, b, KT, 0, 512, 512)
                    elif kind == "sc":
                        _, b, g = step
                        pe.wait_ge(*drained(L, ("wq", g, 1)))
                        w = unit(L, U_KEYS)
                        for j in range(4):
                            li = 4 * g + j
                            last = mm(ps[:, j * P:(j + 1) * P], qpT[:, li, b * P:(b + 1) * P], w[:, li * P:(li + 1) * P], start=True, stop=True)
                    elif kind == "pg":
                        _, c, b = step
                        u = (U_PLE1 if b else U_PLE) + c
                        pe.wait_ge(*drained(L, ("h1T", b, 1)))
                        last = token_major(ps, unit(L, u), hT, b, KT, 0, 512, 512)
                    elif kind == "pp":
                        _, c, b = step
                        pT = par[:, Q_PT:Q_PT + 2 * T].rearrange("p (k t) -> p k t", k=2)
                        u = U_KEYS if b else U_PLE + 2
                        last = token_major(ps, unit(L, u)[:, 2048:4096], pT, b, 2, c * 512, 512, D)
                    last.then_inc(bank_filled[bk], 1)

        @block.scalar
        def _(act):
            AC = nc.scalar.activation
            links = [0]

            def link(ins):
                links[0] += 1
                ins.then_inc(act_step, 1)
                act.wait_ge(act_step, links[0])

            def inv_sqrt(dst, src, tmp, ready):
                link(AC(tmp, src, ACT.Ln))
                AC(dst, tmp, ACT.Exp, scale=-0.5).then_inc(ready, 1)

            act.wait_ge(consts_in, 16)
            for L in range(DEPTH):
                for step in STEPS:
                    kind = step[0]
                    if kind == "softplus":
                        act.wait_ge(sp_neg, L + 1)
                        AC(spe, spz, ACT.Exp).then_inc(sp_exp, 1)
                        AC(spb, sm[:, :, 12:16], ACT.Exp, scale=-1.0).then_inc(sp_exp, 1)
                        AC(aexp[:, :], par[:, Q_ALOG:Q_ALOG + 4], ACT.Exp).then_inc(sp_exp, 1)
                        act.wait_ge(sp_one, L + 1)
                        AC(spl, spu, ACT.Ln).then_inc(sp_ln, 1)
                        continue
                    if kind in ("ln1", "ln2"):
                        n = L * 4 + (step[1] if kind == "ln1" else 2 + step[1]) + 1
                        act.wait_ge(var_ready, n)
                        inv_sqrt(rstd[:, :], mv[:, 1:2], mv[:, 1:2], rstd_ready)
                        continue
                    if kind == "onorm":
                        b = step[1]
                        act.wait_ge(oss_ready, L * NB + b + 1)
                        inv_sqrt(ors[:, b, :], oss[:, b, :], oss[:, b, :], ors_ready)
                        continue
                    if kind == "select":
                        act.wait_ge(top_ready, L * 2 * EH + 1)
                        AC(texp, texp, ACT.Exp).then_inc(texp_ready, 1)
                        continue
                    if kind == "experts":
                        n0 = (L * NB + step[1]) * RANKS
                        g0 = (L * NB + step[1]) * EH

                        def head(r, more):
                            for i in range(TOPK):
                                act.wait_ge(dot_ready, r * TOPK + (n0 + i + 1))
                                act.nop(nofuse=True)
                                AC(gel[:, i:i + 1], dots[:, i:i + 1], ACT.Gelu).then_inc(gelu_ready, 1)
                                if i == 12 and more:
                                    act.wait_ge(top_ready, r + (g0 + 2))
                                    act.nop(nofuse=True)
                                    AC(texp, texp, ACT.Exp).then_inc(texp_ready, 1)

                        with act.Fori(0, EH - step[1]) as r:
                            head(r, True)
                        if step[1]:
                            head(EH - 1, False)
                        continue
                    ps = bank(L, step)
                    bk, use = place(L, step)
                    done = bank_drained[bk]
                    if kind in ("small", "lt", "at", "ty", "uy", "dS", "br", "out", "pp"):
                        continue
                    if kind == "cum":
                        b = step[1]
                        act.wait_ge(*drained(L, step))
                        AC(ecum[:, b, :], cpos[:, b, :], ACT.Exp).then_inc(ecum_ready, 1)
                        continue
                    if kind == "gbc":
                        b = step[1]
                        act.wait_ge(*drained(L, step))
                        AC(DT[:, b, :], DT[:, b, :], ACT.Exp).then_inc(dt_ready, 1)
                        AC(egl[:, b, :], glast[:, b, :], ACT.Exp).then_inc(dt_ready, 1)
                        continue
                    if kind == "tr":
                        _, k3, b = step
                        if k3 < 2:
                            n = L * 4 + b * 2 + k3 + 1
                            act.wait_ge(*filled(L, step))
                            if n > 1:
                                act.wait_ge(ss_ready, n - 1)
                            AC(sq, ps, ACT.Square).then_inc(sq_ready, 1)
                            act.wait_ge(ss_ready, n)
                            inv_sqrt(rsq[:, b, 4 * k3:4 * k3 + 4], ssq[:, b, 4 * k3:4 * k3 + 4], ssq[:, b, 4 * k3:4 * k3 + 4], rs_ready)
                        continue
                    if kind == "fs":
                        _, b, hp = step
                        act.wait_ge(fmax_ready, L * 8 + b * 4 + hp + 1)
                        for j in range(2):
                            hd = 2 * hp + j
                            e = fE[:, hp % 2, j, 0:(b + 1) * P]
                            AC(e, e, ACT.Exp, bias=fmax[:, b, hd:hd + 1], accum_out=fsum[:, b, hd:hd + 1]).then_inc(fexp_ready, 1)
                        continue
                    if kind == "fo":
                        continue
                    act.wait_ge(*filled(L, step))
                    if kind in ("hT", "h1T", "mT"):
                        _, b, q = step
                        dst = mT if kind == "mT" else hT
                        last = AC(dst[:, 4 * q:4 * q + 4, b * P:(b + 1) * P], ps.rearrange("p (k t) -> p k t", k=4), ACT.Copy)
                    elif kind == "pool":
                        last = AC(poolx[:, step[1], :], ps, ACT.Copy)
                    elif kind == "gdn":
                        _, u, p = step
                        if u == 0 and p == 0:
                            act.wait_ge(logs_ready, L + 1)
                        last = AC(cin[:, 4 * u + 2 * p:4 * u + 2 * p + 2, 3:3 + T], ps.rearrange("p (k t) -> p k t", k=2), ACT.Copy)
                    elif kind == "pooled":
                        last = AC(pooledT[:, 2 * step[1]:2 * step[1] + 2, :], ps.rearrange("p (k t) -> p k t", k=2), ACT.Copy)
                    elif kind == "poolmix":
                        for i in range(2):
                            g = 2 * step[1] + i
                            last = AC(brT[:, 4 + g, :], ps[:, i * T:(i + 1) * T], ACT.Copy, scale=par[:, Q_PSC + g:Q_PSC + g + 1])
                    elif kind == "z":
                        last = AC(zs[:, step[1], :], ps, ACT.Silu)
                    elif kind == "fq":
                        last = AC(fq[:, 2 * step[1]:2 * step[1] + 2, :], ps.rearrange("p (k t) -> p k t", k=2), ACT.Copy, scale=FD ** -0.5)
                    elif kind == "fk":
                        last = AC(fk[:, 2 * step[1]:2 * step[1] + 2, :], ps.rearrange("p (k t) -> p k t", k=2), ACT.Copy)
                    elif kind == "fv":
                        last = AC(fv[:, step[1], :], ps, ACT.Copy)
                    elif kind == "t4":
                        last = AC(fT[:, step[2], step[1], :], ps, ACT.Copy)
                    elif kind == "t0":
                        last = AC(Tm[:, step[1], :], ps, ACT.Copy)
                    elif kind == "y":
                        last = AC(Ym[:, step[1], :], ps, ACT.Copy)
                    elif kind == "wT":
                        last = AC(Tm[:, step[1], :], ps, ACT.Copy, scale=-1.0)
                    elif kind in ("vn", "o"):
                        _, b, c = step
                        rows = slice(c * CHUNK, (c + 1) * CHUNK)
                        last = AC((vnew if kind == "vn" else om)[rows, b, :], ps[rows, :], ACT.Copy)
                    elif kind == "oT":
                        b = step[1]
                        last = AC(brT[:, 8:12, b * P:(b + 1) * P], ps.rearrange("p (k t) -> p k t", k=4), ACT.Copy, scale=par[:, Q_NORM:Q_NORM + 1])
                    elif kind == "pt":
                        _, b, hp = step
                        w = 2 * (b + 1) * P
                        last = AC(fP[:, hp % 2, 0:w], ps[:, 0:w], ACT.Copy)
                    elif kind == "foT":
                        b = step[1]
                        last = AC(brT[:, 0:4, b * P:(b + 1) * P], ps.rearrange("p (k t) -> p k t", k=4), ACT.Copy)
                    elif kind == "gate":
                        _, n, c, b = step
                        last = AC(gates[:, b, (2 * n + c) * 512:(2 * n + c + 1) * 512], ps, ACT.Sigmoid)
                    elif kind == "wq":
                        _, u, p = step
                        last = AC(qpT[:, 4 * u + 2 * p:4 * u + 2 * p + 2, :], ps.rearrange("p (k t) -> p k t", k=2), ACT.Copy)
                    elif kind == "sc":
                        _, b, g = step
                        last = AC(scs[:, b, 4 * g:4 * g + 4, :], ps.rearrange("p (l n) -> p l n", l=4), ACT.Copy)
                    elif kind == "pg":
                        _, c, b = step
                        last = AC(base[:, b, c * 512:(c + 1) * 512], ps, ACT.Sigmoid)
                    last.then_inc(done, 1)
                    if kind == "gdn" and step[2] == 1:
                        u = step[1]
                        act.wait_ge(conv_ready, 3 * L + u + 1)
                        AC(cT[:, 4 * u:4 * u + 4, :], cT[:, 4 * u:4 * u + 4, :], ACT.Silu).then_inc(silu_ready, 1)

        @block.vector
        def _(dve):
            TT, TS, STT, CP = nc.vector.tensor_tensor, nc.vector.tensor_scalar, nc.vector.scalar_tensor_tensor, nc.vector.tensor_copy
            links = [0]

            def link(ins, r=None):
                links[0] += 1
                ins.then_inc(dve_step, 1)
                dve.wait_ge(dve_step, links[0] if r is None else r * SELECT_LINKS + links[0])
                if r is not None:
                    dve.nop(nofuse=True)

            def select_head(L, g, r=None):
                link(CP(sl, scs_flat[:, bass.ds(g * 2 * KEYS, 2 * KEYS)].rearrange("p (s n) -> p s n", s=2)), r)
                for s in range(2):
                    last = nc.vector.max(tv[:, s, 0:8], sl[:, s, :])
                link(last, r)
                yield
                for s in range(2):
                    last = nc.vector.max_index(tiu[:, s, 0:8], tv[:, s, 0:8], sl[:, s, :])
                link(last, r)
                yield
                for s in range(2):
                    last = nc.vector.match_replace(sl[:, s, :], tv[:, s, 0:8], sl[:, s, :], -3e38)
                link(last, r)
                yield
                for s in range(2):
                    last = nc.vector.max(tv[:, s, 8:16], sl[:, s, :])
                link(last, r)
                yield
                for s in range(2):
                    last = nc.vector.max_index(tiu[:, s, 8:16], tv[:, s, 8:16], sl[:, s, :])
                link(last, r)
                link(CP(tif, tiu), r)
                link(TS(tif[:, 0, :], tif[:, 0, :], float(KEYS), None, ALU.mult), r)
                yield
                col = 0
                for a, n, w in CAND_RUNS:
                    for dst, src in ((cand, tv), (candi, tif)):
                        o_ = dst[:, col:col + n * w].rearrange("p (n w) -> p n w", n=n)
                        last = TT(o_, over(src[:, 0, a:a + n], w), each(src[:, 1, 0:w], n), ALU.add)
                    col += n * w
                link(last, r)
                yield
                link(nc.vector.max(top[:, 0:8], cand), r)
                yield
                link(nc.vector.max_index(posu[:, 0:8], top[:, 0:8], cand), r)
                yield
                link(nc.vector.match_replace(cand, top[:, 0:8], cand, -3e38), r)
                yield
                link(nc.vector.max(top[:, 8:16], cand), r)
                TS(texp, top, top[:, 0:1], None, ALU.subtract).then_inc(top_ready, 1)
                link(nc.vector.max_index(posu[:, 8:16], top[:, 8:16], cand), r)
                yield
                link(CP(posf, posu[:, :]), r)
                link(TT(eq, each(cst[:, C_IOTA:C_IOTA + NCAND], TOPK), over(posf, NCAND), ALU.is_equal), r)
                yield
                link(TT(eq, eq, each(candi, TOPK), ALU.mult), r)
                yield
                link(nc.vector.tensor_reduce(idxf, eq, AX_X, ALU.add), r)
                yield
                TS(idxu[:, bass.ds(g * TOPK, TOPK)], idxf, float(L * NE), None, ALU.add)
                n = L * 2 * EH + g + 1
                dve.wait_ge(texp_ready, n)
                dve.nop(nofuse=True)
                link(nc.vector.tensor_reduce(tsum[:, :], texp, AX_X, ALU.add), r)
                link(nc.vector.reciprocal(trec[:, :], tsum[:, :]), r)
                TS(wts[:, bass.ds(g * TOPK, TOPK)], texp, trec[:, 0:1], None, ALU.mult).then_inc(idx_ready, 1)

            def layer_norm(r, b, n):
                nc.vector.bn_stats(bst[:, 0:6], r[:, 0:512])
                link(nc.vector.bn_stats(bst[:, 6:12], r[:, 512:1024]))
                link(nc.vector.bn_aggr(mv[:, :], bst[:, :]))
                TS(mv[:, 1:2], mv[:, 1:2], LN_EPS, None, ALU.add).then_inc(var_ready, 1)
                dve.wait_ge(rstd_ready, n)
                link(TS(r, r, mv[:, 0:1], rstd[:, 0:1], ALU.subtract, ALU.mult))
                link(TT(r, r, lnr[:, 0:D], ALU.mult))
                return TT(h[:, b, :], r, lnr[:, D:2 * D], ALU.add)

            dve.sem_inc(diag_ready, 1)
            dve.wait_ge(consts_in, 16)
            for L in range(DEPTH):
                for step in STEPS:
                    kind = step[0]
                    if kind == "softplus":
                        dve.wait_ge(*drained(L, ("small", 1)))
                        link(TT(spy, sm[:, :, 0:12], each(cst[:, C_SIGN:C_SIGN + 12], 2), ALU.mult))
                        STT(spz, spy, -1.0, spy, ALU.mult, ALU.min).then_inc(sp_neg, 1)
                        nc.vector.memset(cin[:, :, 0:3], 0.0)
                        dve.wait_ge(sp_exp, 3 * (L + 1))
                        TS(spb, spb, 1.0, None, ALU.add)
                        TS(spu, spe, 1.0, None, ALU.add).then_inc(sp_one, 1)
                        dve.wait_ge(sp_one, L + 1)
                        nc.vector.reciprocal(beta, spb)
                        link(TS(spz, spu, -1.0, 0.0, ALU.add, ALU.is_equal))
                        link(STT(spd, spu, -1.0, spz, ALU.add, ALU.add))
                        link(nc.vector.reciprocal(spd, spd))
                        link(TT(spd, spd, spe, ALU.mult))
                        dve.wait_ge(sp_ln, L + 1)
                        link(TT(spz, spl, spz, ALU.add))
                        link(TT(spd, spd, spz, ALU.mult))
                        link(STT(logs, spy, 0.0, spd, ALU.max, ALU.add))
                        STT(logs[:, :, 8:12], logs[:, :, 8:12], -1.0, each(aexp[:, :], 2), ALU.mult, ALU.mult).then_inc(logs_ready, 1)
                        continue
                    if kind == "onorm":
                        b = step[1]
                        o = heads(om[:, b, :])
                        dve.wait_ge(*drained(L, ("o", b, 1)))
                        link(TT(heads(sq), o, o, ALU.mult))
                        link(nc.vector.tensor_reduce(oss[:, b, :], heads(sq), AX_X, ALU.add))
                        TS(oss[:, b, :], oss[:, b, :], 1.0 / GD, RMS_EPS, ALU.mult, ALU.add).then_inc(oss_ready, 1)
                        dve.wait_ge(ors_ready, L * NB + b + 1)
                        link(TT(o, o, over(ors[:, b, :], GD), ALU.mult))
                        TT(o, o, heads(zs[:, b, :]), ALU.mult).then_inc(on_ready, 1)
                        continue
                    if kind == "ln1":
                        b = step[1]
                        if b == 0:
                            dve.wait_ge(ln_in, 16 * (2 * L + 1))
                        dve.wait_ge(*drained(L, ("out", 1, b)))
                        layer_norm(rr[:, b, :], b, L * 4 + b + 1).then_inc(h1_ready, 1)
                        continue
                    if kind == "ln2":
                        b = step[1]
                        dve.wait_ge(ln_in, 16 * (2 * L + 2))
                        dve.wait_ge(acc_filled, L * NB + b + 1)
                        dve.wait_ge(base_ready, L * NB + b + 1)
                        for c in range(2):
                            cs = slice(c * 512, (c + 1) * 512)
                            last = TT(base[:, b, cs], base[:, b, cs], acc[:, cs], ALU.add)
                        last.then_inc(acc_drained, 1)
                        dve.wait_ge(acc_drained, L * NB + b + 1)
                        layer_norm(base[:, b, :], b, L * 4 + 2 + b + 1).then_inc(h2_ready, 1)
                        continue
                    if kind == "select":
                        dve.wait_ge(*drained(L, ("sc", 1, 3)))
                        n = links[0]
                        for _ in select_head(L, 0):
                            pass
                        assert links[0] - n == SELECT_LINKS
                        continue
                    if kind == "experts":
                        b = step[1]
                        n0 = (L * NB + b) * RANKS
                        g0 = (L * NB + b) * EH

                        def head(r, more, looped):
                            dve.wait_ge(diag_ready, r * TOPK + (n0 + 1))
                            dve.wait_ge(idx_ready, r + (g0 + 1))
                            dve.nop(nofuse=True)
                            CP(wst[:, :], wts[:, bass.ds(r * TOPK + b * RANKS, TOPK)]).then_inc(wts_staged, 1)
                            choose = select_head(L, r + (b * EH + 1), r if looped else None) if more else iter(())
                            for i in range(TOPK + 2):
                                if i < TOPK:
                                    s = i % RING
                                    dve.wait_ge(slot_in[s], r * 32 + (n0 // RING + i // RING + 1) * 16)
                                    dve.nop(nofuse=True)
                                    nc.vector.tensor_tensor_reduce(slots[:, s, 0:D], slots[:, s, 0:D], h[:, b, :], 1.0, 0.0, ALU.mult, ALU.add, dots[:, i:i + 1]).then_inc(dot_ready, 1)
                                    next(choose, None)
                                if i >= 2:
                                    j = i - 2
                                    if j == 0:
                                        dve.wait_ge(wts_staged, r + (g0 + 1))
                                    dve.wait_ge(gelu_ready, r * TOPK + (n0 + j + 1))
                                    dve.wait_ge(row_used, r * TOPK + (n0 + j + RING - 3))
                                    dve.nop(nofuse=True)
                                    TS(diag[:, j % 4, :], ident, gel[:, j:j + 1], wst[:, j:j + 1], ALU.mult, ALU.mult).then_inc(diag_ready, 1)
                            for _ in choose:
                                pass

                        turns = EH - b
                        with dve.Fori(0, turns) as r:
                            head(r, True, True)
                        links[0] += SELECT_LINKS * (turns - 1)
                        if b:
                            head(EH - 1, False, False)
                        continue
                    if kind in NO_BANK:
                        continue
                    ps = bank(L, step)
                    bk, use = place(L, step)
                    done = bank_drained[bk]
                    if kind == "gdn":
                        _, u, p = step
                        dve.wait_ge(*drained(L, step))
                        tiles = (4 * u + 2 * p, 4 * u + 2 * p + 1)
                        for j in range(CONV):
                            for f in tiles:
                                tap = par[:, Q_CONV + 4 * f + j:Q_CONV + 4 * f + j + 1]
                                src = cin[:, f, j:j + T]
                                last = TS(cT[:, f, :], src, tap, None, ALU.mult) if j == 0 else STT(cT[:, f, :], src, tap, cT[:, f, :], ALU.mult, ALU.add)
                            if j < CONV - 1:
                                link(last)
                        if p:
                            last.then_inc(conv_ready, 1)
                        continue
                    if kind == "small":
                        dve.wait_ge(*filled(L, step))
                        TT(sm[:, step[1], :], ps[:, 0:16], par[:, Q_BIAS:Q_BIAS + 16], ALU.add).then_inc(done, 1)
                    elif kind == "cum":
                        b = step[1]
                        dve.wait_ge(*filled(L, step))
                        TS(cneg[:, b, :], ps[:, 0:12], -1.0, None, ALU.mult)
                        CP(cpos[:, b, :], ps[:, 8:16]).then_inc(done, 1)
                    elif kind == "gbc":
                        b = step[1]
                        dve.wait_ge(*drained(L, ("cum", b)))
                        dve.wait_ge(*filled(L, step))
                        CP(glast[:, b, :].rearrange("p (h c) -> p h c", h=4), ps.rearrange("p (h c t) -> p h c t", h=4, c=2)[:, :, :, CHUNK - 1])
                        for hd in range(GH):
                            cs = slice(hd * P, (hd + 1) * P)
                            last = STT(DT[:, b, cs], ps[:, cs], cneg[:, b, 8 + hd:9 + hd], dmask, ALU.add, ALU.add)
                        last.then_inc(done, 1)
                    elif kind == "tr":
                        _, k3, b = step
                        if k3 < 2:
                            n = L * 4 + b * 2 + k3 + 1
                            cols = slice(4 * k3, 4 * k3 + 4)
                            dve.wait_ge(sq_ready, n)
                            link(nc.vector.tensor_reduce(ssq[:, b, cols], heads(sq), AX_X, ALU.add))
                            TS(ssq[:, b, cols], ssq[:, b, cols], L2_EPS, None, ALU.add).then_inc(ss_ready, 1)
                            if k3 == 0:
                                dve.wait_ge(ecum_ready, L * NB + b + 1)
                                if b:
                                    dve.wait_ge(*filled(L, ("t4", 3, 0)))
                            dve.wait_ge(rs_ready, n)
                            if k3 == 0:
                                link(TS(rs2[:, 0, :], rsq[:, b, cols], GD ** -0.5, None, ALU.mult))
                                link(TT(rs2[:, 1, :], rs2[:, 0, :], ecum[:, b, 0:4], ALU.mult))
                                outs = ((tmp4[:, 0, :], rs2[:, 0, :]), (tmp4[:, 1, :], rs2[:, 1, :]))
                            else:
                                link(TT(rs2[:, 2, :], rsq[:, b, cols], beta[:, b, :], ALU.mult))
                                TT(rs2[:, 3, :], rs2[:, 2, :], ecum[:, b, 0:4], ALU.mult)
                                link(TT(rs2[:, 4, :], rsq[:, b, cols], ecum[:, b, 4:8], ALU.mult))
                                outs = ((tmp4[:, 2, :], rsq[:, b, cols]), (tmp4[:, 3, :], rs2[:, 2, :]), (kbe[:, b, :], rs2[:, 3, :]), (kdec[:, b, :], rs2[:, 4, :]))
                        else:
                            dve.wait_ge(*filled(L, step))
                            outs = ((vb[:, b, :], beta[:, b, :]),)
                        for dst, scale in outs:
                            last = TT(heads(dst), heads(ps), over(scale, GD), ALU.mult)
                        last.then_inc(done, 1)
                    elif kind == "lt":
                        b = step[1]
                        dve.wait_ge(dt_ready, 2 * (L * NB + b + 1))
                        dve.wait_ge(*filled(L, step))
                        TT(lt[:, b, :], ps, DT[:, b, :], ALU.mult).then_inc(done, 1)
                        dve.wait_ge(*drained(L, step))
                        link(TT(heads(Um[:, b, :]), heads(lt[:, b, :]), each(lev(0), GH), ALU.mult))
                        TT(heads(Xm[:, b, :]), heads(lt[:, b, :]), each(lev(1), GH), ALU.mult).then_inc(x1_ready, 1)
                        TT(heads(Um[:, b, :]), heads(Um[:, b, :]), each(ident, GH), ALU.add).then_inc(u_init, 1)
                    elif kind == "at":
                        b = step[1]
                        dve.wait_ge(*filled(L, step))
                        TT(att[:, b, :], ps, DT[:, b, :], ALU.mult).then_inc(done, 1)
                    elif kind in ("ty", "uy"):
                        b = step[1]
                        m = Tm if kind == "ty" else Um
                        dve.wait_ge(*filled(L, step))
                        TT(m[:, b, :], m[:, b, :], ps, ALU.add).then_inc(done, 1)
                    elif kind == "dS":
                        _, b, c = step
                        n = 2 * b + c
                        dve.wait_ge(*filled(L, step))
                        if n == 0:
                            last = CP(Sm[:, 1, :], ps)
                        else:
                            for hd in range(GH):
                                cs = slice(hd * P, (hd + 1) * P)
                                last = STT(Sm[:, (n + 1) % 2, cs], Sm[:, n % 2, cs], egl[:, b, 2 * hd + c:2 * hd + c + 1], ps[:, cs], ALU.mult, ALU.add)
                        last.then_inc(done, 1)
                    elif kind == "fs":
                        _, b, hp = step
                        w = (b + 1) * P
                        dve.wait_ge(*filled(L, step))
                        if hp >= 2:
                            dve.wait_ge(*filled(L, ("pt", b, hp - 2)))
                        elif b:
                            dve.wait_ge(*filled(L, ("pt", 0, hp + 2)))
                        for j in range(2):
                            hd = 2 * hp + j
                            last = STT(fE[:, hp % 2, j, 0:w], ps[:, j * T:j * T + w], cneg[:, b, hd:hd + 1], fmask[:, T - w:T], ALU.add, ALU.add)
                        last.then_inc(done, 1)
                        dve.wait_ge(*drained(L, step))
                        nc.vector.tensor_reduce(fmax[:, b, 2 * hp:2 * hp + 2], fE[:, hp % 2, :, 0:w], AX_X, ALU.max, negate=True).then_inc(fmax_ready, 1)
                    elif kind == "fo":
                        _, b, hp = step
                        dve.wait_ge(fexp_ready, 2 * (L * 8 + b * 4 + hp + 1))
                        link(nc.vector.reciprocal(frs[:, b, 2 * hp:2 * hp + 2], fsum[:, b, 2 * hp:2 * hp + 2]))
                        if b and hp == 0:
                            dve.wait_ge(*filled(L, ("foT", 0)))
                        dve.wait_ge(*filled(L, step))
                        TT(fo[:, hp * P:(hp + 1) * P].rearrange("p (j d) -> p j d", j=2), ps[:, 0:P].rearrange("p (j d) -> p j d", j=2), over(frs[:, b, 2 * hp:2 * hp + 2], FD), ALU.mult).then_inc(done, 1)
                    elif kind == "br":
                        _, n, c, b = step
                        cs = slice(c * 512, (c + 1) * 512)
                        g = gates[:, b, (2 * n + c) * 512:(2 * n + c + 1) * 512]
                        dve.wait_ge(*filled(L, step))
                        dve.wait_ge(*drained(L, ("gate", n, c, b)))
                        if n == 0:
                            TT(merged[:, b, cs], ps, g, ALU.mult).then_inc(done, 1)
                        else:
                            TT(g, ps, g, ALU.mult).then_inc(done, 1)
                            dve.wait_ge(*drained(L, step))
                            last = TT(merged[:, b, cs], merged[:, b, cs], g, ALU.add)
                            if n == 2:
                                last.then_inc(merged_ready, 1)
                            else:
                                link(last)
                    elif kind == "out":
                        _, c, b = step
                        cs = slice(c * 512, (c + 1) * 512)
                        dve.wait_ge(*filled(L, step))
                        STT(rr[:, b, cs], h[:, b, cs], ALPHA, ps, ALU.mult, ALU.add).then_inc(done, 1)
                    elif kind == "pp":
                        _, c, b = step
                        cs = slice(c * 512, (c + 1) * 512)
                        dve.wait_ge(*filled(L, step))
                        dve.wait_ge(*drained(L, ("pg", c, b)))
                        TT(base[:, b, cs], base[:, b, cs], ps, ALU.mult).then_inc(done, 1)
                        dve.wait_ge(*drained(L, step))
                        last = STT(base[:, b, cs], h[:, b, cs], ALPHA, base[:, b, cs], ALU.mult, ALU.add)
                        if c:
                            last.then_inc(base_ready, 1)


def constants():
    c = np.zeros((P, NCONST), np.float32)
    r, t = np.arange(P)[:, None], np.arange(P)[None, :]
    same = r // CHUNK == t // CHUNK
    c[:, C_ID:C_ID + P] = r == t
    c[:, C_TRI:C_TRI + P] = r <= t
    c[:, C_ONES:C_ONES + P] = 1
    c[:, C_BTRI:C_BTRI + P] = (r <= t) & same
    c[:, C_AFTER:C_AFTER + P] = (r > t) & same
    c[:, C_CMASK:C_CMASK + P] = np.where(t <= r, 0, MASKED)
    c[:, C_DMASK:C_DMASK + P] = np.where((t >= r) & same, 0, MASKED)
    for i in range(LEVELS):
        s = 1 << i
        c[:, C_LEV + i * P:C_LEV + (i + 1) * P] = -1.0 * ((r // (2 * s) == t // (2 * s)) & (t // s % 2 == 1) & (r // s % 2 == 0))
    for g, w in enumerate(WINDOWS):
        for kind, (rb, tb) in enumerate(((0, 0), (0, 1), (1, 1))):
            rr, tt = r + rb * P, t + tb * P
            inside = (rr <= tt) & (rr > tt - w)
            c[:, C_BAND + (4 * kind + g) * P:][:, :P] = np.where(inside, 1.0 / np.minimum(tt + 1, w), 0) - (rr == tt)
    c[:, C_IOTA:C_IOTA + 64] = np.arange(64)
    c[:, C_SIGN:C_SIGN + 8] = -1
    c[:, C_SIGN + 8:C_SIGN + 12] = 1
    return c


def k_tiles(w):
    k, n = w.shape
    return w.reshape(k // P, P, n).transpose(1, 0, 2).reshape(P, -1)


def kernel(x, p, w_in, fox_fb, pool_w, pool_scale, gdn_conv, gdn_a_log, gdn_dt_bias, gdn_norm, w_branch, w_out,
           ln1_g, ln1_b, peer_wq, peer_k1, peer_k2, peer_u, peer_v, ple_gate, ple_proj, ln2_g, ln2_b):
    import concourse.bacc as bacc
    from concourse.bass_utils import run_bass_kernel_spmd

    x, p, w_in, fox_fb, pool_w, pool_scale, gdn_conv, gdn_a_log, gdn_dt_bias, gdn_norm, w_branch, w_out, \
        ln1_g, ln1_b, peer_wq, peer_k1, peer_k2, peer_u, peer_v, ple_gate, ple_proj, ln2_g, ln2_b = (
            np.asarray(a) for a in (x, p, w_in, fox_fb, pool_w, pool_scale, gdn_conv, gdn_a_log, gdn_dt_bias, gdn_norm,
                                    w_branch, w_out, ln1_g, ln1_b, peer_wq, peer_k1, peer_k2, peer_u, peer_v, ple_gate,
                                    ple_proj, ln2_g, ln2_b))
    o_f = 3 * BW
    o_pool = o_f + FH
    o_gdn = o_pool + BW
    o_b = o_gdn + 3 * BW
    o_a = o_b + GH
    o_z = o_a + GH
    o_gate = o_z + BW
    starts = [o_pool, o_gdn, o_gdn + BW, o_gdn + 2 * BW, o_z, 0, BW, 2 * BW] + [o_gate + i * BW for i in range(6)]
    units = np.empty((DEPTH * KINDS, P, UCOLS), np.float32)
    params = np.zeros((DEPTH, P, NPARAM), np.float32)
    lnrows = np.empty((DEPTH, 2, P, 2 * D), np.float32)
    for L in range(DEPTH):
        u = units[L * KINDS:(L + 1) * KINDS]
        for i, s in enumerate(starts):
            u[i] = k_tiles(w_in[L][:, s:s + BW])
        for n in range(3):
            u[U_BR + n] = k_tiles(w_branch[L, n])
        for c in range(2):
            u[U_OUT + c] = k_tiles(w_out[L][:, c * BW:(c + 1) * BW])
            u[M_PLE + c] = k_tiles(ple_gate[L][:, c * BW:(c + 1) * BW])
        for c in range(4):
            u[M_WQ + c] = k_tiles(peer_wq[L][:, c * BW:(c + 1) * BW])
        keys = np.stack([peer_k1[L], peer_k2[L]], 1)
        u[M_PLE + 2][:, 0:2048] = keys.transpose(3, 0, 1, 2).reshape(P, -1)
        u[M_PLE + 2][:, 2048:4096] = k_tiles(ple_proj[L])
        q = params[L]
        q[:, Q_CONV:Q_CONV + 48] = gdn_conv[L][:, 0, :].reshape(CONV, 12, P).transpose(2, 1, 0).reshape(P, 48)
        q[:, Q_PSC:Q_PSC + 4] = pool_scale[L].reshape(4, P).T
        q[:, Q_NORM] = gdn_norm[L]
        q[:, Q_BIAS:Q_BIAS + 8] = fox_fb[L]
        q[:, Q_BIAS + 8:Q_BIAS + 12] = gdn_dt_bias[L]
        q[:, Q_ALOG:Q_ALOG + 4] = gdn_a_log[L]
        small = np.concatenate([w_in[L][:, o_f:o_f + FH], w_in[L][:, o_a:o_a + GH], w_in[L][:, o_b:o_b + GH]], 1)
        q[:, Q_WS:Q_WS + KT * 16] = k_tiles(small)
        q[:, Q_PW:Q_PW + 512] = pool_w[L].transpose(1, 0, 2).reshape(P, 512)
        q[:, Q_PT:Q_PT + 2 * T] = k_tiles(p[L, 0].T)
        lnrows[L, 0] = np.concatenate([ln1_g[L], ln1_b[L]])
        lnrows[L, 1] = np.concatenate([ln2_g[L], ln2_b[L]])
    experts = np.concatenate([peer_u.reshape(DEPTH * NE, D), peer_v.reshape(DEPTH * NE, D)], 1)
    arrays = {"x": np.ascontiguousarray(x[0]), "weights": units, "params": params, "lnrows": lnrows,
              "consts": constants(), "experts": experts}

    nc = bacc.Bacc("TRN2", target_bir_lowering=False, num_devices=1)
    args = [nc.dram_tensor(n + "_dram", a.shape, F32, kind="ExternalInput").ap() for n, a in arrays.items()]
    out = nc.dram_tensor("out_dram", (T, D), F32, kind="ExternalOutput").ap()
    build(nc, *args, out)
    r = run_bass_kernel_spmd(nc, [{n + "_dram": a for n, a in arrays.items()}], core_ids=[0])
    return r.results[0]["out_dram"].reshape(1, T, D)
```

```python
from contextlib import ExitStack

import numpy as np

import concourse.bass as bass
from concourse import mybir

F32 = mybir.dt.float32
F32R = mybir.dt.float32r
U32 = mybir.dt.uint32
ALU = mybir.AluOpType
ACT = mybir.ActivationFunctionType
AX_X = mybir.AxisListType.X

P = 128
D = 1024
KT = D // P
T = 256
NB = T // P
DEPTH = 2
PLE = 256
FH, FD = 8, 64
GH, GD = 4, 128
CHUNK = 64
WINDOWS = (2, 4, 8, 16)
CONV = 4
BW = 512
EH, KEYS, TOPK = 8, 128, 16
NE = KEYS * KEYS
ALPHA = (2 * DEPTH) ** 0.25
LN_EPS, RMS_EPS, L2_EPS = 1e-5, 1e-6, 1e-6
MASKED = -1e30
LEVELS = 6

CAND_RUNS = ((0, 1, 16), (1, 1, 8), (2, 1, 5), (3, 1, 4), (4, 1, 3), (5, 3, 2), (8, 8, 1))
NCAND = sum(n * w for _, n, w in CAND_RUNS)

PIECE = 1024
RAWS, HIS = 7, 6

C_ID, C_TRI, C_ONES, C_BTRI, C_AFTER, C_ZERO, C_CMASK, C_DMASK = (i * P for i in range(8))
C_LEV = 8 * P
C_BAND = C_LEV + LEVELS * P
C_IOTA = C_BAND + 3 * 4 * P
C_SIGN = C_IOTA + 64
NCONST = C_SIGN + 16
Q_CONV, Q_PSC, Q_NORM = 0, 48, 52
Q_BIAS, Q_ALOG = 56, 72
Q_WS = 80
Q_PW = Q_WS + KT * 16
Q_PT = Q_PW + 512
NPARAM = Q_PT + 2 * T

RING = 8
RANKS = EH * TOPK
SELECT_LINKS = 20


def steps():
    s = [("hT", b, q) for b in range(2) for q in range(2)]
    s += [("smallT",), ("pool", 0), ("pool", 1), ("small", 0), ("small", 1), ("softplus",)]
    s += [("gdn", 0, 0), ("gdn", 0, 1), ("cum", 0), ("cum", 1)]
    s += [("gdn", 1, 0), ("gdn", 1, 1), ("gbc", 0), ("gbc", 1)]
    s += [("gdn", 2, 0), ("gdn", 2, 1), ("pooled", 0), ("pooled", 1), ("z", 0), ("z", 1)]
    s += [("poolmix", 0), ("poolmix", 1)]
    s += [("tr", 0, 0), ("tr", 1, 0), ("tr", 2, 0), ("fq", 0), ("fq", 1)]
    s += [("t4", k, 0) for k in range(4)]
    s += [("tr", 0, 1), ("tr", 1, 1), ("tr", 2, 1), ("fk", 0), ("fk", 1)]
    s += [("t4", k, 1) for k in range(4)]
    s += [("lt", 0), ("at", 0), ("lt", 1), ("at", 1), ("fv", 0), ("fv", 1), ("t0", 0), ("t0", 1)]
    fox = []
    for b in range(2):
        for hp in range(4):
            fox.append(("fs", b, hp))
            if hp:
                fox += [("pt", b, hp - 1), ("fo", b, hp - 1)]
        fox += [("pt", b, 3), ("fo", b, 3), ("foT", b)]
    def gate(n):
        return [[("gate", n, c, b) for b in range(2)] for c in range(2)]

    def br(n):
        return [[("br", n, c, b) for b in range(2)] for c in range(2)]

    chain = []
    for lev in range(1, LEVELS):
        chain.append([("y", b, lev) for b in range(2)])
        chain.append([(k, b, lev) for b in range(2) for k in (("ty", "uy") if lev < LEVELS - 1 else ("uy",))])
    chain.append([("wT", 0), ("wT", 1)])
    for b in range(2):
        for c in range(2):
            chain.append([("vn", b, c)])
            chain.append([("o", b, c)] + ([("dS", b, c)] if (b, c) != (1, 1) else []))
        chain.append([("onorm", b)])
    fill = [fox[i:i + 3] for i in range(0, len(fox), 3)] + gate(0) + gate(1) + br(0) + [[]] + br(1) + gate(2)[:1] + [[]] + gate(2)[1:]
    tail = [("oT", 0), ("oT", 1)]
    for i in range(max(len(chain), len(fill))):
        s += chain[i] if i < len(chain) else []
        s += fill[i] if i < len(fill) else []
    s += tail
    s += sum(br(2), [])
    s += [("mT", b, q) for b in range(2) for q in range(2)]
    s += [("out", 0, 0), ("out", 0, 1), ("out", 1, 0), ("ln1", 0), ("out", 1, 1), ("ln1", 1)]
    s += [("pp", 0, 0), ("pp", 1, 0), ("h1T", 0, 0), ("h1T", 0, 1), ("pp", 0, 1), ("h1T", 1, 0), ("h1T", 1, 1), ("pp", 1, 1)]
    s += [("wq", u, p) for u in range(2) for p in range(2)] + [("sc", b, g) for g in range(2) for b in range(2)]
    s += [("select",), ("wq", 2, 0), ("wq", 2, 1), ("wq", 3, 0), ("texp",), ("wq", 3, 1)]
    s += [("sc", b, g) for g in range(2, 4) for b in range(2)]
    s += [("pg", c, b) for c in range(2) for b in range(2)]
    s += [("experts", 0), ("ln2", 0), ("experts", 1), ("ln2", 1)]
    return s


NO_BANK = {"softplus", "onorm", "ln1", "ln2", "select", "texp", "experts"}
STEPS = steps()
FILLS = [s for s in STEPS if s[0] not in NO_BANK]
NBANK = 6


def group_list():
    g = []
    for kind in ("pool", "gdn0", "gdn1", "gdn2", "z", "fq", "fk", "fv"):
        if kind in ("fq", "fk"):
            g.append(([(kind, 0), (kind, 1)], True, [None, (kind, 0), None, (kind, 1)]))
        elif kind[:3] == "gdn":
            st = [("gdn", int(kind[3]), p) for p in range(2)]
            g.append((st, True, [None, st[0], None, st[1]]))
        else:
            g.append(([(kind, 0), (kind, 1)], True, [None, None, None, (kind, 1)]))
    for kind, n in (("gate", 0), ("gate", 1), ("br", 0), ("br", 1), ("gate", 2), ("br", 2)):
        if kind == "gate":
            g += [([(kind, n, c, 0), (kind, n, c, 1)], True, [None, None, None, (kind, n, c, 1)]) for c in range(2)]
        else:
            g.append(([(kind, n, c, b) for c in range(2) for b in range(2)], True, [None, (kind, n, 0, 1), None, (kind, n, 1, 1)]))
    g += [([("out", c, 0), ("out", c, 1)], True, [None, None, None, ("out", c, 1)]) for c in range(2)]
    g.append(([("pp", c, b) for b in range(2) for c in range(2)], False, [("pp", 0, 1), ("pp", 1, 1)]))
    for half in range(2):
        us = (2 * half, 2 * half + 1)
        g += [([("wq", u, 0), ("wq", u, 1)], True, [None, ("wq", u, 0), None, ("wq", u, 1)]) for u in us]
        g.append(([("sc", b, u) for u in us for b in range(2)], False, [("sc", 1, us[1])]))
    g += [([("pg", c, 0), ("pg", c, 1)], True, [None, None, None, ("pg", c, 1)]) for c in range(2)]
    return g


GROUPS = group_list()
GROUP_OF = {step: i for i, g in enumerate(GROUPS) for step in g[0]}
PIECES = [(i, j) for i, g in enumerate(GROUPS) for j in range(len(g[2]))]
SPLIT_PIECES = [(i, j) for i, j in PIECES if GROUPS[i][1]]
COUNTED = [(i, j) for i, j in PIECES if GROUPS[i][2][j] is None]


def splits():
    order = [i for i, g in enumerate(GROUPS) if g[1]]
    at = {GROUPS[a][0][0]: b for a, b in zip(order, order[1:])}
    at["out", 1, 1] = at.pop(("out", 1, 0))
    return at


SPLIT_AT = splits()
DVE_SPLIT = GROUP_OF["pg", 1, 0]


def build(nc, x, weights, params, lnrows, consts, experts, out):
    with ExitStack() as ctx:
        def sb(name, cols, dt=F32):
            return ctx.enter_context(nc.sbuf_tensor(name, [P, cols], dt))

        def sem(name):
            return ctx.enter_context(nc.semaphore(name))

        cst = sb("cst", NCONST)
        par = sb("par", NPARAM)
        lnr = sb("lnr", 2 * D)
        h = sb("h", NB * D).rearrange("p (b d) -> p b d", b=NB)

        def two_ways(name, cols):
            with nc.sbuf_tensor(name + "_r", [P, cols], F32R) as rounded:
                pass
            return sb(name, cols), rounded

        hidden, hidden_r = two_ways("hidden", 2 * KT * T)
        raw_all, lo_all = two_ways("raw", RAWS * PIECE)
        raw = raw_all.rearrange("p (s n) -> p s n", s=RAWS)
        w_lo = lo_all.rearrange("p (s n) -> p s n", s=RAWS)
        w_hi = sb("w_hi", HIS * PIECE, F32R).rearrange("p (s n) -> p s n", s=HIS)
        hT = hidden_r.rearrange("p (i k t) -> p i k t", i=2, k=KT)
        w_small = sb("w_small", 2 * KT * 16, F32R).rearrange("p (i n) -> p i n", i=2)
        arena, arena_r = two_ways("arena", 25612)

        def at(off, n):
            return arena[:, off:off + n]

        brT = arena_r[:, 21516:21516 + 4096].rearrange("p (s i k t) -> p s i k t", s=2, i=2, k=4)
        zs = at(0, 1024).rearrange("p (b n) -> p b n", b=2)
        gates = at(1024, 4096).rearrange("p (i b n) -> p i b n", i=2, b=2)
        merged = at(5120, 2048).rearrange("p (b d) -> p b d", b=2)
        fq = at(1024, 1024).rearrange("p (k t) -> p k t", k=4)
        fk = at(2048, 1024).rearrange("p (k t) -> p k t", k=4)
        fv = at(3072, 1024).rearrange("p (b n) -> p b n", b=2)
        fE = at(4096, 1024).rearrange("p (i j k) -> p i j k", i=2, j=2)
        fP = at(5120, 1024).rearrange("p (i n) -> p i n", i=2)
        fo = at(6144, 512)
        sq = at(6656, 512)
        cT = at(7168, 12 * 256).rearrange("p (k t) -> p k t", k=12)
        cin = at(10240, 4 * 259).rearrange("p (k t) -> p k t", k=4)
        lt, att, Um = (at(7168 + 1024 * i, 1024).rearrange("p (b n) -> p b n", b=2) for i in range(3))
        vnew = at(10240, 1024).rearrange("p (b n) -> p b n", b=2)
        fT = at(11276, 4096).rearrange("p (b k n) -> p b k n", b=2, k=4)
        Tm, Ym, Xm = fT[:, :, 0, :], fT[:, :, 2, :], fT[:, :, 3, :]
        kbe = at(15372, 1024).rearrange("p (b n) -> p b n", b=2)
        kdec = at(16396, 1024).rearrange("p (b n) -> p b n", b=2)
        vb = at(17420, 1024).rearrange("p (b n) -> p b n", b=2)
        tmp4 = at(18444, 2048).rearrange("p (k n) -> p k n", k=4)
        poolx = at(18444, 1024).rearrange("p (b n) -> p b n", b=2)
        pooledT = at(19468, 1024).rearrange("p (g t) -> p g t", g=4)
        om = at(18444, 1024).rearrange("p (b n) -> p b n", b=2)
        Sm = at(19468, 1024).rearrange("p (i n) -> p i n", i=2)
        DT = at(20492, 1024).rearrange("p (b n) -> p b n", b=2)
        osq = at(20492, 512)
        rr = at(1024, 2048).rearrange("p (b d) -> p b d", b=2)
        slots = [at(2 * D * i, 2 * D) for i in range(4)] + [at(21516 + 2 * D * i, 2 * D) for i in range(2)]
        slots += [hidden[:, 2 * D * i:2 * D * (i + 1)] for i in range(2)]
        qpT = at(4096, 4096).rearrange("p (k t) -> p k t", k=16)
        base = at(8192, 2048).rearrange("p (b d) -> p b d", b=2)
        scs_flat = at(10240, 4096)
        scs = scs_flat.rearrange("p (b l n) -> p b l n", b=2, l=16)
        sl = at(14336, 256).rearrange("p (s n) -> p s n", s=2)
        tv = at(14592, 32).rearrange("p (s k) -> p s k", s=2)
        tif = at(14624, 32).rearrange("p (s k) -> p s k", s=2)
        cand, candi = at(14656, NCAND), at(14720, NCAND)
        top, posf, idxf, texp = (at(14784 + 16 * i, 16) for i in range(4))
        eq = at(14848, TOPK * NCAND).rearrange("p (k c) -> p k c", k=TOPK)
        diag = at(17760, 512).rearrange("p (i n) -> p i n", i=4)
        emb_gate = at(18272, 2048).rearrange("p (b d) -> p b d", b=2)
        tiu = sb("tiu", 32, U32)[:, :].rearrange("p (s k) -> p s k", s=2)
        posu = sb("posu", TOPK, U32)
        idxu = sb("idxu", NB * RANKS, U32)
        stage = sb("stage", 16, U32)
        wts = sb("wts", NB * RANKS)
        wst, dots, gel = sb("wst", 16), sb("dots", 16), sb("gel", 16)
        tsum, trec = sb("tsum", 1), sb("trec", 1)
        smallT = at(6656, T)
        sm = sb("sm", 32)[:, :].rearrange("p (b n) -> p b n", b=2)
        spy, spe, spu, spl, spz, spd = (sb(f"sp{i}", 24)[:, :].rearrange("p (b n) -> p b n", b=2) for i in range(6))
        logs = sb("logs", 24)[:, :].rearrange("p (b n) -> p b n", b=2)
        spb, beta = sb("spb", 8)[:, :].rearrange("p (b n) -> p b n", b=2), sb("beta", 8)[:, :].rearrange("p (b n) -> p b n", b=2)
        aexp = sb("aexp", 4)
        cneg = sb("cneg", 24)[:, :].rearrange("p (b n) -> p b n", b=2)
        cpos, ecum = (sb(n, 16)[:, :].rearrange("p (b n) -> p b n", b=2) for n in ("cpos", "ecum"))
        glast, egl = (sb(n, 16)[:, :].rearrange("p (b n) -> p b n", b=2) for n in ("glast", "egl"))
        ssq, rsq = (sb(n, 16)[:, :].rearrange("p (b n) -> p b n", b=2) for n in ("ssq", "rsq"))
        rs2 = sb("rs2", 24)[:, :].rearrange("p (i n) -> p i n", i=6)
        fmax, fsum, frs = (sb(n, 16)[:, :].rearrange("p (b n) -> p b n", b=2) for n in ("fmax", "fsum", "frs"))
        oss, ors = (sb(n, 8)[:, :].rearrange("p (b n) -> p b n", b=2) for n in ("oss", "ors"))
        bst, mv, rstd = sb("bst", 12), sb("mv", 2), sb("rstd", 1)

        psum = ctx.enter_context(nc.psum_tensor("psum", [P, NBANK, 512], F32))
        acc = ctx.enter_context(nc.psum_tensor("acc", [P, D], F32))

        ident = cst[:, C_ID:C_ID + P]
        tri = cst[:, C_TRI:C_TRI + P]
        tri_ones = cst[:, C_TRI:C_TRI + 2 * P]
        ones = cst[:, C_ONES:C_ONES + P]
        btri = cst[:, C_BTRI:C_BTRI + P]
        after = cst[:, C_AFTER:C_AFTER + P]
        zero = cst[:, C_ZERO:C_ZERO + P]
        fmask = cst[:, C_ZERO:C_ZERO + 2 * P]
        dmask = cst[:, C_DMASK:C_DMASK + P]

        def lev(i):
            return cst[:, C_LEV + i * P:C_LEV + (i + 1) * P]

        def band(kind, g):
            return cst[:, C_BAND + (4 * kind + g) * P:][:, 0:P]

        def heads(ap, n=GH):
            return ap.rearrange("p (h d) -> p h d", h=n)

        def over(ap, n):
            return ap.unsqueeze(2).broadcast_to([ap.shape[0], ap.shape[1], n])

        def each(ap, n):
            return ap.unsqueeze(1).broadcast_to([ap.shape[0], n, ap.shape[1]])

        ident_in, consts_in, out_sent = sem("ident_in"), sem("consts_in"), sem("out_sent")
        x_in = [sem(f"x_in{b}") for b in range(NB)]
        params_in, ln_in = sem("params_in"), sem("ln_in")
        piece_in = [sem(f"piece_in{i}") for i in range(RAWS)]
        piece_used, w_hi_ready = sem("piece_used"), sem("w_hi_ready")
        w_lo_ready, w_lo_dve_ready = sem("w_lo_ready"), sem("w_lo_dve_ready")
        act_hi_ready, small_hi_ready, small_lo_ready = (sem(n) for n in ("act_hi_ready", "small_hi_ready", "small_lo_ready"))
        bank_filled = [sem(f"bank_filled{i}") for i in range(NBANK)]
        bank_drained = [sem(f"bank_drained{i}") for i in range(NBANK)]
        dve_step, act_step, pe_step = sem("dve_step"), sem("act_step"), sem("pe_step")
        sp_neg, sp_exp, sp_one, sp_ln, logs_ready = (sem(n) for n in ("sp_neg", "sp_exp", "sp_one", "sp_ln", "logs_ready"))
        ecum_ready, dt_ready, conv_ready, silu_ready = (sem(n) for n in ("ecum_ready", "dt_ready", "conv_ready", "silu_ready"))
        sq_ready, ss_ready, rs_ready = (sem(n) for n in ("sq_ready", "ss_ready", "rs_ready"))
        u_init, x1_ready, x_ready = (sem(n) for n in ("u_init", "x1_ready", "x_ready"))
        fmax_ready, fexp_ready = sem("fmax_ready"), sem("fexp_ready")
        oss_ready, ors_ready, on_ready = (sem(n) for n in ("oss_ready", "ors_ready", "on_ready"))
        merged_ready, var_ready, rstd_ready = (sem(n) for n in ("merged_ready", "var_ready", "rstd_ready"))
        h1_ready, h2_ready = sem("h1_ready"), sem("h2_ready")
        top_ready, texp_ready, idx_ready = (sem(n) for n in ("top_ready", "texp_ready", "idx_ready"))
        slot_in = [sem(f"slot_in{i}") for i in range(RING)]
        idx_staged, wts_staged = sem("idx_staged"), sem("wts_staged")
        dot_ready, gelu_ready, diag_ready, row_used = (sem(n) for n in ("dot_ready", "gelu_ready", "diag_ready", "row_used"))
        acc_filled, acc_drained, base_ready = sem("acc_filled"), sem("acc_drained"), sem("base_ready")

        def place(L, step):
            n = L * len(FILLS) + FILLS.index(step)
            return n % NBANK, n // NBANK

        def bank(L, step):
            return psum[:, place(L, step)[0], :]

        def filled(L, step):
            b, use = place(L, step)
            return bank_filled[b], use + 1

        def drained(L, step):
            b, use = place(L, step)
            return bank_drained[b], use + 1

        def loaded(L, piece):
            n = L * len(PIECES) + PIECES.index(piece)
            return piece_in[n % RAWS], 16 * (n // RAWS + 1)

        def used(L, piece):
            step = GROUPS[piece[0]][2][piece[1]]
            if step is None:
                return piece_used, L * len(COUNTED) + COUNTED.index(piece) + 1
            return filled(L, step)

        def raw_slot(L, piece):
            return (L * len(PIECES) + PIECES.index(piece)) % RAWS

        def split_number(L, piece):
            return L * len(SPLIT_PIECES) + SPLIT_PIECES.index(piece)

        def lo_ready(L, piece):
            by_dve = [p for p in SPLIT_PIECES if p[0] == DVE_SPLIT]
            by_pool = [p for p in SPLIT_PIECES if p[0] != DVE_SPLIT]
            if piece in by_dve:
                return w_lo_dve_ready, L * len(by_dve) + by_dve.index(piece) + 1
            return w_lo_ready, L * len(by_pool) + by_pool.index(piece) + 1

        def split_at(L, step):
            if step not in SPLIT_AT:
                return []
            g = SPLIT_AT[step]
            return [(L, (g, j)) for j in range(len(GROUPS[g][2]))]

        def first_group(L):
            return [(L, (0, j)) for j in range(len(GROUPS[0][2]))] if L < DEPTH else []

        HI_STEPS = [st for st in FILLS if st[0] in ("hT", "h1T", "mT", "poolmix", "foT", "oT")]

        def hi_count(L, step):
            return L * len(HI_STEPS) + HI_STEPS.index(step) + 1

        def split_target(step):
            kind = step[0]
            if kind in ("hT", "h1T", "mT"):
                _, b, q = step
                return [hT[:, i, 4 * q:4 * q + 4, b * P:(b + 1) * P] for i in range(2)]
            if kind == "poolmix":
                return [brT[:, 0, i, 2 * step[1]:2 * step[1] + 2, :] for i in range(2)]
            b = step[1]
            return [brT[:, 1 if kind == "foT" else 0, i, :, b * P:(b + 1) * P] for i in range(2)]

        block = ctx.enter_context(nc.Block())

        @block.sync
        def _(sp):
            sp.dma_start(cst[:, C_ID:C_ID + P], consts[:, C_ID:C_ID + P]).then_inc(ident_in, 16)
            for b in range(NB):
                sp.dma_start(h[:, b, :], x[b * P:(b + 1) * P, :]).then_inc(x_in[b], 16)
            stream = [(L, piece) for L in range(DEPTH) for piece in PIECES]
            for n, (L, piece) in enumerate(stream):
                if n >= RAWS:
                    sp.wait_ge(*used(*stream[n - RAWS]))
                if n == 4:
                    sp.dma_start(cst[:, C_ID + P:], consts[:, C_ID + P:]).then_inc(consts_in, 16)
                sp.dma_start(raw[:, n % RAWS, :], weights[L * len(PIECES) + PIECES.index(piece)]).then_inc(piece_in[n % RAWS], 16)
            for b in range(NB):
                sp.wait_ge(h2_ready, (DEPTH - 1) * NB + b + 1)
                sp.dma_start(out[b * P:(b + 1) * P, :], h[:, b, :]).then_inc(out_sent, 16)
            sp.wait_ge(out_sent, 16 * NB)

        @block.gpsimd
        def _(pool):
            pool.dma_start(par[:, :], params[0]).then_inc(params_in, 16)
            pool.dma_start(lnr[:, :], lnrows[0, 0]).then_inc(ln_in, 16)
            pool.sem_inc(row_used, RING)

            def split_lo(L, piece):
                n, s = split_number(L, piece), raw_slot(L, piece)
                pool.wait_ge(w_hi_ready, n + 1)
                nc.gpsimd.tensor_tensor(w_lo[:, s, :], raw[:, s, :], w_hi[:, n % HIS, :].bitcast(F32), ALU.subtract).then_inc(w_lo_ready, 1)

            for L in range(DEPTH):
                for step in STEPS:
                    kind = step[0]
                    if SPLIT_AT.get(step) != DVE_SPLIT:
                        for piece in split_at(L, step):
                            split_lo(*piece)
                    if step == ("hT", 0, 0):
                        pool.wait_ge(small_hi_ready, L + 1)
                        nc.gpsimd.tensor_tensor(w_small[:, 1, :], par[:, Q_WS:Q_WS + KT * 16], w_small[:, 0, :].bitcast(F32), ALU.subtract).then_inc(small_lo_ready, 1)
                        if L == 0:
                            for piece in first_group(0):
                                split_lo(*piece)
                            pool.wait_ge(consts_in, 16)
                    if kind == "y" and step[2] < LEVELS - 1:
                        _, b, l = step
                        pool.wait_ge(*filled(L, step))
                        nc.gpsimd.tensor_tensor(heads(Xm[:, b, :]), heads(lt[:, b, :]), each(lev(l + 1), GH), ALU.mult).then_inc(x_ready, 1)
                    if kind == "select":
                        pool.wait_ge(h1_ready, NB * (L + 1))
                        pool.dma_start(lnr[:, :], lnrows[L, 1]).then_inc(ln_in, 16)
                    if kind == "experts":
                        b = step[1]
                        n0 = (L * NB + b) * RANKS
                        pool.wait_ge(*filled(L, ("sc", 1, 3)))
                        with pool.Fori(0, EH) as r:
                            for i in range(TOPK):
                                pool.wait_ge(row_used, r * TOPK + (n0 + i + 1))
                                pool.nop(nofuse=True)
                                if i == 0:
                                    pool.wait_ge(idx_ready, r + ((L * NB + b) * EH + 1))
                                    pool.nop(nofuse=True)
                                if b == 0 and i == RING - 2:
                                    pool.wait_ge(*filled(L, ("pg", 1, 1)))
                                if i % RING == 0:
                                    nc.gpsimd.tensor_copy(stage[:, i:i + RING], idxu[:, bass.ds(r * TOPK + (b * RANKS + i), RING)]).then_inc(idx_staged, 1)
                                    pool.wait_ge(idx_staged, r * 2 + ((L * NB + b) * 2 * EH + i // RING + 1))
                                    pool.nop(nofuse=True)
                                nc.gpsimd.indirect_dma_start(
                                    slots[i % RING][:, :], None, experts[:, :],
                                    bass.IndirectOffsetOnAxis(stage[:, i:i + 1], 0)).then_inc(slot_in[i % RING], 16)
                        if b == 0 and L + 1 < DEPTH:
                            pool.wait_ge(*filled(L, ("pp", 1, 1)))
                            pool.dma_start(par[:, :], params[L + 1]).then_inc(params_in, 16)
                    if kind == "ln2" and step[1] == 1 and L + 1 < DEPTH:
                        for piece in first_group(L + 1):
                            split_lo(*piece)
                        pool.wait_ge(h2_ready, NB * (L + 1))
                        pool.dma_start(lnr[:, :], lnrows[L + 1, 0]).then_inc(ln_in, 16)

        @block.tensor
        def _(pe):
            mm, tp = nc.tensor.matmul, nc.tensor.transpose
            links = [0]
            pe.wait_ge(ident_in, 16)

            def split(L, g, j):
                n = split_number(L, (g, j))
                pe.wait_ge(*lo_ready(L, (g, j)))
                return w_hi[:, n % HIS, :], w_lo[:, raw_slot(L, (g, j)), :]

            def whole(L, g, j):
                pe.wait_ge(*loaded(L, (g, j)))
                return raw[:, raw_slot(L, (g, j)), :]

            def read(L, g, j, last):
                if GROUPS[g][2][j] is None:
                    last.then_inc(piece_used, 1)

            def mm3(dst, left, right, start, stop):
                mm(dst, left[0], right[0], start=start, stop=False)
                mm(dst, left[0], right[1], start=False, stop=False)
                return mm(dst, left[1], right[0], start=False, stop=stop)

            def token_major(L, g, pieces, src, blocks, kt, uses):
                for j in pieces:
                    w = split(L, g, j)
                    for ps, b in blocks:
                        for i in range(2):
                            k = 2 * (j - pieces[0]) + i
                            last = mm3(ps, [src[:, i2, k, b * P:(b + 1) * P] for i2 in range(2)], [x[:, i * 512:(i + 1) * 512] for x in w], k == 0, k == kt - 1)
                        if j == pieces[-1]:
                            ends[b] = last
                    if uses and j != pieces[-1]:
                        read(L, g, j, last)

            def feature_major(L, g, ps, p):
                for i in range(2):
                    w = split(L, g, 2 * p + i)
                    for k in range(KT):
                        last = mm3(ps[:, i * T:(i + 1) * T], [x[:, k * P:(k + 1) * P] for x in w], [hT[:, i2, k, :] for i2 in range(2)], k == 0, k == KT - 1)
                    if i == 0:
                        read(L, g, 2 * p, last)
                return last

            ends = [None, None]

            for L in range(DEPTH):
                for step in FILLS + [("experts", 0), ("experts", 1)]:
                    kind = step[0]
                    if kind == "experts":
                        b = step[1]
                        n0 = (L * NB + b) * RANKS
                        if L or b:
                            pe.wait_ge(acc_drained, L * NB + b)
                        for c in range(2):
                            mm(acc[:, c * 512:(c + 1) * 512], zero, cst[:, 0:512], start=True, stop=False)

                        def weigh(r, i, closes):
                            pe.wait_ge(diag_ready, r * TOPK + (n0 + i + 2))
                            pe.nop(nofuse=True)
                            for c in range(2):
                                last = mm(acc[:, c * 512:(c + 1) * 512], diag[:, i % 4, :], slots[i % RING][:, D + c * 512:D + (c + 1) * 512], start=False, stop=closes)
                            last.then_inc(acc_filled if closes else row_used, 1)

                        with pe.Fori(0, EH - 1) as r:
                            for i in range(TOPK):
                                weigh(r, i, False)
                        for i in range(TOPK):
                            weigh(EH - 1, i, i == TOPK - 1)
                        pe.wait_ge(acc_filled, L * NB + b + 1)
                        pe.sem_inc(row_used, 1)
                        continue
                    bk, use = place(L, step)
                    ps = psum[:, bk, :]
                    both = kind in ("pool", "z", "fv", "gate", "br", "pg") or kind == "out" and step[1] == 0
                    blocks = [(ps, step[-1])]
                    if both and step[-1]:
                        ends[1].then_inc(bank_filled[bk], 1)
                        continue
                    if use:
                        pe.wait_ge(bank_drained[bk], use)
                    if both:
                        other = step[:-1] + (1,)
                        bk2, use2 = place(L, other)
                        if use2:
                            pe.wait_ge(bank_drained[bk2], use2)
                        blocks.append((psum[:, bk2, :], 1))
                    g = GROUP_OF.get(step)
                    if kind in ("hT", "h1T"):
                        _, b, q = step
                        if kind == "h1T":
                            pe.wait_ge(h1_ready, L * NB + b + 1)
                        elif L:
                            pe.wait_ge(h2_ready, (L - 1) * NB + b + 1)
                        else:
                            pe.wait_ge(x_in[b], 16)
                        for j in range(4):
                            last = tp(ps[:, j * P:(j + 1) * P], h[:, b, (4 * q + j) * P:(4 * q + j + 1) * P], ident)
                    elif kind == "smallT":
                        pe.wait_ge(small_lo_ready, L + 1)
                        for b in range(2):
                            for q in range(2):
                                pe.wait_ge(*drained(L, ("hT", b, q)))
                        for k in range(KT):
                            last = mm3(ps[0:16, 0:T], [w_small[:, i2, k * 16:(k + 1) * 16] for i2 in range(2)], [hT[:, i2, k, :] for i2 in range(2)], k == 0, k == KT - 1)
                    elif kind == "small":
                        b = step[1]
                        pe.wait_ge(*drained(L, ("smallT",)))
                        last = tp(ps[:, 0:16], smallT[0:16, b * P:(b + 1) * P], ident[0:16, 0:16])
                    elif kind in ("pool", "z", "fv", "gate"):
                        token_major(L, g, range(4), hT, blocks, KT, True)
                    elif kind in ("gdn", "fq", "fk", "wq"):
                        if kind == "wq":
                            for b in range(2):
                                for q in range(2):
                                    pe.wait_ge(*drained(L, ("h1T", b, q)))
                        last = feature_major(L, g, ps, step[-1])
                    elif kind == "cum":
                        b = step[1]
                        pe.wait_ge(logs_ready, L + 1)
                        pe.wait_ge(consts_in, 16)
                        if b:
                            mm(ps[:, 0:8], ones, logs[:, 0, 0:8], start=True, stop=False)
                        mm(ps[:, 0:8], tri, logs[:, b, 0:8], start=not b, stop=True)
                        mm(ps[:, 8:12], btri, logs[:, b, 8:12], start=True, stop=True)
                        last = mm(ps[:, 12:16], after, logs[:, b, 8:12], start=True, stop=True)
                    elif kind == "gbc":
                        b = step[1]
                        for hd in range(GH):
                            last = mm(ps[:, hd * P:(hd + 1) * P], logs[:, b, 8 + hd:9 + hd].broadcast_to([P, P]), btri, start=True, stop=True)
                    elif kind == "pooled":
                        pe.wait_ge(*drained(L, ("pool", 1)))
                        for i in range(2):
                            g = 2 * step[1] + i
                            cs = slice(g * P, (g + 1) * P)
                            mm(ps[:, i * T:i * T + P], poolx[:, 0, cs], band(0, g), start=True, stop=True)
                            mm(ps[:, i * T + P:(i + 1) * T], poolx[:, 0, cs], band(1, g), start=True, stop=False)
                            last = mm(ps[:, i * T + P:(i + 1) * T], poolx[:, 1, cs], band(2, g), start=False, stop=True)
                    elif kind == "poolmix":
                        pe.wait_ge(*drained(L, ("pooled", step[1])))
                        for i in range(2):
                            g = 2 * step[1] + i
                            last = mm(ps[:, i * T:(i + 1) * T], par[:, Q_PW + g * P:Q_PW + (g + 1) * P], pooledT[:, g, :], start=True, stop=True)
                    elif kind == "tr":
                        _, k3, b = step
                        pe.wait_ge(silu_ready, 3 * L + k3 + 1)
                        for hd in range(GH):
                            last = tp(ps[:, hd * P:(hd + 1) * P], cT[:, 4 * k3 + hd, b * P:(b + 1) * P], ident)
                    elif kind == "t4":
                        _, k4, b = step
                        pe.wait_ge(*drained(L, ("tr", k4 // 2, b)))
                        for hd in range(GH):
                            last = tp(ps[:, hd * P:(hd + 1) * P], tmp4[:, k4, hd * P:(hd + 1) * P], ident)
                    elif kind in ("lt", "at"):
                        b = step[1]
                        moving = 3 if kind == "lt" else 0
                        pe.wait_ge(*drained(L, ("t4", 2, b)))
                        pe.wait_ge(*drained(L, ("t4", moving, b)))
                        for hd in range(GH):
                            cs = slice(hd * P, (hd + 1) * P)
                            last = mm(ps[:, cs], fT[:, b, 2, cs], fT[:, b, moving, cs], start=True, stop=True)
                    elif kind == "t0":
                        b = step[1]
                        pe.wait_ge(u_init, L * NB + b + 1)
                        for hd in range(GH):
                            last = tp(ps[:, hd * P:(hd + 1) * P], Um[:, b, hd * P:(hd + 1) * P], ident)
                    elif kind == "y":
                        _, b, l = step
                        if l == 1:
                            pe.wait_ge(x1_ready, L * NB + b + 1)
                            pe.wait_ge(*drained(L, ("t0", b)))
                        else:
                            pe.wait_ge(x_ready, L * NB * (LEVELS - 2) + (l - 2) * NB + b + 1)
                            pe.wait_ge(*drained(L, ("ty", b, l - 1)))
                        for hd in range(GH):
                            cs = slice(hd * P, (hd + 1) * P)
                            last = mm(ps[:, cs], Xm[:, b, cs], Tm[:, b, cs], start=True, stop=True)
                    elif kind in ("ty", "uy"):
                        _, b, l = step
                        pe.wait_ge(*drained(L, ("y", b, l)))
                        if l == 1:
                            pe.wait_ge(u_init, L * NB + b + 1)
                        else:
                            pe.wait_ge(*drained(L, ("uy", b, l - 1)))
                        for hd in range(GH):
                            cs = slice(hd * P, (hd + 1) * P)
                            if kind == "ty":
                                last = mm(ps[:, cs], Um[:, b, cs], Ym[:, b, cs], start=True, stop=True)
                            else:
                                last = mm(ps[:, cs], Ym[:, b, cs], Um[:, b, cs], start=True, stop=True)
                    elif kind == "wT":
                        b = step[1]
                        pe.wait_ge(*drained(L, ("uy", b, LEVELS - 1)))
                        for hd in range(GH):
                            cs = slice(hd * P, (hd + 1) * P)
                            last = mm(ps[:, cs], kbe[:, b, cs], Um[:, b, cs], start=True, stop=True)
                    elif kind in ("vn", "o"):
                        _, b, c = step
                        n = 2 * b + c
                        rows = slice(c * CHUNK, (c + 1) * CHUNK)
                        if kind == "vn":
                            pe.wait_ge(*drained(L, ("wT", b)))
                            if n:
                                pe.wait_ge(*drained(L, ("dS", (n - 1) // 2, (n - 1) % 2)))
                        else:
                            pe.wait_ge(*drained(L, ("vn", b, c)))
                        for hd in range(GH):
                            cs = slice(hd * P, (hd + 1) * P)
                            t0 = hd * P + c * CHUNK
                            left = Tm[:, b, t0:t0 + CHUNK] if kind == "vn" else fT[:, b, 1, t0:t0 + CHUNK]
                            if n:
                                mm(ps[rows, cs], left, Sm[:, n % 2, cs], start=True, stop=False)
                            if kind == "vn":
                                last = mm(ps[rows, cs], Um[:, b, t0:t0 + CHUNK], vb[:, b, cs], start=not n, stop=True)
                            else:
                                last = mm(ps[rows, cs], att[rows, b, t0:t0 + CHUNK], vnew[rows, b, cs], start=not n, stop=True)
                    elif kind == "dS":
                        _, b, c = step
                        rows = slice(c * CHUNK, (c + 1) * CHUNK)
                        for hd in range(GH):
                            cs = slice(hd * P, (hd + 1) * P)
                            last = mm(ps[:, cs], kdec[rows, b, cs], vnew[rows, b, cs], start=True, stop=True)
                    elif kind == "oT":
                        b = step[1]
                        pe.wait_ge(on_ready, L * NB + b + 1)
                        for hd in range(GH):
                            last = tp(ps[:, hd * P:(hd + 1) * P], om[:, b, hd * P:(hd + 1) * P], ident)
                    elif kind == "fs":
                        _, b, hp = step
                        if hp == 0:
                            pe.wait_ge(*drained(L, ("fq", 1)))
                            pe.wait_ge(*drained(L, ("fk", 1)))
                        width = (b + 1) * P
                        for j in range(2):
                            hd = 2 * hp + j
                            rows = slice(j * FD, (j + 1) * FD)
                            if j:
                                links[0] += 1
                                last.then_inc(pe_step, 1)
                                pe.wait_ge(pe_step, links[0])
                            mm(ps[:, j * T:j * T + width], fq[rows, hp, b * P:(b + 1) * P], fk[rows, hp, 0:width], start=True, stop=False)
                            last = mm(ps[:, j * T:j * T + width], logs[:, 0, hd:hd + 1].broadcast_to([P, P]), tri_ones[:, 0:width], start=False, stop=b == 0)
                            if b:
                                last = mm(ps[:, j * T + P:(j + 1) * T], logs[:, 1, hd:hd + 1].broadcast_to([P, P]), tri, start=False, stop=True)
                    elif kind == "pt":
                        _, b, hp = step
                        pe.wait_ge(fexp_ready, 2 * (L * 8 + b * 4 + hp + 1))
                        for j in range(2):
                            for kb in range(b + 1):
                                col = (j * (b + 1) + kb) * P
                                last = tp(ps[:, col:col + P], fE[:, hp % 2, j, kb * P:(kb + 1) * P], ident)
                    elif kind == "fo":
                        _, b, hp = step
                        pe.wait_ge(*drained(L, ("pt", b, hp)))
                        pe.wait_ge(*drained(L, ("fv", 1)))
                        for j in range(2):
                            hd = 2 * hp + j
                            for kb in range(b + 1):
                                col = (j * (b + 1) + kb) * P
                                last = mm(ps[:, j * FD:(j + 1) * FD], fP[:, hp % 2, col:col + P], fv[:, kb, hd * FD:(hd + 1) * FD], start=kb == 0, stop=kb == b)
                    elif kind == "foT":
                        b = step[1]
                        pe.wait_ge(*drained(L, ("fo", b, 3)))
                        for j in range(4):
                            last = tp(ps[:, j * P:(j + 1) * P], fo[:, j * P:(j + 1) * P], ident)
                    elif kind == "br":
                        _, n, c, b = step
                        pe.wait_ge(*drained(L, (("foT", 1), ("poolmix", 1), ("oT", 1))[n]))
                        pe.wait_ge(*drained(L, (("foT", 0), ("poolmix", 0), ("oT", 0))[n]))
                        token_major(L, g, range(2 * c, 2 * c + 2), brT[:, 1 if n == 0 else 0], blocks, 4, True)
                    elif kind == "mT":
                        _, b, q = step
                        pe.wait_ge(merged_ready, L * 4 + 2 + b + 1)
                        for j in range(4):
                            last = tp(ps[:, j * P:(j + 1) * P], merged[:, b, (4 * q + j) * P:(4 * q + j + 1) * P], ident)
                    elif kind == "out":
                        _, c, b = step
                        for b2 in range(2) if both else (b,):
                            for q in range(2):
                                pe.wait_ge(*drained(L, ("mT", b2, q)))
                        token_major(L, g, range(4), hT, blocks, KT, both or b == 1)
                        last = ends[b]
                    elif kind == "sc":
                        _, b, q = step
                        pe.wait_ge(*drained(L, ("wq", q, 1)))
                        w = whole(L, g, 0)
                        for j in range(4):
                            li = 4 * q + j
                            last = mm(ps[:, j * P:(j + 1) * P], qpT[:, li, b * P:(b + 1) * P], w[:, li % 8 * P:(li % 8 + 1) * P], start=True, stop=True)
                    elif kind == "pg":
                        token_major(L, g, range(4), hT, blocks, KT, True)
                    elif kind == "pp":
                        _, c, b = step
                        pT = par[:, Q_PT:Q_PT + 2 * T].rearrange("p (k t) -> p k t", k=2)
                        w = whole(L, g, c)
                        for k in range(2):
                            last = mm(ps, pT[:, k, b * P:(b + 1) * P], w[:, k * 512:(k + 1) * 512], start=k == 0, stop=k == 1)
                    if both:
                        last = ends[0]
                    last.then_inc(bank_filled[bk], 1)

        @block.scalar
        def _(act):
            AC = nc.scalar.activation
            links = [0]

            def link(ins):
                links[0] += 1
                ins.then_inc(act_step, 1)
                act.wait_ge(act_step, links[0])

            def inv_sqrt(dst, src, tmp, ready):
                link(AC(tmp, src, ACT.Ln))
                AC(dst, tmp, ACT.Exp, scale=-0.5).then_inc(ready, 1)

            def split_hi(L, piece):
                n = split_number(L, piece)
                act.wait_ge(*loaded(L, piece))
                if n >= HIS:
                    m = n - HIS
                    act.wait_ge(*used(m // len(SPLIT_PIECES), SPLIT_PIECES[m % len(SPLIT_PIECES)]))
                AC(w_hi[:, n % HIS, :], raw[:, raw_slot(L, piece), :], ACT.Copy).then_inc(w_hi_ready, 1)

            for L in range(DEPTH):
                for step in STEPS:
                    kind = step[0]
                    for piece in split_at(L, step):
                        split_hi(*piece)
                    if step == ("hT", 0, 0):
                        act.wait_ge(params_in, 16 * (L + 1))
                        AC(w_small[:, 0, :], par[:, Q_WS:Q_WS + KT * 16], ACT.Copy).then_inc(small_hi_ready, 1)
                    if L == 0 and step == ("smallT",):
                        for piece in first_group(0):
                            split_hi(*piece)
                    if step == ("ln2", 0):
                        for piece in first_group(L + 1):
                            split_hi(*piece)
                    if kind == "select":
                        continue
                    if kind == "softplus":
                        act.wait_ge(sp_neg, L + 1)
                        AC(spe, spz, ACT.Exp).then_inc(sp_exp, 1)
                        AC(spb, sm[:, :, 12:16], ACT.Exp, scale=-1.0).then_inc(sp_exp, 1)
                        AC(aexp[:, :], par[:, Q_ALOG:Q_ALOG + 4], ACT.Exp).then_inc(sp_exp, 1)
                        act.wait_ge(sp_one, L + 1)
                        AC(spl, spu, ACT.Ln).then_inc(sp_ln, 1)
                        continue
                    if step == ("ln2", 0):
                        continue
                    if kind in ("ln1", "ln2"):
                        n = L * 4 + (step[1] if kind == "ln1" else 2 + step[1]) + 1
                        act.wait_ge(var_ready, n)
                        inv_sqrt(rstd[:, :], mv[:, 1:2], mv[:, 1:2], rstd_ready)
                        continue
                    if kind == "onorm":
                        b = step[1]
                        act.wait_ge(oss_ready, L * NB + b + 1)
                        inv_sqrt(ors[:, b, :], oss[:, b, :], oss[:, b, :], ors_ready)
                        continue
                    if kind == "texp":
                        act.wait_ge(top_ready, L * 2 * EH + 1)
                        AC(texp, texp, ACT.Exp).then_inc(texp_ready, 1)
                        continue
                    if kind == "experts":
                        n0 = (L * NB + step[1]) * RANKS
                        g0 = (L * NB + step[1]) * EH

                        def head(r, more):
                            for i in range(TOPK):
                                act.wait_ge(dot_ready, r * TOPK + (n0 + i + 1))
                                act.nop(nofuse=True)
                                AC(gel[:, i:i + 1], dots[:, i:i + 1], ACT.Gelu).then_inc(gelu_ready, 1)
                                if i == 12 and more:
                                    act.wait_ge(top_ready, r + (g0 + 2))
                                    act.nop(nofuse=True)
                                    AC(texp, texp, ACT.Exp).then_inc(texp_ready, 1)
                                if i == 2 and not more:
                                    act.wait_ge(var_ready, L * 4 + 3)
                                    inv_sqrt(rstd[:, :], mv[:, 1:2], mv[:, 1:2], rstd_ready)

                        with act.Fori(0, EH - step[1]) as r:
                            head(r, True)
                        if step[1]:
                            head(EH - 1, False)
                        continue
                    ps = bank(L, step)
                    bk, use = place(L, step)
                    done = bank_drained[bk]
                    if kind in ("small", "lt", "at", "ty", "uy", "dS", "br", "out"):
                        continue
                    if kind == "cum":
                        b = step[1]
                        act.wait_ge(*drained(L, step))
                        AC(ecum[:, b, :], cpos[:, b, :], ACT.Exp).then_inc(ecum_ready, 1)
                        continue
                    if kind == "gbc":
                        b = step[1]
                        act.wait_ge(*drained(L, step))
                        AC(DT[:, b, :], DT[:, b, :], ACT.Exp).then_inc(dt_ready, 1)
                        AC(egl[:, b, :], glast[:, b, :], ACT.Exp).then_inc(dt_ready, 1)
                        continue
                    if kind == "tr":
                        _, k3, b = step
                        if k3 < 2:
                            n = L * 4 + b * 2 + k3 + 1
                            act.wait_ge(*filled(L, step))
                            if n > 1:
                                act.wait_ge(ss_ready, n - 1)
                            AC(sq, ps, ACT.Square).then_inc(sq_ready, 1)
                            act.wait_ge(ss_ready, n)
                            inv_sqrt(rsq[:, b, 4 * k3:4 * k3 + 4], ssq[:, b, 4 * k3:4 * k3 + 4], ssq[:, b, 4 * k3:4 * k3 + 4], rs_ready)
                        continue
                    if kind == "fs":
                        _, b, hp = step
                        act.wait_ge(fmax_ready, L * 8 + b * 4 + hp + 1)
                        for j in range(2):
                            hd = 2 * hp + j
                            e = fE[:, hp % 2, j, 0:(b + 1) * P]
                            AC(e, e, ACT.Exp, bias=fmax[:, b, hd:hd + 1], accum_out=fsum[:, b, hd:hd + 1]).then_inc(fexp_ready, 1)
                        continue
                    if kind == "fo":
                        continue
                    act.wait_ge(*filled(L, step))
                    if step in HI_STEPS:
                        hi, _ = split_target(step)
                        if kind == "poolmix":
                            for i in range(2):
                                g = 2 * step[1] + i
                                last = AC(hi[:, i, :], ps[:, i * T:(i + 1) * T], ACT.Copy, scale=par[:, Q_PSC + g:Q_PSC + g + 1])
                        else:
                            scale = {"scale": par[:, Q_NORM:Q_NORM + 1]} if kind == "oT" else {}
                            last = AC(hi, ps.rearrange("p (k t) -> p k t", k=4), ACT.Copy, **scale)
                        last.then_inc(act_hi_ready, 1)
                        continue
                    elif kind == "smallT":
                        last = AC(smallT[0:16, :], ps[0:16, 0:T], ACT.Copy)
                    elif kind == "pool":
                        last = AC(poolx[:, step[1], :], ps, ACT.Copy)
                    elif kind == "gdn":
                        _, u, p = step
                        if u == 0 and p == 0:
                            act.wait_ge(logs_ready, L + 1)
                        last = AC(cin[:, 2 * p:2 * p + 2, 3:3 + T], ps.rearrange("p (k t) -> p k t", k=2), ACT.Copy)
                    elif kind == "pooled":
                        last = AC(pooledT[:, 2 * step[1]:2 * step[1] + 2, :], ps.rearrange("p (k t) -> p k t", k=2), ACT.Copy)
                    elif kind == "z":
                        last = AC(zs[:, step[1], :], ps, ACT.Silu)
                    elif kind == "fq":
                        last = AC(fq[:, 2 * step[1]:2 * step[1] + 2, :], ps.rearrange("p (k t) -> p k t", k=2), ACT.Copy, scale=FD ** -0.5)
                    elif kind == "fk":
                        last = AC(fk[:, 2 * step[1]:2 * step[1] + 2, :], ps.rearrange("p (k t) -> p k t", k=2), ACT.Copy)
                    elif kind == "fv":
                        last = AC(fv[:, step[1], :], ps, ACT.Copy)
                    elif kind == "t4":
                        last = AC(fT[:, step[2], step[1], :], ps, ACT.Copy)
                    elif kind == "t0":
                        last = AC(Tm[:, step[1], :], ps, ACT.Copy)
                    elif kind == "y":
                        last = AC(Ym[:, step[1], :], ps, ACT.Copy)
                    elif kind == "wT":
                        last = AC(Tm[:, step[1], :], ps, ACT.Copy, scale=-1.0)
                    elif kind in ("vn", "o"):
                        _, b, c = step
                        rows = slice(c * CHUNK, (c + 1) * CHUNK)
                        last = AC((vnew if kind == "vn" else om)[rows, b, :], ps[rows, :], ACT.Copy)
                    elif kind == "pt":
                        _, b, hp = step
                        w = 2 * (b + 1) * P
                        last = AC(fP[:, hp % 2, 0:w], ps[:, 0:w], ACT.Copy)
                    elif kind == "gate":
                        _, n, c, b = step
                        if n == 2:
                            act.wait_ge(*drained(L, ("br", 0, c, b)))
                        last = AC(gates[:, n % 2, b, c * 512:(c + 1) * 512], ps, ACT.Sigmoid)
                    elif kind == "wq":
                        _, u, p = step
                        last = AC(qpT[:, 4 * u + 2 * p:4 * u + 2 * p + 2, :], ps.rearrange("p (k t) -> p k t", k=2), ACT.Copy)
                    elif kind == "sc":
                        _, b, g = step
                        last = AC(scs[:, b, 4 * g:4 * g + 4, :], ps.rearrange("p (l n) -> p l n", l=4), ACT.Copy)
                    elif kind == "pg":
                        _, c, b = step
                        last = AC(emb_gate[:, b, c * 512:(c + 1) * 512], ps, ACT.Sigmoid)
                    elif kind == "pp":
                        _, c, b = step
                        last = AC(base[:, b, c * 512:(c + 1) * 512], ps, ACT.Copy)
                    last.then_inc(done, 1)
                    if kind == "gdn" and step[2] == 1:
                        u = step[1]
                        act.wait_ge(conv_ready, 3 * L + u + 1)
                        AC(cT[:, 4 * u:4 * u + 4, :], cT[:, 4 * u:4 * u + 4, :], ACT.Silu).then_inc(silu_ready, 1)

        @block.vector
        def _(dve):
            TT, TS, STT, CP = nc.vector.tensor_tensor, nc.vector.tensor_scalar, nc.vector.scalar_tensor_tensor, nc.vector.tensor_copy
            links = [0]

            def link(ins, r=None):
                links[0] += 1
                ins.then_inc(dve_step, 1)
                dve.wait_ge(dve_step, links[0] if r is None else r * SELECT_LINKS + links[0])
                if r is not None:
                    dve.nop(nofuse=True)

            def select_head(L, g, r=None):
                link(CP(sl, scs_flat[:, bass.ds(g * 2 * KEYS, 2 * KEYS)].rearrange("p (s n) -> p s n", s=2)), r)
                for s in range(2):
                    last = nc.vector.max(tv[:, s, 0:8], sl[:, s, :])
                link(last, r)
                yield
                for s in range(2):
                    last = nc.vector.max_index(tiu[:, s, 0:8], tv[:, s, 0:8], sl[:, s, :])
                link(last, r)
                yield
                for s in range(2):
                    last = nc.vector.match_replace(sl[:, s, :], tv[:, s, 0:8], sl[:, s, :], -3e38)
                link(last, r)
                yield
                for s in range(2):
                    last = nc.vector.max(tv[:, s, 8:16], sl[:, s, :])
                link(last, r)
                yield
                for s in range(2):
                    last = nc.vector.max_index(tiu[:, s, 8:16], tv[:, s, 8:16], sl[:, s, :])
                link(last, r)
                link(CP(tif, tiu), r)
                link(TS(tif[:, 0, :], tif[:, 0, :], float(KEYS), None, ALU.mult), r)
                yield
                col = 0
                for a, n, w in CAND_RUNS:
                    for dst, src in ((cand, tv), (candi, tif)):
                        o_ = dst[:, col:col + n * w].rearrange("p (n w) -> p n w", n=n)
                        last = TT(o_, over(src[:, 0, a:a + n], w), each(src[:, 1, 0:w], n), ALU.add)
                    col += n * w
                link(last, r)
                yield
                link(nc.vector.max(top[:, 0:8], cand), r)
                yield
                link(nc.vector.max_index(posu[:, 0:8], top[:, 0:8], cand), r)
                yield
                link(nc.vector.match_replace(cand, top[:, 0:8], cand, -3e38), r)
                yield
                link(nc.vector.max(top[:, 8:16], cand), r)
                TS(texp, top, top[:, 0:1], None, ALU.subtract).then_inc(top_ready, 1)
                link(nc.vector.max_index(posu[:, 8:16], top[:, 8:16], cand), r)
                yield
                link(CP(posf, posu[:, :]), r)
                link(TT(eq, each(cst[:, C_IOTA:C_IOTA + NCAND], TOPK), over(posf, NCAND), ALU.is_equal), r)
                yield
                link(TT(eq, eq, each(candi, TOPK), ALU.mult), r)
                yield
                link(nc.vector.tensor_reduce(idxf, eq, AX_X, ALU.add), r)
                yield
                TS(idxu[:, bass.ds(g * TOPK, TOPK)], idxf, float(L * NE), None, ALU.add)
                n = L * 2 * EH + g + 1
                dve.wait_ge(texp_ready, n)
                dve.nop(nofuse=True)
                link(nc.vector.tensor_reduce(tsum[:, :], texp, AX_X, ALU.add), r)
                link(nc.vector.reciprocal(trec[:, :], tsum[:, :]), r)
                TS(wts[:, bass.ds(g * TOPK, TOPK)], texp, trec[:, 0:1], None, ALU.mult).then_inc(idx_ready, 1)

            def norm(r, b, n, ready):
                nc.vector.bn_stats(bst[:, 0:6], r[:, 0:512])
                link(nc.vector.bn_stats(bst[:, 6:12], r[:, 512:1024]))
                yield
                link(nc.vector.bn_aggr(mv[:, :], bst[:, :]))
                TS(mv[:, 1:2], mv[:, 1:2], LN_EPS, None, ALU.add).then_inc(var_ready, 1)
                yield
                yield
                dve.wait_ge(rstd_ready, n)
                link(TS(r, r, mv[:, 0:1], rstd[:, 0:1], ALU.subtract, ALU.mult))
                yield
                link(TT(r, r, lnr[:, 0:D], ALU.mult))
                yield
                TT(h[:, b, :], r, lnr[:, D:2 * D], ALU.add).then_inc(ready, 1)

            def layer_norm(r, b, n, ready):
                for _ in norm(r, b, n, ready):
                    pass

            def split_lo(L, piece):
                n, s = split_number(L, piece), raw_slot(L, piece)
                dve.wait_ge(w_hi_ready, n + 1)
                TT(w_lo[:, s, :], raw[:, s, :], w_hi[:, n % HIS, :].bitcast(F32), ALU.subtract).then_inc(w_lo_dve_ready, 1)

            dve.sem_inc(diag_ready, 1)
            for L in range(DEPTH):
                for step in STEPS:
                    kind = step[0]
                    if SPLIT_AT.get(step) == DVE_SPLIT:
                        for piece in split_at(L, step):
                            split_lo(*piece)
                    if kind == "softplus":
                        dve.wait_ge(*drained(L, ("small", 1)))
                        dve.wait_ge(consts_in, 16)
                        link(TT(spy, sm[:, :, 0:12], each(cst[:, C_SIGN:C_SIGN + 12], 2), ALU.mult))
                        STT(spz, spy, -1.0, spy, ALU.mult, ALU.min).then_inc(sp_neg, 1)
                        nc.vector.memset(cin[:, :, 0:3], 0.0)
                        dve.wait_ge(sp_exp, 3 * (L + 1))
                        TS(spb, spb, 1.0, None, ALU.add)
                        TS(spu, spe, 1.0, None, ALU.add).then_inc(sp_one, 1)
                        dve.wait_ge(sp_one, L + 1)
                        nc.vector.reciprocal(beta, spb)
                        link(TS(spz, spu, -1.0, 0.0, ALU.add, ALU.is_equal))
                        link(STT(spd, spu, -1.0, spz, ALU.add, ALU.add))
                        link(nc.vector.reciprocal(spd, spd))
                        link(TT(spd, spd, spe, ALU.mult))
                        dve.wait_ge(sp_ln, L + 1)
                        link(TT(spz, spl, spz, ALU.add))
                        link(TT(spd, spd, spz, ALU.mult))
                        link(STT(logs, spy, 0.0, spd, ALU.max, ALU.add))
                        STT(logs[:, :, 8:12], logs[:, :, 8:12], -1.0, each(aexp[:, :], 2), ALU.mult, ALU.mult).then_inc(logs_ready, 1)
                        continue
                    if kind == "onorm":
                        b = step[1]
                        o = heads(om[:, b, :])
                        dve.wait_ge(*drained(L, ("o", b, 1)))
                        link(TT(heads(osq), o, o, ALU.mult))
                        link(nc.vector.tensor_reduce(oss[:, b, :], heads(osq), AX_X, ALU.add))
                        TS(oss[:, b, :], oss[:, b, :], 1.0 / GD, RMS_EPS, ALU.mult, ALU.add).then_inc(oss_ready, 1)
                        dve.wait_ge(ors_ready, L * NB + b + 1)
                        link(TT(o, o, over(ors[:, b, :], GD), ALU.mult))
                        TT(o, o, heads(zs[:, b, :]), ALU.mult).then_inc(on_ready, 1)
                        continue
                    if kind == "ln1":
                        b = step[1]
                        if b == 0:
                            dve.wait_ge(ln_in, 16 * (2 * L + 1))
                        dve.wait_ge(*drained(L, ("out", 1, b)))
                        layer_norm(rr[:, b, :], b, L * 4 + b + 1, h1_ready)
                        continue
                    if kind == "ln2":
                        b = step[1]
                        dve.wait_ge(ln_in, 16 * (2 * L + 2))
                        dve.wait_ge(acc_filled, L * NB + b + 1)
                        dve.wait_ge(base_ready, L * NB + b + 1)
                        for c in range(2):
                            cs = slice(c * 512, (c + 1) * 512)
                            last = TT(base[:, b, cs], base[:, b, cs], acc[:, cs], ALU.add)
                        last.then_inc(acc_drained, 1)
                        dve.wait_ge(acc_drained, L * NB + b + 1)
                        if b:
                            layer_norm(base[:, b, :], b, L * 4 + 2 + b + 1, h2_ready)
                        continue
                    if kind == "select":
                        dve.wait_ge(*drained(L, ("sc", 0, 0)))
                        n = links[0]
                        for _ in select_head(L, 0):
                            pass
                        assert links[0] - n == SELECT_LINKS
                        continue
                    if kind == "experts":
                        b = step[1]
                        n0 = (L * NB + b) * RANKS
                        g0 = (L * NB + b) * EH
                        for q in range(1, 8):
                            dve.wait_ge(*drained(L, ("sc", q % 2, q // 2)))

                        def head(r, more, looped):
                            dve.wait_ge(diag_ready, r * TOPK + (n0 + 1))
                            dve.wait_ge(idx_ready, r + (g0 + 1))
                            dve.nop(nofuse=True)
                            CP(wst[:, :], wts[:, bass.ds(r * TOPK + b * RANKS, TOPK)]).then_inc(wts_staged, 1)
                            choose = select_head(L, r + (b * EH + 1), r if looped else None) if more else norm(base[:, 0, :], 0, L * 4 + 3, h2_ready)
                            for i in range(TOPK + 2):
                                if i < TOPK:
                                    s = i % RING
                                    dve.wait_ge(slot_in[s], r * 32 + (n0 // RING + i // RING + 1) * 16)
                                    dve.nop(nofuse=True)
                                    nc.vector.tensor_tensor_reduce(slots[s][:, 0:D], slots[s][:, 0:D], h[:, b, :], 1.0, 0.0, ALU.mult, ALU.add, dots[:, i:i + 1]).then_inc(dot_ready, 1)
                                    next(choose, None)
                                if i >= 2:
                                    j = i - 2
                                    if j == 0:
                                        dve.wait_ge(wts_staged, r + (g0 + 1))
                                    dve.wait_ge(gelu_ready, r * TOPK + (n0 + j + 1))
                                    dve.wait_ge(row_used, r * TOPK + (n0 + j + RING - 3))
                                    dve.nop(nofuse=True)
                                    TS(diag[:, j % 4, :], ident, gel[:, j:j + 1], wst[:, j:j + 1], ALU.mult, ALU.mult).then_inc(diag_ready, 1)
                            for _ in choose:
                                pass

                        turns = EH - b
                        with dve.Fori(0, turns) as r:
                            head(r, True, True)
                        links[0] += SELECT_LINKS * (turns - 1)
                        if b:
                            head(EH - 1, False, False)
                        continue
                    if kind in NO_BANK:
                        continue
                    ps = bank(L, step)
                    bk, use = place(L, step)
                    done = bank_drained[bk]
                    if kind == "gdn":
                        _, u, p = step
                        dve.wait_ge(*drained(L, step))
                        tiles = (4 * u + 2 * p, 4 * u + 2 * p + 1)
                        for j in range(CONV):
                            for f in tiles:
                                tap = par[:, Q_CONV + 4 * f + j:Q_CONV + 4 * f + j + 1]
                                src = cin[:, f - 4 * u, j:j + T]
                                last = TS(cT[:, f, :], src, tap, None, ALU.mult) if j == 0 else STT(cT[:, f, :], src, tap, cT[:, f, :], ALU.mult, ALU.add)
                            if j < CONV - 1:
                                link(last)
                        if p:
                            last.then_inc(conv_ready, 1)
                        continue
                    if step in HI_STEPS:
                        hi, lo = split_target(step)
                        dve.wait_ge(act_hi_ready, hi_count(L, step))
                        if kind == "poolmix":
                            for i in range(2):
                                g = 2 * step[1] + i
                                last = STT(lo[:, i, :], ps[:, i * T:(i + 1) * T], par[:, Q_PSC + g:Q_PSC + g + 1], hi[:, i, :].bitcast(F32), ALU.mult, ALU.subtract)
                        elif kind == "oT":
                            last = STT(lo, ps.rearrange("p (k t) -> p k t", k=4), par[:, Q_NORM:Q_NORM + 1], hi.bitcast(F32), ALU.mult, ALU.subtract)
                        else:
                            last = TT(lo, ps.rearrange("p (k t) -> p k t", k=4), hi.bitcast(F32), ALU.subtract)
                        last.then_inc(done, 1)
                    elif kind == "small":
                        dve.wait_ge(*filled(L, step))
                        TT(sm[:, step[1], :], ps[:, 0:16], par[:, Q_BIAS:Q_BIAS + 16], ALU.add).then_inc(done, 1)
                    elif kind == "cum":
                        b = step[1]
                        dve.wait_ge(*filled(L, step))
                        TS(cneg[:, b, :], ps[:, 0:12], -1.0, None, ALU.mult)
                        CP(cpos[:, b, :], ps[:, 8:16]).then_inc(done, 1)
                    elif kind == "gbc":
                        b = step[1]
                        dve.wait_ge(*drained(L, ("cum", b)))
                        dve.wait_ge(*filled(L, step))
                        CP(glast[:, b, :].rearrange("p (h c) -> p h c", h=4), ps.rearrange("p (h c t) -> p h c t", h=4, c=2)[:, :, :, CHUNK - 1])
                        for hd in range(GH):
                            cs = slice(hd * P, (hd + 1) * P)
                            last = STT(DT[:, b, cs], ps[:, cs], cneg[:, b, 8 + hd:9 + hd], dmask, ALU.add, ALU.add)
                        last.then_inc(done, 1)
                    elif kind == "tr":
                        _, k3, b = step
                        if k3 < 2:
                            n = L * 4 + b * 2 + k3 + 1
                            cols = slice(4 * k3, 4 * k3 + 4)
                            dve.wait_ge(sq_ready, n)
                            link(nc.vector.tensor_reduce(ssq[:, b, cols], heads(sq), AX_X, ALU.add))
                            TS(ssq[:, b, cols], ssq[:, b, cols], L2_EPS, None, ALU.add).then_inc(ss_ready, 1)
                            if k3 == 0:
                                dve.wait_ge(ecum_ready, L * NB + b + 1)
                                if b:
                                    dve.wait_ge(*filled(L, ("t4", 3, 0)))
                            dve.wait_ge(rs_ready, n)
                            if k3 == 0:
                                link(TS(rs2[:, 0, :], rsq[:, b, cols], GD ** -0.5, None, ALU.mult))
                                link(TT(rs2[:, 1, :], rs2[:, 0, :], ecum[:, b, 0:4], ALU.mult))
                                outs = ((tmp4[:, 0, :], rs2[:, 0, :]), (tmp4[:, 1, :], rs2[:, 1, :]))
                            else:
                                link(TT(rs2[:, 2, :], rsq[:, b, cols], beta[:, b, :], ALU.mult))
                                TT(rs2[:, 3, :], rs2[:, 2, :], ecum[:, b, 0:4], ALU.mult)
                                link(TT(rs2[:, 4, :], rsq[:, b, cols], ecum[:, b, 4:8], ALU.mult))
                                outs = ((tmp4[:, 2, :], rsq[:, b, cols]), (tmp4[:, 3, :], rs2[:, 2, :]), (kbe[:, b, :], rs2[:, 3, :]), (kdec[:, b, :], rs2[:, 4, :]))
                        else:
                            dve.wait_ge(*filled(L, step))
                            outs = ((vb[:, b, :], beta[:, b, :]),)
                        for dst, scale in outs:
                            last = TT(heads(dst), heads(ps), over(scale, GD), ALU.mult)
                        last.then_inc(done, 1)
                    elif kind == "lt":
                        b = step[1]
                        dve.wait_ge(dt_ready, 2 * (L * NB + b + 1))
                        dve.wait_ge(*filled(L, step))
                        TT(lt[:, b, :], ps, DT[:, b, :], ALU.mult).then_inc(done, 1)
                        dve.wait_ge(*drained(L, step))
                        link(TT(heads(Um[:, b, :]), heads(lt[:, b, :]), each(lev(0), GH), ALU.mult))
                        TT(heads(Xm[:, b, :]), heads(lt[:, b, :]), each(lev(1), GH), ALU.mult).then_inc(x1_ready, 1)
                        TT(heads(Um[:, b, :]), heads(Um[:, b, :]), each(ident, GH), ALU.add).then_inc(u_init, 1)
                    elif kind == "at":
                        b = step[1]
                        dve.wait_ge(*filled(L, step))
                        TT(att[:, b, :], ps, DT[:, b, :], ALU.mult).then_inc(done, 1)
                    elif kind in ("ty", "uy"):
                        b = step[1]
                        m = Tm if kind == "ty" else Um
                        dve.wait_ge(*filled(L, step))
                        TT(m[:, b, :], m[:, b, :], ps, ALU.add).then_inc(done, 1)
                    elif kind == "dS":
                        _, b, c = step
                        n = 2 * b + c
                        dve.wait_ge(*filled(L, step))
                        if n == 0:
                            last = CP(Sm[:, 1, :], ps)
                        else:
                            for hd in range(GH):
                                cs = slice(hd * P, (hd + 1) * P)
                                last = STT(Sm[:, (n + 1) % 2, cs], Sm[:, n % 2, cs], egl[:, b, 2 * hd + c:2 * hd + c + 1], ps[:, cs], ALU.mult, ALU.add)
                        last.then_inc(done, 1)
                    elif kind == "fs":
                        _, b, hp = step
                        w = (b + 1) * P
                        dve.wait_ge(*filled(L, step))
                        if hp >= 2:
                            dve.wait_ge(*filled(L, ("pt", b, hp - 2)))
                        elif b:
                            dve.wait_ge(*filled(L, ("pt", 0, hp + 2)))
                        for j in range(2):
                            hd = 2 * hp + j
                            last = STT(fE[:, hp % 2, j, 0:w], ps[:, j * T:j * T + w], cneg[:, b, hd:hd + 1], fmask[:, T - w:T], ALU.add, ALU.add)
                        last.then_inc(done, 1)
                        dve.wait_ge(*drained(L, step))
                        nc.vector.tensor_reduce(fmax[:, b, 2 * hp:2 * hp + 2], fE[:, hp % 2, :, 0:w], AX_X, ALU.max, negate=True).then_inc(fmax_ready, 1)
                    elif kind == "fo":
                        _, b, hp = step
                        dve.wait_ge(fexp_ready, 2 * (L * 8 + b * 4 + hp + 1))
                        link(nc.vector.reciprocal(frs[:, b, 2 * hp:2 * hp + 2], fsum[:, b, 2 * hp:2 * hp + 2]))
                        if b and hp == 0:
                            dve.wait_ge(*filled(L, ("foT", 0)))
                        dve.wait_ge(*filled(L, step))
                        TT(fo[:, hp * P:(hp + 1) * P].rearrange("p (j d) -> p j d", j=2), ps[:, 0:P].rearrange("p (j d) -> p j d", j=2), over(frs[:, b, 2 * hp:2 * hp + 2], FD), ALU.mult).then_inc(done, 1)
                    elif kind == "br":
                        _, n, c, b = step
                        cs = slice(c * 512, (c + 1) * 512)
                        g = gates[:, n % 2, b, c * 512:(c + 1) * 512]
                        dve.wait_ge(*filled(L, step))
                        dve.wait_ge(*drained(L, ("gate", n, c, b)))
                        if n == 0:
                            TT(merged[:, b, cs], ps, g, ALU.mult).then_inc(done, 1)
                        else:
                            TT(g, ps, g, ALU.mult).then_inc(done, 1)
                            dve.wait_ge(*drained(L, step))
                            last = TT(merged[:, b, cs], merged[:, b, cs], g, ALU.add)
                            if n == 2:
                                last.then_inc(merged_ready, 1)
                            else:
                                link(last)
                    elif kind == "out":
                        _, c, b = step
                        cs = slice(c * 512, (c + 1) * 512)
                        dve.wait_ge(*filled(L, step))
                        STT(rr[:, b, cs], h[:, b, cs], ALPHA, ps, ALU.mult, ALU.add).then_inc(done, 1)
                    elif kind == "pg":
                        _, c, b = step
                        cs = slice(c * 512, (c + 1) * 512)
                        dve.wait_ge(*drained(L, step))
                        dve.wait_ge(*drained(L, ("pp", c, b)))
                        link(TT(base[:, b, cs], base[:, b, cs], emb_gate[:, b, cs], ALU.mult))
                        last = STT(base[:, b, cs], h[:, b, cs], ALPHA, base[:, b, cs], ALU.mult, ALU.add)
                        if c:
                            last.then_inc(base_ready, 1)


def constants():
    c = np.zeros((P, NCONST), np.float32)
    r, t = np.arange(P)[:, None], np.arange(P)[None, :]
    same = r // CHUNK == t // CHUNK
    c[:, C_ID:C_ID + P] = r == t
    c[:, C_TRI:C_TRI + P] = r <= t
    c[:, C_ONES:C_ONES + P] = 1
    c[:, C_BTRI:C_BTRI + P] = (r <= t) & same
    c[:, C_AFTER:C_AFTER + P] = (r > t) & same
    c[:, C_CMASK:C_CMASK + P] = np.where(t <= r, 0, MASKED)
    c[:, C_DMASK:C_DMASK + P] = np.where((t >= r) & same, 0, MASKED)
    for i in range(LEVELS):
        s = 1 << i
        c[:, C_LEV + i * P:C_LEV + (i + 1) * P] = -1.0 * ((r // (2 * s) == t // (2 * s)) & (t // s % 2 == 1) & (r // s % 2 == 0))
    for g, w in enumerate(WINDOWS):
        for kind, (rb, tb) in enumerate(((0, 0), (0, 1), (1, 1))):
            rr, tt = r + rb * P, t + tb * P
            inside = (rr <= tt) & (rr > tt - w)
            c[:, C_BAND + (4 * kind + g) * P:][:, :P] = np.where(inside, 1.0 / np.minimum(tt + 1, w), 0) - (rr == tt)
    c[:, C_IOTA:C_IOTA + 64] = np.arange(64)
    c[:, C_SIGN:C_SIGN + 8] = -1
    c[:, C_SIGN + 8:C_SIGN + 12] = 1
    return c


def k_tiles(w):
    k, n = w.shape
    return w.reshape(k // P, P, n).transpose(1, 0, 2).reshape(P, -1)


def kernel(x, p, w_in, fox_fb, pool_w, pool_scale, gdn_conv, gdn_a_log, gdn_dt_bias, gdn_norm, w_branch, w_out,
           ln1_g, ln1_b, peer_wq, peer_k1, peer_k2, peer_u, peer_v, ple_gate, ple_proj, ln2_g, ln2_b):
    import concourse.bacc as bacc
    from concourse.bass_utils import run_bass_kernel_spmd

    x, p, w_in, fox_fb, pool_w, pool_scale, gdn_conv, gdn_a_log, gdn_dt_bias, gdn_norm, w_branch, w_out, \
        ln1_g, ln1_b, peer_wq, peer_k1, peer_k2, peer_u, peer_v, ple_gate, ple_proj, ln2_g, ln2_b = (
            np.asarray(a) for a in (x, p, w_in, fox_fb, pool_w, pool_scale, gdn_conv, gdn_a_log, gdn_dt_bias, gdn_norm,
                                    w_branch, w_out, ln1_g, ln1_b, peer_wq, peer_k1, peer_k2, peer_u, peer_v, ple_gate,
                                    ple_proj, ln2_g, ln2_b))
    o_f = 3 * BW
    o_pool = o_f + FH
    o_gdn = o_pool + BW
    o_b = o_gdn + 3 * BW
    o_a = o_b + GH
    o_z = o_a + GH
    o_gate = o_z + BW
    columns = [o_pool, o_gdn, o_gdn + BW, o_gdn + 2 * BW, o_z, 0, BW, 2 * BW]
    pieces = np.empty((DEPTH * len(PIECES), P, PIECE), np.float32)
    params = np.zeros((DEPTH, P, NPARAM), np.float32)
    lnrows = np.empty((DEPTH, 2, P, 2 * D), np.float32)
    for L in range(DEPTH):
        def put(step, w, by_tile=False):
            g = GROUP_OF[step]
            n = L * len(PIECES) + PIECES.index((g, 0))
            for j in range(len(GROUPS[g][2])):
                pieces[n + j] = k_tiles(w[:, j * P:(j + 1) * P]) if by_tile else k_tiles(w[j * 2 * P:(j + 1) * 2 * P])

        w = w_in[L]
        for step, start in zip((("pool", 0), ("gdn", 0, 0), ("gdn", 1, 0), ("gdn", 2, 0), ("z", 0), ("fq", 0), ("fk", 0), ("fv", 0)), columns):
            put(step, w[:, start:start + BW], step[0] in ("gdn", "fq", "fk"))
        for n in range(3):
            for c in range(2):
                put(("gate", n, c, 0), w[:, o_gate + (2 * n + c) * BW:][:, :BW])
            put(("br", n, 0, 0), np.concatenate([w_branch[L, n][:, :BW], w_branch[L, n][:, BW:]]))
        for c in range(2):
            put(("out", c, 0), w_out[L][:, c * BW:(c + 1) * BW])
            put(("pg", c, 0), ple_gate[L][:, c * BW:(c + 1) * BW])
        put(("pp", 0, 0), np.concatenate([ple_proj[L][:, :BW], ple_proj[L][:, BW:]]))
        for c in range(4):
            put(("wq", c, 0), peer_wq[L][:, c * BW:(c + 1) * BW], True)
        keys = np.stack([peer_k1[L], peer_k2[L]], 1)
        keys = keys.transpose(3, 0, 1, 2).reshape(P, 2 * PIECE)
        for j in range(2):
            pieces[L * len(PIECES) + PIECES.index((GROUP_OF["sc", 0, 2 * j], 0))] = keys[:, j * PIECE:(j + 1) * PIECE]
        q = params[L]
        q[:, Q_CONV:Q_CONV + 48] = gdn_conv[L][:, 0, :].reshape(CONV, 12, P).transpose(2, 1, 0).reshape(P, 48)
        q[:, Q_PSC:Q_PSC + 4] = pool_scale[L].reshape(4, P).T
        q[:, Q_NORM] = gdn_norm[L]
        q[:, Q_BIAS:Q_BIAS + 8] = fox_fb[L]
        q[:, Q_BIAS + 8:Q_BIAS + 12] = gdn_dt_bias[L]
        q[:, Q_ALOG:Q_ALOG + 4] = gdn_a_log[L]
        small = np.concatenate([w_in[L][:, o_f:o_f + FH], w_in[L][:, o_a:o_a + GH], w_in[L][:, o_b:o_b + GH]], 1)
        q[:, Q_WS:Q_WS + KT * 16] = k_tiles(small)
        q[:, Q_PW:Q_PW + 512] = pool_w[L].transpose(1, 0, 2).reshape(P, 512)
        q[:, Q_PT:Q_PT + 2 * T] = k_tiles(p[L, 0].T)
        lnrows[L, 0] = np.concatenate([ln1_g[L], ln1_b[L]])
        lnrows[L, 1] = np.concatenate([ln2_g[L], ln2_b[L]])
    experts = np.concatenate([peer_u.reshape(DEPTH * NE, D), peer_v.reshape(DEPTH * NE, D)], 1)
    arrays = {"x": np.ascontiguousarray(x[0]), "weights": pieces, "params": params, "lnrows": lnrows,
              "consts": constants(), "experts": experts}

    nc = bacc.Bacc("TRN2", target_bir_lowering=False, num_devices=1)
    args = [nc.dram_tensor(n + "_dram", a.shape, F32, kind="ExternalInput").ap() for n, a in arrays.items()]
    out = nc.dram_tensor("out_dram", (T, D), F32, kind="ExternalOutput").ap()
    build(nc, *args, out)
    r = run_bass_kernel_spmd(nc, [{n + "_dram": a for n, a in arrays.items()}], core_ids=[0])
    return r.results[0]["out_dram"].reshape(1, T, D)
```
